# Optimizing a Trainium2 kernel written in Bass

```python
import jax, jax.numpy as jnp
from jax import lax
import numpy as np
import jax
import jax.numpy as jnp

D_MODEL = 2048
BATCH = 1
SEQ = 512
DEPTH = 1

D_MIX = D_MODEL
WIDTH_A = D_MIX // 2
WIDTH_B = D_MIX - WIDTH_A
CHUNK = 128
HEADS_A = 8
DH_A = WIDTH_A // HEADS_A
HEADS_B = 16
DH_B = WIDTH_B // HEADS_B
Q_BLOCK = 128
EPS = 1e-6
SPLIT_SIZES = (WIDTH_A, WIDTH_A, WIDTH_A, WIDTH_B, WIDTH_B, WIDTH_B, WIDTH_B, HEADS_B)
D_IN = sum(SPLIT_SIZES)


def _split_points(sizes):
    pts, acc = [], 0
    for s in sizes[:-1]:
        acc += s
        pts.append(acc)
    return pts

def rms_norm(x, g):
    xf = x.astype(jnp.float32)
    y = xf * lax.rsqrt(jnp.mean(xf * xf, axis=-1, keepdims=True) + EPS)
    return (y * g.astype(jnp.float32)).astype(x.dtype)

def layer_norm(x, g, b):
    xf = x.astype(jnp.float32)
    mu = jnp.mean(xf, axis=-1, keepdims=True)
    xc = xf - mu
    var = jnp.mean(xc * xc, axis=-1, keepdims=True)
    y = xc * lax.rsqrt(var + EPS) * g.astype(jnp.float32) + b.astype(jnp.float32)
    return y.astype(x.dtype)

def chunked_spatial_gating(u, v, ln_g, ln_b, w_s, b_s):
    bsz, s, _ = v.shape
    n = s // CHUNK
    v = layer_norm(v, ln_g, ln_b)
    vc = v.reshape(bsz, n, CHUNK, HEADS_A, DH_A)
    causal = jnp.tril(jnp.ones((CHUNK, CHUNK), dtype=bool))
    w = jnp.where(causal[None], w_s, jnp.zeros_like(w_s))
    mixed = jnp.einsum('hts,bnshd->bnthd', w, vc) + b_s.T[None, None, :, :, None]
    return u * mixed.reshape(bsz, s, WIDTH_A)

def forgetting_attention(q, k, v, f_logit, b_f):
    bsz, s, _ = q.shape
    nb = s // Q_BLOCK
    to_heads = lambda t: t.reshape(bsz, s, HEADS_B, DH_B).transpose(0, 2, 1, 3)
    q, k, v = to_heads(q), to_heads(k), to_heads(v)
    log_f = jax.nn.log_sigmoid(f_logit.astype(jnp.float32) + b_f.astype(jnp.float32))
    F = jnp.cumsum(log_f, axis=1).transpose(0, 2, 1)
    qb = q.reshape(bsz, HEADS_B, nb, Q_BLOCK, DH_B).transpose(2, 0, 1, 3, 4)
    Fb = F.reshape(bsz, HEADS_B, nb, Q_BLOCK).transpose(2, 0, 1, 3)
    k_pos = jnp.arange(s)
    scale = DH_B ** -0.5

    def block(args):
        qi, Fi, i = args
        q_pos = i * Q_BLOCK + jnp.arange(Q_BLOCK)
        logits = jnp.einsum('bhqd,bhkd->bhqk', qi, k).astype(jnp.float32) * scale
        logits = logits + (Fi[..., :, None] - F[..., None, :])
        logits = jnp.where(q_pos[:, None] >= k_pos[None, :], logits, -jnp.inf)
        p = jax.nn.softmax(logits, axis=-1)
        return jnp.einsum('bhqk,bhkd->bhqd', p.astype(v.dtype), v)

    out = lax.map(block, (qb, Fb, jnp.arange(nb)))
    return out.transpose(1, 0, 3, 2, 4).reshape(bsz, s, WIDTH_B)

def first_inputs(seed: int = 0) -> dict:
    key = jax.random.key(seed)
    ks = jax.random.split(key, 16)
    f32 = jnp.float32
    nrm = lambda k, shape: jax.random.normal(k, shape, dtype=f32)
    row_scale = (1.0 / jnp.sqrt(jnp.arange(1, CHUNK + 1, dtype=f32)))[None, None, :, None]
    b_f = jnp.linspace(1.0, 5.0, HEADS_B, dtype=f32)[None, :] + 0.1 * nrm(ks[11], (DEPTH, HEADS_B))
    return {
        "x": nrm(ks[0], (BATCH, SEQ, D_MODEL)),
        "c": nrm(ks[1], (BATCH, D_MODEL)),
        "norm_g": 1.0 + 0.1 * nrm(ks[2], (DEPTH, D_MODEL)),
        "w_ada": nrm(ks[3], (DEPTH, D_MODEL, 3 * D_MODEL)) * D_MODEL ** -0.5,
        "b_ada": 0.01 * nrm(ks[4], (DEPTH, 3 * D_MODEL)),
        "w_in": nrm(ks[5], (DEPTH, D_MODEL, D_IN)) * D_MODEL ** -0.5,
        "ln_v_g": 1.0 + 0.1 * nrm(ks[6], (DEPTH, WIDTH_A)),
        "ln_v_b": 0.01 * nrm(ks[7], (DEPTH, WIDTH_A)),
        "w_s": nrm(ks[8], (DEPTH, HEADS_A, CHUNK, CHUNK)) * row_scale,
        "b_s": 1.0 + 0.1 * nrm(ks[9], (DEPTH, HEADS_A, CHUNK)),
        "b_f": b_f,
        "w_out": nrm(ks[10], (DEPTH, D_MIX, D_MODEL)) * D_MIX ** -0.5,
        "final_g": 1.0 + 0.1 * nrm(ks[12], (D_MODEL,)),
    }

def first_block(x, c, norm_g, w_ada, b_ada, w_in, ln_v_g, ln_v_b, w_s, b_s, b_f, w_out, final_g):
    cond = jax.nn.silu(c)
    pts = _split_points(SPLIT_SIZES)
    for l in range(DEPTH):
        mod = cond @ w_ada[l] + b_ada[l]
        shift, scale, gate = jnp.split(mod, 3, axis=-1)
        h = rms_norm(x, norm_g[l]) * (1.0 + scale[:, None, :]) + shift[:, None, :]
        z = h @ w_in[l]
        u_a, v_a, g_a, q_b, k_b, v_b, g_b, f_b = jnp.split(z, pts, axis=-1)
        y_a = chunked_spatial_gating(jax.nn.gelu(u_a, approximate=False),
                                     jax.nn.gelu(v_a, approximate=False),
                                     ln_v_g[l], ln_v_b[l], w_s[l], b_s[l]) * jax.nn.silu(g_a)
        y_b = forgetting_attention(q_b, k_b, v_b, f_b, b_f[l]) * jax.nn.silu(g_b)
        y = jnp.concatenate([y_a, y_b], axis=-1) @ w_out[l]
        x = x + gate[:, None, :] * y
    return rms_norm(x, final_g)


DEPTH_2 = 2

GRID_W = 64
CTX_LEN = 256

GLA_HEADS = 4
GLA_DK = 256
GLA_DV = 256
GLA_KEY_W = GLA_HEADS * GLA_DK
GLA_VAL_W = GLA_HEADS * GLA_DV
GLA_GATE_RANK = 16
GLA_TAU = 16.0
GLA_CHUNK = 64

CONV_W = D_MODEL // 2
CONV_K = 3

POOL_W = D_MODEL
POOL_WINDOWS = (2, 4, 8, 16)
POOL_GROUP = POOL_W // len(POOL_WINDOWS)

E_SIZES = (GLA_KEY_W, GLA_VAL_W, GLA_GATE_RANK, GLA_GATE_RANK, GLA_KEY_W, GLA_VAL_W,
           CONV_W, CONV_W, CONV_W, CONV_W)
E_IN = sum(E_SIZES)
E_STATE_COLS = GLA_KEY_W + GLA_VAL_W + 2 * GLA_GATE_RANK
E_MIX = GLA_VAL_W + CONV_W
O_IN = 2 * POOL_W
LN_EPS = 1e-5


def layer_norm_2(x, g, b):
    xf = x.astype(jnp.float32)
    mu = jnp.mean(xf, axis=-1, keepdims=True)
    var = jnp.mean(jnp.square(xf - mu), axis=-1, keepdims=True)
    return ((xf - mu) * lax.rsqrt(var + LN_EPS)).astype(x.dtype) * g + b

def rms_norm_2(x, g):
    xf = x.astype(jnp.float32)
    return xf * lax.rsqrt(jnp.mean(jnp.square(xf), axis=-1, keepdims=True) + LN_EPS) * g.astype(jnp.float32)

def modulation(cond, w, b, n):
    m = jax.nn.silu(cond) @ w[:, :n * D_MODEL] + b[:n * D_MODEL]
    return jnp.split(m, n, axis=-1)

def split_cols(h, sizes):
    idx = [int(i) for i in np.cumsum(sizes)[:-1]]
    return jnp.split(h, idx, axis=-1)

def to_heads(t, d):
    bn, L, _ = t.shape
    return t.reshape(bn, L, -1, d).transpose(0, 2, 1, 3)

def from_heads(t):
    bn, H, L, d = t.shape
    return t.transpose(0, 2, 1, 3).reshape(bn, L, H * d)

def flip_seq(t):
    return jnp.flip(t, axis=2)

def gate_log(r, w, b):
    return jax.nn.log_sigmoid((r @ w + b).astype(jnp.float32)) / GLA_TAU

def gla_chunked(q, k, v, log_a, s0):
    bn, H, L, _ = q.shape
    dv = v.shape[-1]
    C = GLA_CHUNK
    nc = L // C

    def to_chunks(t):
        return jnp.moveaxis(t.astype(jnp.float32).reshape(bn, H, nc, C, t.shape[-1]), 2, 0)

    lower = np.tril(np.ones((C, C), dtype=bool))[:, :, None]

    def step(s, inp):
        qc, kc, vc, lac = inp
        g = jnp.cumsum(lac, axis=-2)
        diff = g[..., :, None, :] - g[..., None, :, :]
        decay = jnp.exp(jnp.where(lower, diff, -jnp.inf))
        scores = jnp.einsum('bhik,bhjk,bhijk->bhij', qc, kc, decay)
        o = (jnp.einsum('bhij,bhjv->bhiv', scores, vc)
             + jnp.einsum('bhik,bhkv->bhiv', qc * jnp.exp(g), s))
        g_last = g[..., -1:, :]
        s_new = (jnp.exp(g_last)[..., 0, :, None] * s
                 + jnp.einsum('bhjk,bhjv->bhkv', kc * jnp.exp(g_last - g), vc))
        return s_new, o

    s_fin, o = lax.scan(step, s0, (to_chunks(q), to_chunks(k), to_chunks(v), to_chunks(log_a)))
    o = jnp.moveaxis(o, 0, 2).reshape(bn, H, L, dv)
    return o, s_fin

def gla_final_state(k, v, log_a):
    g = jnp.cumsum(log_a, axis=-2)
    return jnp.einsum('bhtk,bhtv->bhkv', k * jnp.exp(g[..., -1:, :] - g), v)

def context_states(hs, w_gf, b_gf, w_gb, b_gb):
    k, v, rf, rb = split_cols(hs, E_SIZES[:4])
    k = to_heads(k, GLA_DK).astype(jnp.float32)
    v = to_heads(v, GLA_DV).astype(jnp.float32)
    la_f = to_heads(gate_log(rf, w_gf, b_gf), GLA_DK)
    la_b = to_heads(gate_log(rb, w_gb, b_gb), GLA_DK)
    s_f = gla_final_state(k, v, la_f)
    s_b = gla_final_state(flip_seq(k), flip_seq(v), flip_seq(la_b))
    return s_f, s_b

def conv3_centred(x, w):
    zero = jnp.zeros_like(x[..., :1, :])
    x_prev = jnp.concatenate([zero, x[..., :-1, :]], axis=-2)
    x_next = jnp.concatenate([x[..., 1:, :], zero], axis=-2)
    return w[0] * x_prev + w[1] * x + w[2] * x_next

def centred_window_mean(x, window, axis):
    L = x.shape[axis]
    xf = jnp.moveaxis(x, axis, 0).astype(jnp.float32)
    cs = jnp.concatenate([jnp.zeros_like(xf[:1]), jnp.cumsum(xf, axis=0)], axis=0)
    t = np.arange(L)
    lo = np.clip(t - window // 2, 0, L)
    hi = np.clip(t + window - window // 2, 0, L)
    cnt = (hi - lo).astype(np.float32).reshape((L,) + (1,) * (xf.ndim - 1))
    mean = (cs[hi] - cs[lo]) / cnt
    return jnp.moveaxis(mean, 0, axis).astype(x.dtype)

def even_mixer(h, s0_f, s0_b, w_gf, b_gf, w_gb, b_gb, gla_norm_w, conv_w, w_out, grid):
    bn, L, _ = h.shape
    k, v, rf, rb, q, gate_b, a_b, a_c, a_x, gate_a = split_cols(h, E_SIZES)
    qh = to_heads(q * (GLA_DK ** -0.5), GLA_DK)
    kh = to_heads(k, GLA_DK)
    vh = to_heads(v, GLA_DV)
    la_f = to_heads(gate_log(rf, w_gf, b_gf), GLA_DK)
    la_b = to_heads(gate_log(rb, w_gb, b_gb), GLA_DK)
    o_f, s_f = gla_chunked(qh, kh, vh, la_f, s0_f)
    o_b, s_b = gla_chunked(flip_seq(qh), flip_seq(kh), flip_seq(vh), flip_seq(la_b), s0_b)
    o = rms_norm_2(o_f + flip_seq(o_b), gla_norm_w)
    y_b = from_heads(o).astype(h.dtype) * jax.nn.silu(gate_b)
    u = (a_c * a_x).reshape(bn, grid[0], grid[1], CONV_W)
    u = conv3_centred(u, conv_w).reshape(bn, L, CONV_W)
    y_a = a_b * u * jax.nn.silu(gate_a)
    return jnp.concatenate([y_b, y_a], axis=-1) @ w_out, s_f, s_b

def odd_mixer(h, w_pool, pool_scale, w_out, grid):
    bn, L, _ = h.shape
    xp, gate = jnp.split(h, 2, axis=-1)
    xg = xp.reshape(bn, grid[0], grid[1], POOL_W)
    groups = jnp.split(xg, len(POOL_WINDOWS), axis=-1)
    z = jnp.stack([centred_window_mean(g, w, 1) - g for g, w in zip(groups, POOL_WINDOWS)], axis=-2)
    z = jnp.einsum('brcgi,gio->brcgo', z, w_pool).reshape(bn, L, POOL_W) * pool_scale
    return (z * jax.nn.silu(gate)) @ w_out

def second_inputs(seed: int = 0) -> dict:
    key = jax.random.key(seed)
    ks = jax.random.split(key, 20)
    ne = (DEPTH_2 + 1) // 2
    no = DEPTH_2 // 2
    beta = (8.0 * DEPTH_2) ** -0.25

    def nrm(k, shape, s):
        return jax.random.normal(k, shape, jnp.float32) * s

    return {
        'x': nrm(ks[0], (BATCH, SEQ, D_MODEL), 1.0),
        'c': nrm(ks[1], (BATCH, D_MODEL), 1.0),
        'ctx': nrm(ks[2], (BATCH, CTX_LEN, D_MODEL), 1.0),
        'c_ctx': nrm(ks[3], (D_MODEL,), 1.0),
        'w_ada': nrm(ks[4], (DEPTH_2, D_MODEL, 3 * D_MODEL), 0.5 * D_MODEL ** -0.5),
        'b_ada': nrm(ks[5], (DEPTH_2, 3 * D_MODEL), 0.02),
        'ln_g': 1.0 + nrm(ks[6], (DEPTH_2, D_MODEL), 0.02),
        'ln_b': nrm(ks[7], (DEPTH_2, D_MODEL), 0.02),
        'w_in_e': nrm(ks[8], (ne, D_MODEL, E_IN), D_MODEL ** -0.5),
        'w_gate_f': nrm(ks[9], (ne, GLA_GATE_RANK, GLA_KEY_W), GLA_GATE_RANK ** -0.5),
        'b_gate_f': nrm(ks[10], (ne, GLA_KEY_W), 0.1),
        'w_gate_b': nrm(ks[11], (ne, GLA_GATE_RANK, GLA_KEY_W), GLA_GATE_RANK ** -0.5),
        'b_gate_b': nrm(ks[12], (ne, GLA_KEY_W), 0.1),
        'gla_norm_w': 1.0 + nrm(ks[13], (ne, GLA_DV), 0.02),
        'conv_w': nrm(ks[14], (ne, CONV_K, CONV_W), CONV_K ** -0.5),
        'w_out_e': nrm(ks[15], (ne, E_MIX, D_MODEL), beta * E_MIX ** -0.5),
        'w_in_o': nrm(ks[16], (no, D_MODEL, O_IN), D_MODEL ** -0.5),
        'w_pool': nrm(ks[17], (no, len(POOL_WINDOWS), POOL_GROUP, POOL_GROUP), POOL_GROUP ** -0.5),
        'pool_scale': 1.0 + nrm(ks[18], (no, POOL_W), 0.02),
        'w_out_o': nrm(ks[19], (no, POOL_W, D_MODEL), beta * POOL_W ** -0.5),
    }

def second_block(x, c, ctx, c_ctx, w_ada, b_ada, ln_g, ln_b, w_in_e, w_gate_f, b_gate_f,
              w_gate_b, b_gate_b, gla_norm_w, conv_w, w_out_e, w_in_o, w_pool, pool_scale, w_out_o):
    alpha = (2.0 * DEPTH_2) ** 0.25
    bn, L, _ = x.shape
    rows = L // GRID_W
    lc = ctx.shape[1]
    c_lat = c[:, None, :]
    c_c = c_ctx[None, None, :]
    s_zero = jnp.zeros((bn, GLA_HEADS, GLA_DK, GLA_DV), jnp.float32)
    ctx_s = ctx
    for i in range(DEPTH_2):
        j = i // 2
        ctx_needed = any(l % 2 == 0 for l in range(i + 1, DEPTH_2))
        sh, sc, gt = modulation(c_lat, w_ada[i], b_ada[i], 3)
        u = x * (1.0 + sc) + sh
        if i % 2 == 0:
            if ctx_needed:
                sh_c, sc_c, gt_c = modulation(c_c, w_ada[i], b_ada[i], 3)
                uc = ctx_s * (1.0 + sc_c) + sh_c
                yc, s_f, s_b = even_mixer(uc @ w_in_e[j], s_zero, s_zero, w_gate_f[j], b_gate_f[j],
                                          w_gate_b[j], b_gate_b[j], gla_norm_w[j], conv_w[j],
                                          w_out_e[j], (1, lc))
                ctx_s = layer_norm_2(alpha * ctx_s + gt_c * yc, ln_g[i], ln_b[i])
            else:
                sh_c, sc_c = modulation(c_c, w_ada[i], b_ada[i], 2)
                uc = ctx_s * (1.0 + sc_c) + sh_c
                s_f, s_b = context_states(uc @ w_in_e[j][:, :E_STATE_COLS], w_gate_f[j], b_gate_f[j],
                                          w_gate_b[j], b_gate_b[j])
            y, _, _ = even_mixer(u @ w_in_e[j], s_f, s_b, w_gate_f[j], b_gate_f[j], w_gate_b[j],
                                 b_gate_b[j], gla_norm_w[j], conv_w[j], w_out_e[j], (rows, GRID_W))
        else:
            if ctx_needed:
                sh_c, sc_c, gt_c = modulation(c_c, w_ada[i], b_ada[i], 3)
                uc = ctx_s * (1.0 + sc_c) + sh_c
                yc = odd_mixer(uc @ w_in_o[j], w_pool[j], pool_scale[j], w_out_o[j], (lc, 1))
                ctx_s = layer_norm_2(alpha * ctx_s + gt_c * yc, ln_g[i], ln_b[i])
            y = odd_mixer(u @ w_in_o[j], w_pool[j], pool_scale[j], w_out_o[j], (rows, GRID_W))
        x = layer_norm_2(alpha * x + gt * y, ln_g[i], ln_b[i])
    return x


def setup_inputs(seed=0):
    out = dict(first_inputs(seed))
    for name, value in second_inputs(seed + 1).items():
        if name != "x":
            out[name + "_2"] = value
    return out


def reference(
    x, c, norm_g, w_ada, b_ada, w_in, ln_v_g, ln_v_b, w_s, b_s, b_f, w_out, final_g, c_2, ctx_2,
    c_ctx_2, w_ada_2, b_ada_2, ln_g_2, ln_b_2, w_in_e_2, w_gate_f_2, b_gate_f_2, w_gate_b_2,
    b_gate_b_2, gla_norm_w_2, conv_w_2, w_out_e_2, w_in_o_2, w_pool_2, pool_scale_2, w_out_o_2,
):
    x = first_block(
        x, c, norm_g, w_ada, b_ada, w_in, ln_v_g, ln_v_b, w_s, b_s, b_f, w_out, final_g,
    )
    return second_block(
        x, c_2, ctx_2, c_ctx_2, w_ada_2, b_ada_2, ln_g_2, ln_b_2, w_in_e_2, w_gate_f_2,
        b_gate_f_2, w_gate_b_2, b_gate_b_2, gla_norm_w_2, conv_w_2, w_out_e_2, w_in_o_2,
        w_pool_2, pool_scale_2, w_out_o_2,
    )


_drawn_inputs = setup_inputs


def setup_inputs(seed=0):
    import zlib

    import numpy as np

    out = dict(_drawn_inputs(seed))
    spreads = {}
    factors = {'b_ada': 4.917,
     'ln_v_b': 8.0,
     'ctx_2': 8.0,
     'c_ctx_2': 8.0,
     'b_ada_2': 6.424,
     'w_gate_f_2': 8.0,
     'b_gate_f_2': 8.0,
     'w_gate_b_2': 8.0,
     'b_gate_b_2': 8.0,
     'gla_norm_w_2': 47.913,
     'pool_scale_2': 46.305}
    for name, (base, spread) in spreads.items():
        noise = np.random.default_rng([zlib.crc32(name.encode()), seed]).standard_normal(out[name].shape)
        drawn = base * np.exp(spread * noise) if base else spread * noise
        out[name] = jnp.asarray(drawn.astype(out[name].dtype))
    for name, factor in factors.items():
        out[name] = (out[name] * factor).astype(out[name].dtype)
    return out
```

```python
import numpy as np
import concourse.bass as bass
from concourse import mybir

P = 128
D = 2048
S = 512
SC = 256
KT = D // P
GC = 512
NT = S // P
NTC = SC // P
EPS, LN_EPS = 1e-6, 1e-5
ALPHA = float(np.float32(4.0 ** 0.25))
TAU = 16.0
HEADS_A, HEADS_B, DH_B = 8, 16, 64
GLA_HEADS, DK = 4, 256
GRID_R, GRID_W = 8, 64
LEVELS = (64, 32, 16, 8, 4, 2, 1)
RING = 4
RAW = 4
NEG = -1.0e30

B1, E_IN = "w_in", "w_in_e_2"


def plan():
    g = []

    def add(name, w, col, n, mode, operand, kt=KT, tile0=0, tok=S, width=GC):
        for i in range(n):
            g.append(dict(name=name, i=i, n=n, w=w, col=col + GC * i, width=width, mode=mode,
                          operand=operand, kt=kt, tile0=tile0 + 4 * i if kt < KT else 0, tok=tok, part=None))

    add("va", B1, 1024, 2, "N", 0)
    add("f", B1, 7072, 1, "T", 0, width=112)
    add("q", B1, 3072, 2, "T", 0)
    add("k", B1, 4096, 2, "T", 0)
    add("v", B1, 5120, 2, "N", 0)
    add("ua", B1, 0, 2, "T", 0)
    add("ga", B1, 2048, 2, "T", 0)
    add("gb", B1, 6144, 2, "T", 0)
    add("wo1", "w_out", 0, 4, "T", 1)
    add("cr", E_IN, 2048, 1, "T", 2, tok=SC, width=P)
    add("ck", E_IN, 0, 2, "N", 2, tok=SC)
    add("cv", E_IN, 1024, 2, "N", 2, tok=SC)
    add("r", E_IN, 2048, 1, "T", 3, width=P)
    add("ek", E_IN, 0, 2, "T", 3)
    add("eq", E_IN, 2080, 2, "T", 3)
    add("ev", E_IN, 1024, 2, "N", 3)
    add("beside", E_IN, 4128, 2 * GLA_HEADS, "T", 3)
    add("egb", E_IN, 3104, 2, "T", 3)
    add("wo2", "w_out_e_2", 0, 4, "T", 4)
    add("xp", "w_in_o_2", 0, 4, "T", 5)
    add("gt", "w_in_o_2", 2048, 4, "T", 5)
    for i in range(4):
        g.append(dict(name="pool", i=i, n=4, w=f"w_pool_2.{i}", col=0, width=GC, mode="T", operand=6,
                      kt=4, tile0=4 * i, tok=S, part=None))
    add("wo3", "w_out_o_2", 0, 4, "T", 7)
    first = {}
    kc = 0
    for n, x in enumerate(g):
        x["kc"] = kc
        kc += x["kt"]
        first.setdefault(x["name"], n)
    total = kc
    n0, n1, n2 = first["va"], first["r"], first["wo2"]
    for j in range(16):
        g[n0 + j]["part"] = 8 + j
    for j in range(6):
        g[n1 + j]["part"] = 24 + j
        g[n2 + j]["part"] = 30 + j
    return g, first, total


GROUPS, FIRST, CHUNKS = plan()
DVE_EVAC = ("wo1", "wo2", "wo3", "xp", "pool")
N_START = 8
VEC = {}
_at = 0
for _n, _k in (("c", 16), ("c2", 16), ("cc", 16), ("norm_g", 16), ("final_g", 16), ("b_ada", 144),
               ("ln_g", 32), ("ln_b", 32), ("gla_w", 2), ("conv", 24), ("pool_s", 16)):
    VEC[_n] = _at
    _at += _k
NVEC = _at


T_ENTER, T_LOGIT, T_DIAGONAL = 1, 4, 3
T_LEVEL = [2 if n % 3 == 2 and n < 12 else 1 for n in range(2 * len(LEVELS))]
T_CROSS, T_TAKEN, T_OUT = 4, 1, 1
T_HEAD = T_ENTER + T_LOGIT + T_DIAGONAL
assert T_HEAD + sum(T_LEVEL) + T_CROSS + T_TAKEN + T_OUT == 2 * KT


def level_tiles(n):
    return T_HEAD + sum(T_LEVEL[:n + 1]) if n >= 0 else T_HEAD + n + 1


N_CONST = 7 * P + S
TMP = 0
AT_X_TOK, AT_START, AT_WS_RAW = 0, 8192, 16384
AT_VA, AT_K, AT_V, AT_WST, AT_BS, AT_F, AT_FQ = 2048, 6144, 10240, 14336, 15360, 16384, 16896
AT_NEGF, AT_LOGIT, AT_PT, AT_OTOK, AT_KST, AT_QST = 2048, 3072, 4096, 5120, 5632, 0
AT_XRES, AT_SQ, AT_RSTD = 2048, 4096, 8192
AT_CTOK, AT_KC, AT_VC, AT_RC, AT_WGC = 8704, 8704, 10752, 12800, 13056
AT_LAC, AT_TC, AT_STO = 0, 4096, 13056
AT_RT, AT_WG, AT_VE, AT_ST, AT_VH, AT_G, AT_E, AT_M, AT_AM, AT_R, AT_QB = (
    2048, 2560, 3072, 7168, 8192, 9216, 10240, 11264, 13312, 15360, 15872)
AT_CONV, CONV_SLOTS = 3072, 7
AT_ROWS, AT_GATE = 2048, 4352
AT_OUT = 8704
ARENA = 17408


class Build:

    def __init__(self, nc, A, out):
        self.nc, self.A, self.out = nc, A, out
        f32, f32r, u8 = mybir.dt.float32, mybir.dt.float32r, mybir.dt.uint8

        def sb(name, shape, dt=f32):
            return nc.alloc_sbuf_tensor(name, shape, dt)

        self.op_hi = sb("op_hi", [P, KT, S], f32r)
        self.op_lo = sb("op_lo", [P, KT, S], f32r)
        self.Y = sb("Y", [P, KT, S])
        self.w_raw = sb("w_raw", [P, RAW, 2, GC])
        self.w_hi = sb("w_hi", [P, RING, GC], f32r)
        self.w_lo = sb("w_lo", [P, RING, GC], f32r)
        self.a_raw = sb("a_raw", [P, 2, 2, GC])
        self.acc = sb("acc", [P, 2, 2, GC])
        self.const = sb("const", [P, N_CONST])
        self.masks = sb("masks", [P, 2 * len(LEVELS), P], u8)
        self.vec = sb("vec", [P, NVEC])
        self.mod = sb("mod", [P, 144 + 32])
        self.bf = sb("bf", [P, 1])
        self.small = sb("small", [P, 96])
        self.arena = sb("arena", [P, ARENA])
        self.ps = nc.alloc_psum_tensor("ps", [P, 8, GC], f32)
        c = self.const
        self.ident, self.ones = c[:, 0:P], c[:, P:2 * P]
        self.tri_gt, self.tri_lt = c[:, 2 * P:3 * P], c[:, 3 * P:4 * P]
        self.causal, self.eye2 = c[:, 4 * P:5 * P], c[:, 5 * P:6 * P]
        self.tri_le = c[:, 6 * P:7 * P]
        self.restart = c[:, 7 * P:7 * P + S]
        self.x_sp = nc.dram_tensor("x_spill", (P, KT, S), f32, kind="Internal").ap()
        self.f_sp = nc.dram_tensor("f_spill", (HEADS_B, S), f32, kind="Internal").ap()
        self.s_sp = nc.dram_tensor("state_spill", (P, GLA_HEADS, 4 * DK), f32, kind="Internal").ap()
        self.c_sp = nc.dram_tensor("conv_spill", (P, 2 * GLA_HEADS, 4 * S), f32, kind="Internal").ap()
        self.sems = {}
        self.bank_free = [self.sem("even_banks_free"), self.sem("odd_banks_free")]
        self.w_in = [self.sem(f"weights_in_{i}") for i in range(RAW)]
        self.a_in = [self.sem(f"modulation_in_{i}") for i in range(2)]
        self.start_in = [self.sem(f"start_in_{i}") for i in range(8)]

    def at(self, word, *shape):
        n = 1
        for k in shape:
            n *= k
        assert word + n <= ARENA, (word, shape)
        v = self.arena[:, word:word + n]
        if len(shape) == 2:
            v = v.rearrange("p (a b) -> p a b", a=shape[0])
        if len(shape) == 3:
            v = v.rearrange("p (a b c) -> p a b c", a=shape[0], b=shape[1])
        return v

    def sem(self, name):
        if name not in self.sems:
            self.sems[name] = self.nc.alloc_semaphore(name)
        return self.sems[name]

    def weight(self, g):
        name, _, part = g["w"].partition(".")
        w = self.A[name]
        w = w[0, int(part)] if part else w[0]
        return w.rearrange("(k p) n -> p k n", p=P)


def ordinal(n):
    return sum(x["part"] is not None for x in GROUPS[:n])


def ctx_part(part):
    return 12 <= part < 20


TMP_USERS = ("ua", "ga", "gb", "egb")


def tmp_uses(n):
    return sum(x["name"] in TMP_USERS for x in GROUPS[:n])


def sync_program(B, sp):
    A, sem, at = B.A, B.sem, B.at

    rows = B.Y[:, 15, :].rearrange("p (r c) -> p r c", c=P)
    loads = 0

    def vector(name, src):
        nonlocal loads
        k, n = VEC[name], src.shape[0]
        while n:
            r, q = divmod(k, P)
            m = min(n, P - q)
            sp.dma_start(rows[q:q + m, r, :], src[0:m, :]).then_inc(sem("rows_in"), 16)
            loads += 1
            k, n = k + m, n - m
            src = src[m:, :] if n else src

    cut = lambda a: a.rearrange("(k p) -> k p", p=P)
    vector("c", cut(A["c"][0]))
    vector("c2", cut(A["c_2"][0]))
    vector("cc", cut(A["c_ctx_2"]))
    vector("norm_g", cut(A["norm_g"][0]))
    vector("final_g", cut(A["final_g"]))
    vector("b_ada", cut(A["b_ada"][0]))
    VEC["b_ada_2"] = VEC["b_ada"] + 48
    vector("b_ada_2", A["b_ada_2"].rearrange("l (k p) -> (l k) p", p=P))
    vector("ln_g", A["ln_g_2"].rearrange("l (k p) -> (l k) p", p=P))
    vector("ln_b", A["ln_b_2"].rearrange("l (k p) -> (l k) p", p=P))
    vector("gla_w", cut(A["gla_norm_w_2"][0]))
    vector("conv", A["conv_w_2"][0].rearrange("t (k p) -> (t k) p", p=P))
    vector("pool_s", cut(A["pool_scale_2"][0]))
    assert loads == N_ROW_LOADS, loads
    sp.dma_start(B.const[:, :], A["const"]).then_inc(sem("const_in"), 16)

    ring = at(AT_START, 8, 1024)
    w_ada = A["w_ada"][0].rearrange("(k p) n -> p k n", p=P)
    for n in range(64):
        pair, kt = divmod(n, KT)
        if n >= 8:
            sp.wait_ge(sem("acc_step"), start_step(n - 8))
        sp.dma_start(ring[:, n % 8, :], w_ada[:, kt, pair * 1024:(pair + 1) * 1024]).then_inc(B.start_in[n % 8], 16)
        if n == 7:
            sp.dma_start(at(AT_X_TOK, NT, D), A["x"][0].rearrange("(n p) d -> p n d", p=P)).then_inc(sem("x_in"), 16)
            sp.dma_start(at(AT_WS_RAW, HEADS_A, P), A["w_s"][0].rearrange("h t s -> t h s")).then_inc(sem("ws_in"), 16)
            sp.dma_start(B.bf[96:112, :], A["b_f"].rearrange("o h -> h o")).then_inc(sem("bf_in"), 16)
            sp.dma_start(B.a_raw[:, :, :, :].rearrange("p a b c -> p (a b c)")[:, 0:2 * len(LEVELS) * P],
                         A["masks"]).then_inc(sem("masks_in"), 16)
    sp.wait_ge(sem("x_turned"), KT)
    sp.dma_start(B.x_sp, B.Y[:, :, :]).then_inc(sem("spilled"), 16)

    def spill_stream(m):
        sp.wait_ge(sem("scaled"), 4 * (m + 1))
        sp.dma_start(B.x_sp, B.Y[:, :, :]).then_inc(sem("spilled"), 16)

    def weights(n, m, r=0):
        g = GROUPS[n]
        slot = (g["kc"] // 2 + m) % RAW
        if g["kc"] + 2 * m >= 2 * RAW:
            sp.wait_ge(sem("lo_done"), r * 8 + (g["kc"] + 2 * m - 2 * RAW + 2))
        tiles = slice(2 * m, 2 * m + 2) if isinstance(r, int) else bass.ds(r * 8 + 2 * m, 2)
        sp.dma_start(B.w_raw[:, slot, :, 0:g["width"]],
                     B.weight(g)[:, tiles, g["col"]:g["col"] + g["width"]]).then_inc(B.w_in[slot], 16)

    def modulation(n, m):
        part, o = GROUPS[n]["part"], ordinal(n)
        if part is None:
            return
        src = A["w_ada"][0] if part < 12 else A["w_ada_2"][(part - 12) // 12]
        src = src.rearrange("(k p) n -> p k n", p=P)
        c = part % 12 * GC
        if o or m >= 2:
            sp.wait_ge(sem("part_tile"), KT * o + 2 * m - 2)
        sp.dma_start(B.a_raw[:, m % 2, :, :], src[:, 2 * m:2 * m + 2, c:c + GC]).then_inc(B.a_in[m % 2], 16)

    def stream(n, middle=None):
        pairs = GROUPS[n]["kt"] // 2
        before = n and GROUPS[n - 1]["part"] is not None
        if GROUPS[n]["part"] is None and not before and not middle and pairs == 8 and GROUPS[n]["name"] != "egb":
            with sp.Fori(0, 2) as r:
                for m in range(4):
                    weights(n, m, r)
            return
        for m in range(pairs):
            weights(n, m)
            if GROUPS[n]["name"] == "egb":
                conv_loads(GROUPS[n]["i"], m)
            if m < LAG and before and not (middle and m == 2):
                modulation(n - 1, 8 - LAG + m)
            if middle and m == 1:
                if before:
                    modulation(n - 1, 7)
                middle()
            if m >= LAG:
                modulation(n, m - LAG)

    def residual(n):
        i = GROUPS[n]["i"]
        if i == 0:
            if GROUPS[n]["name"] == "wo2":
                sp.wait_ge(sem("conv_done"), 8)
            sp.wait_ge(sem("spilled"), 16 * (1 + ("wo1", "wo2", "wo3").index(GROUPS[n]["name"])))
            sp.wait_ge(B.bank_free[(n - 1) % 2], (n - 1) // 2 + 1)
        else:
            sp.wait_ge(B.bank_free[(n - 1) % 2], (n - 1) // 2 + 1)
        sp.dma_start(at(AT_XRES, 4, S), B.x_sp[:, 4 * i:4 * i + 4, :]).then_inc(sem("residual_in"), 16)

    def attention_loads():
        sp.wait_ge(sem("mixed"), HEADS_A)
        for h in range(2):
            sp.dma_start(at(AT_NEGF, 2, S)[:, h, :], B.f_sp[h:h + 1, :].to_broadcast([P, S])).then_inc(B.sem(f"f_row_in_{h}"), 16)
        with sp.Fori(1, HEADS_B // 2) as i:
            for h in range(2):
                sp.wait_ge(sem("logits"), i * 8 + (4 * h - 4))
                sp.dma_start(at(AT_NEGF, 2, S)[:, h, :],
                             B.f_sp[bass.ds(i * 2 + h, 1), :].to_broadcast([P, S])).then_inc(B.sem(f"f_row_in_{h}"), 16)

    def state_stores():
        spill_stream(1)
        sp.wait_ge(sem("states_out"), 1)
        sp.dma_start(B.s_sp.rearrange("p h w -> p (h w)"), at(AT_STO, 1, 4096)[:, 0, :]).then_inc(sem("states_spilled"), 16)

    def head_loads(i):
        at_int = isinstance(i, int)
        gate_weights(B, sp, at(AT_WG, 2, DK), slice(0, DK) if at_int else bass.ds(i * DK, DK), sem("head_in"))
        sp.dma_start(at(AT_ST, 1, 4 * DK)[:, 0, :], B.s_sp[:, i, :] if at_int else
                     B.s_sp[:, bass.ds(i, 1), :].rearrange("p o w -> p (o w)")).then_inc(sem("head_in"), 16)

    def beside_store(k, i):
        sp.wait_ge(sem("beside_left"), i * 8 + (4 * k + 8))
        rows = B.c_sp[:, 2 * i + k, :] if isinstance(i, int) else \
            B.c_sp[:, bass.ds(i * 2 + k, 1), :].rearrange("p o w -> p (o w)")
        sp.dma_start(rows, B.a_raw[:, :, :, :].rearrange("p a b c -> p (a b c)")).then_inc(sem("beside_stored"), 16)

    def head_turn(i):
        g = GROUPS[FIRST["beside"]]
        for m in range(KT):
            slot = (g["kc"] // 2 + m) % RAW
            sp.wait_ge(sem("lo_done"), i * 32 + (g["kc"] + 2 * m - 2 * RAW + 2))
            col = g["col"] + m // 8 * GC
            cols = slice(col, col + GC) if isinstance(i, int) else bass.ds(i * 2 * GC + col, GC)
            sp.dma_start(B.w_raw[:, slot, :, :], B.weight(g)[:, 2 * (m % 8):2 * (m % 8) + 2, cols])\
                .then_inc(B.w_in[slot], 16)
            if m == 1 and isinstance(i, int):
                state_in()
            if m == 5 and not isinstance(i, int):
                sp.wait_ge(sem("o_mm"), i)
                head_loads(i)
                beside_store(1, i - 1)
            if m == 12:
                beside_store(0, i)

    def state_in():
        sp.wait_ge(sem("states_spilled"), 16)
        sp.wait_ge(sem("gates_cleared"), 2)
        head_loads(0)

    def conv_loads(i, m):
        if i == 0 and m == 3:
            sp.wait_ge(sem("heads_done"), GLA_HEADS + 1)
            beside_store(1, GLA_HEADS - 1)
            sp.wait_ge(sem("beside_stored"), 16 * (2 * GLA_HEADS + 1))
        j = m - 3 if i == 0 else m + 5
        if 0 <= j < 8:
            if j >= CONV_SLOTS:
                sp.wait_ge(sem("conv_done"), j - CONV_SLOTS + 1)
            src = B.c_sp.rearrange("p (v h) (t s) -> p v (h t) s", v=4, t=4)
            sp.dma_start(at(AT_CONV, CONV_SLOTS, 4, S)[:, j % CONV_SLOTS, :, :], src[:, :, j, :])\
                .then_inc(B.sem(f"conv_in_{j}"), 16)

    middles = {FIRST["ua"]: attention_loads, FIRST["r"]: state_stores,
               FIRST["xp"]: lambda: spill_stream(2)}
    sp.wait_ge(sem("masks_made"), 1)
    sp.wait_ge(sem("acc_step"), start_step(63))
    sp.dma_start(at(AT_BS, 1, HEADS_A * P)[:, 0, :],
                 A["b_s"].rearrange("o h t -> o (h t)").to_broadcast([P, HEADS_A * P])).then_inc(sem("bs_in"), 16)
    names = [x["name"] for x in GROUPS]
    for n, name in enumerate(names):
        g = GROUPS[n]
        if name == "beside":
            if g["i"] == 0:
                head_turn(0)
                with sp.Fori(1, GLA_HEADS) as i:
                    head_turn(i)
            continue
        if name == "va" and g["i"] == 1:
            sp.wait_ge(sem("op_tile"), KT)
            for r, v in enumerate(("ln_v_g", "ln_v_b")):
                sp.dma_start(at(TMP, 2, 1024)[:, r, :], A[v].to_broadcast([P, 1024])).then_inc(sem("ln_rows_in"), 16)
        stream(n, middles.get(n))
        if name == "q" and g["i"] == 0:
            sp.wait_ge(sem("f_summed"), 1)
            sp.dma_start(B.f_sp, B.arena[96:112, AT_F:AT_F + S]).then_inc(sem("f_spilled"), 16)
            sp.wait_ge(sem("f_spilled"), 16)
            for b in range(NT):
                sp.dma_start(at(AT_FQ, NT, HEADS_B)[:, b, :],
                             B.f_sp[:, b * P:(b + 1) * P].rearrange("h p -> p h")).then_inc(sem("f_cols_in"), 16)
        if name in ("wo1", "wo2", "wo3"):
            residual(n)
        if name == "wo1" and g["i"] == 3:
            sp.dma_start(at(AT_CTOK, NTC, D), A["ctx_2"][0].rearrange("(n p) d -> p n d", p=P)).then_inc(sem("ctx_in"), 16)
        if name == "cr":
            sp.wait_ge(sem("gates_cleared"), 1)
            gate_weights(B, sp, at(AT_WGC, 2, 1024), slice(0, 1024), sem("ctx_gates_in"))
    for t in range(NT):
        sp.wait_ge(sem("out_rows"), t + 1)
        sp.dma_start(B.out[0, t * P:(t + 1) * P, :], at(AT_OUT, 2, D)[:, t % 2, :]).then_inc(sem(f"out_done_{t % 2}"), 16)
    for k in range(2):
        sp.wait_ge(sem(f"out_done_{k}"), 16 * NT // 2)


def gate_weights(B, sp, dst, cols, signal):
    for d, (w, b) in enumerate((("w_gate_f_2", "b_gate_f_2"), ("w_gate_b_2", "b_gate_b_2"))):
        sp.dma_start(dst[16 * d:16 * d + 16, d, :], B.A[w][0][:, cols]).then_inc(signal, 16)
        sp.dma_start(dst[32:33, d, :], B.A[b][0:1, cols]).then_inc(signal, 16)


N_ROW_LOADS = 12
LAG = 3


def start_step(n):
    pair, kt = divmod(n, KT)
    return 34 * pair + 2 + 2 * (kt + 1)


def pool_program(B, pool):
    nc, sem, at = B.nc, B.sem, B.at
    n = FIRST["wo1"]
    pool.wait_ge(B.bank_free[n % 2], n // 2 + 1)
    nc.gpsimd.memset(at(AT_WGC, 1, 2048)[0:33, 0, :], 0.0)
    nc.gpsimd.drain()
    nc.gpsimd.memset(B.arena[32:33, AT_RC:AT_RC + SC], 1.0)
    nc.gpsimd.drain()
    nc.gpsimd.memset(B.small[0:1, 95:96], 0.0).then_inc(sem("gates_cleared"), 1)
    pool.wait_ge(sem("states_out"), 1)
    nc.gpsimd.memset(at(AT_WG, 1, 512)[0:33, 0, :], 0.0)
    nc.gpsimd.drain()
    nc.gpsimd.memset(B.arena[32:33, AT_RT:AT_RT + S], 1.0)
    nc.gpsimd.drain()
    nc.gpsimd.memset(B.small[0:1, 95:96], 0.0).then_inc(sem("gates_cleared"), 1)


def scalar_program(B, act):
    nc, sem, at, ps, Y = B.nc, B.sem, B.at, B.ps, B.Y
    ACT = mybir.ActivationFunctionType
    f32 = mybir.dt.float32
    Act = nc.scalar.activation

    def high_tile(c, width):
        raw, fill = c // 2 % RAW, c // (2 * RAW)
        if c % 2 == 0:
            act.wait_ge(B.w_in[raw], 16 * (fill + 1))
        if c >= RING:
            act.wait_ge(sem("w_used"), c - RING + 1)
        Act(B.w_hi[:, c % RING, 0:width], B.w_raw[:, raw, c % 2, 0:width], ACT.Copy).then_inc(sem("hi_done"), 1)

    def ahead(n):
        c, k, width = GROUPS[n]["kc"], GROUPS[n]["kt"], GROUPS[n]["width"]
        after = GROUPS[n + 1]["width"] if n + 1 < len(GROUPS) else 0
        if k == KT and after == width:
            with act.Fori(0, 2) as r:
                for t in range(c + 4, c + 12):
                    raw = t // 2 % RAW
                    if t % 2 == 0:
                        act.wait_ge(B.w_in[raw], r * 16 + 16 * (t // (2 * RAW) + 1))
                    act.wait_ge(sem("w_used"), r * 8 + (t - RING + 1))
                    Act(B.w_hi[:, t % RING, 0:width], B.w_raw[:, raw, t % 2, 0:width],
                        ACT.Copy).then_inc(sem("hi_done"), 1)
        else:
            for t in range(c + 4, c + k):
                high_tile(t, width)
            if after:
                for t in range(c + k, c + k + 4):
                    high_tile(t, after)

    def conv_ahead(n):
        for t in range(KT):
            high_tile(GROUPS[n]["kc"] + 4 + t, GC)
            for j in range(8):
                if CONV_AT[j] == (GROUPS[n]["i"], t):
                    act.wait_ge(sem(f"conv_in_{j}"), 16)
                    x = at(AT_CONV, CONV_SLOTS, 4, S)[:, j % CONV_SLOTS, 3, :]
                    Act(x, x, ACT.Silu).then_inc(sem("conv_gate"), 1)

    def split_hi(operand, src, tok=S, tiles=KT, ready=None):
        if operand:
            last = max(x["kc"] + x["kt"] for x in GROUPS if x["operand"] == operand - 1)
            act.wait_ge(sem("w_used"), last)
        for t in range(tiles):
            Act(B.op_hi[:, t, 0:tok], src(t), ACT.Copy).then_inc(sem("op_high"), 1)

    def from_mod(operand, tok=S):
        def src(t):
            act.wait_ge(sem("modulated"), modulated(operand) + t + 1)
            return at(TMP, 4, S)[:, t % 4, 0:tok]
        split_hi(operand, src, tok)

    def from_y(operand, first=0, tiles=KT):
        def src(t):
            return Y[:, t, :]
        split_hi(operand, src)

    def norm(m):
        sqr = at(AT_SQ, 2, 2048)
        for j in range(4):
            if m >= 2:
                act.wait_ge(sem("centred"), 4 * (m - 2) + j + 1)
            elif m == 1:
                n = FIRST["wo1"] + j
                act.wait_ge(B.bank_free[n % 2], n // 2 + 1)
            if m == 0:
                act.wait_ge(sem("x_turned"), 4 * j + 4)
            k = 4 * m + j
            if j >= 2:
                act.wait_ge(sem("squares_summed"), k - 1)
            Act(sqr[:, j % 2, :], Y[:, 4 * j:4 * j + 4, :].rearrange("p a b -> p (a b)"),
                ACT.Square).then_inc(sem("squared"), 1)
        act.wait_ge(sem("variance"), m + 1)
        Act(at(AT_RSTD, 1, S)[:, 0, :], at(AT_RSTD, 1, S)[:, 0, :], ACT.Sqrt).then_inc(sem("deviation"), 1)
        gain = VEC["norm_g"] if m == 0 else VEC["final_g"] if m == 1 else VEC["ln_g"] + 16 * (m - 2)
        for j in range(4):
            act.wait_ge(sem("normed"), 4 * m + j + 1)
            for t in range(4 * j, 4 * j + 4):
                scale = B.vec[:, gain + t:gain + t + 1]
                if m < 2:
                    last = Act(Y[:, t, :], Y[:, t, :], ACT.Copy, scale=scale)
                else:
                    b = VEC["ln_b"] + 16 * (m - 2) + t
                    last = Act(Y[:, t, :], Y[:, t, :], ACT.Identity, scale=scale, bias=B.vec[:, b:b + 1])
            last.then_inc(sem("scaled"), 1)

    act.wait_ge(sem("columns"), 1)
    Act(B.vec[:, :], ps[:, 0, 0:NVEC], ACT.Copy)
    nc.scalar.drain()
    Act(B.vec[:, 0:48], B.vec[:, 0:48], ACT.Silu).then_inc(sem("vec_ready"), 1)
    for t in range(KT):
        act.wait_ge(sem("turned"), t + 1)
        Act(Y[:, t, :], ps[:, 1 + t % 4, :], ACT.Copy).then_inc(sem("x_turned"), 1)
    norm(0)
    from_mod(0)
    for s in range(4):
        high_tile(s, GC)

    for n, g in enumerate(GROUPS):
        name, i = g["name"], g["i"]
        if name == "beside":
            if i == 0:
                gla_scalar(B, act)
            continue
        if name == "egb":
            conv_ahead(n)
        else:
            ahead(n)
        bank = 4 * (n % 2)
        free = B.bank_free[n % 2]
        if name not in DVE_EVAC:
            act.wait_ge(sem("w_used"), g["kc"] + g["kt"])
        banks = ps[:, bank:bank + 4, :]
        if name == "va":
            Act(at(AT_VA, NT, 1024)[:, :, i * GC:(i + 1) * GC], banks, ACT.Gelu).then_inc(free, 1)
            if i == 1:
                act.wait_ge(sem("value_variance"), 1)
                Act(B.small[:, 0:4], B.small[:, 0:4], ACT.Sqrt).then_inc(sem("value_deviation"), 1)
        if name == "f":
            f = B.arena[96:112, AT_F:AT_F + S]
            f2 = B.arena[96:112, AT_FQ:AT_FQ + S]
            act.wait_ge(sem("bf_in"), 16)
            Act(f, ps[96:112, bank, :], ACT.Identity, bias=B.bf[96:112, :]).then_inc(free, 1)
            nc.scalar.drain()
            Act(f2, f, ACT.Abs)
            nc.scalar.drain()
            Act(f2, f2, ACT.Exp, scale=-1.0)
            nc.scalar.drain()
            Act(f2, f2, ACT.Ln, bias=1.0).then_inc(sem("f_log"), 1)
        if name == "q":
            Act(Y[:, 8 + 4 * i:12 + 4 * i, :], banks, ACT.Copy, scale=DH_B ** -0.5).then_inc(free, 1)
        if name == "k":
            Act(at(AT_K, 8, S)[:, 4 * i:4 * i + 4, :], banks, ACT.Copy).then_inc(free, 1)
        if name == "v":
            Act(at(AT_V, NT, 1024)[:, :, i * GC:(i + 1) * GC], banks, ACT.Copy).then_inc(free, 1)
            if i == 1:
                nc.scalar.drain()
                act.wait_ge(sem("value_normed"), 1)
                act.wait_ge(sem("mixing"), HEADS_A)
                attention_scalar(B, act)
        if name in TMP_USERS:
            if tmp_uses(n):
                act.wait_ge(sem("tmp_free"), tmp_uses(n))
            Act(at(TMP, 4, S), banks, ACT.Gelu if name == "ua" else ACT.Silu).then_inc(sem("tmp_full"), 1)
            nc.scalar.drain().then_inc(free, 1)
        if name == "gb" and i == 1:
            act.wait_ge(sem("mixer_out"), 1)
            from_y(1)
        if name == "wo1" and i == 3:
            from_mod(2, SC)
        if name == "cr":
            Act(B.arena[0:32, AT_RC:AT_RC + SC], ps[0:32, bank, 0:SC], ACT.Copy).then_inc(free, 1)
            norm(1)
        if name == "ck":
            Act(at(AT_KC, NTC, 1024)[:, :, i * GC:(i + 1) * GC], ps[:, bank:bank + 2, :], ACT.Copy).then_inc(free, 1)
        if name == "cv":
            Act(at(AT_VC, NTC, 1024)[:, :, i * GC:(i + 1) * GC], ps[:, bank:bank + 2, :], ACT.Copy).then_inc(free, 1)
            if i == 1:
                context_scalar(B, act)
                from_mod(3)
        if name == "r":
            act.wait_ge(sem("gates_cleared"), 2)
            Act(B.arena[0:32, AT_RT:AT_RT + S], ps[0:32, bank, :], ACT.Copy).then_inc(free, 1)
        if name == "ek":
            Act(Y[:, 4 * i:4 * i + 4, :], banks, ACT.Copy).then_inc(free, 1)
        if name == "eq":
            Act(Y[:, 8 + 4 * i:12 + 4 * i, :], banks, ACT.Copy, scale=DK ** -0.5).then_inc(free, 1)
        if name == "ev":
            Act(at(AT_VE, NT, 1024)[:, :, i * GC:(i + 1) * GC], banks, ACT.Copy).then_inc(free, 1)
        if name == "gt":
            Act(at(AT_GATE, KT, S)[:, 4 * i:4 * i + 4, :], banks, ACT.Silu).then_inc(free, 1)
            if i == 3:
                act.wait_ge(sem("pooled"), 4)
                from_y(6)
        if name == "egb" and i == 1:
            act.wait_ge(sem("mixer_out"), 2)
            from_y(4)
        if name == "wo2" and i == 3:
            norm(2)
            from_mod(5)
        if name == "pool" and i == 3:
            act.wait_ge(sem("mixer_out"), 3)
            from_y(7)
    norm(3)
    for t in range(NT):
        for j in range(4):
            k = 4 * t + j
            act.wait_ge(sem("out_turned"), k + 1)
            if t >= 2 and j == 0:
                act.wait_ge(sem(f"out_done_{t % 2}"), 16 * (t // 2))
            Act(at(AT_OUT, 2, D)[:, t % 2, j * GC:(j + 1) * GC], ps[:, k % 4, :], ACT.Copy).then_inc(sem("out_taken"), 1)
        nc.scalar.drain().then_inc(sem("out_rows"), 1)


CONV_AT = [(0, 9), (0, 12), (0, 15), (1, 1), (1, 4), (1, 7), (1, 10), (1, 13)]
MOD_OPERANDS = {0: 0, 2: 16, 3: 32, 5: 48}


def modulated(operand):
    return MOD_OPERANDS[operand]


def attention_scalar(B, act):
    nc, sem, at, ps, Y = B.nc, B.sem, B.at, B.ps, B.Y
    ACT = mybir.ActivationFunctionType
    Act = nc.scalar.activation
    logit, p_t = at(AT_LOGIT, 2, S), at(AT_PT, 2, S)
    act.sem_inc(sem("p_taken"), 2)
    act.sem_inc(sem("o_taken"), 1)
    with act.Fori(0, HEADS_B // 2) as i:
        act.wait_ge(sem("scores"), i * 8 + 1)
        act.sem_inc(sem("scalar_passed"), 1)
        Act(at(AT_QST, 1, S), Y[:, bass.ds(i + 8, 1), :], ACT.Copy).then_inc(sem("staged"), 1)
        Act(at(AT_KST, 1, S), at(AT_K, 8, S)[:, bass.ds(i, 1), :], ACT.Copy).then_inc(sem("staged"), 1)
        for u in range(9):
            if u < 8:
                w = P * (u % 4 + 1)
                act.wait_ge(sem("logits"), i * 8 + u + 1)
                Act(logit[:, u % 2, 0:w], logit[:, u % 2, 0:w], ACT.Exp, bias=B.small[:, 8 + u % 2:9 + u % 2],
                    accum_out=B.small[:, 16 + u:17 + u]).then_inc(sem("probs"), 1)
            if u >= 1:
                w = P * ((u - 1) % 4 + 1)
                act.wait_ge(sem("p_turned"), i * 8 + u + 2)
                act.wait_ge(sem("pv"), i * 8 + u)
                Act(p_t[:, (u - 1) % 2, 0:w], ps[:, 2 + (u - 1) % 2, 0:w], ACT.Copy).then_inc(sem("p_taken"), 1)
        act.wait_ge(sem("o_turned"), i + 2)
        act.sem_inc(sem("scalar_passed"), 1)
        Act(Y[:, bass.ds(i + 8, 1), :], ps[:, 6:7, :], ACT.Copy).then_inc(sem("o_taken"), 1)


def context_scalar(B, act):
    nc, sem, at, ps = B.nc, B.sem, B.at, B.ps
    ACT = mybir.ActivationFunctionType
    Act = nc.scalar.activation
    tc = at(AT_TC, 8, GC)
    act.wait_ge(sem("ctx_logits"), 1)
    Act(tc, ps[:, :, :], ACT.Abs)
    nc.scalar.drain()
    Act(tc, tc, ACT.Exp, scale=-1.0)
    nc.scalar.drain()
    Act(tc, tc, ACT.Ln, bias=1.0).then_inc(sem("ctx_log"), 1)
    act.wait_ge(sem("ctx_sums"), 1)
    act.wait_ge(sem("ctx_gates"), 1)
    Act(tc, ps[:, :, :], ACT.Exp, scale=1.0 / TAU).then_inc(sem("ctx_decays"), 1)
    act.wait_ge(sem("ctx_states"), 1)
    Act(at(AT_STO, 8, GC), ps[:, :, :], ACT.Copy).then_inc(sem("states_out"), 1)


def gla_scalar(B, act):
    nc, sem, at, ps, Y = B.nc, B.sem, B.at, B.ps, B.Y
    ACT = mybir.ActivationFunctionType
    Act = nc.scalar.activation
    M, tmp, G, E = at(AT_M, 2, 2, S), at(TMP, 4, S), at(AT_G, 2, S), at(AT_E, 2, S)
    am = at(AT_AM, NT, S)
    tot = B.small[:, 0:16]
    first = FIRST["beside"]
    kc = GROUPS[first]["kc"]
    nc.scalar.drain()
    act.sem_inc(sem("beside_left"), 4)
    act.sem_inc(sem("beside_stored"), 16)
    act.wait_ge(sem("part_tile"), KT * ordinal(first))
    with act.Fori(0, GLA_HEADS) as i:
        made = 4

        def high_to(tiles):
            nonlocal made
            while made < tiles:
                c = kc + made
                if c % 2 == 0:
                    act.wait_ge(B.w_in[c // 2 % RAW], i * 64 + 16 * (c // (2 * RAW) + 1))
                act.wait_ge(sem("w_used"), i * 32 + (c - RING + 1))
                Act(B.w_hi[:, c % RING, :], B.w_raw[:, c // 2 % RAW, c % 2, :], ACT.Copy).then_inc(sem("hi_done"), 1)
                made += 1

        def leave(k):
            act.wait_ge(sem("w_used"), i * 32 + (kc + KT * (k + 1)))
            act.wait_ge(sem("beside_stored"), i * 32 + 16 * (k + 1))
            out = B.a_raw[:, :, :, :].rearrange("p a b c -> p (a b) c")
            for b in range(4):
                Act(out[:, b, :], ps[:, b, :], ACT.Copy).then_inc(sem("beside_left"), 1)

        act.wait_ge(sem("heads_done"), i + 1)
        act.sem_inc(sem("scalar_passed"), 1)
        Act(at(AT_VH, NT, DK), at(AT_VE, NT, 1024)[:, :, bass.ds(i * DK, DK)], ACT.Copy)
        Act(M[:, 0, :, :], Y[:, bass.ds(i * 2, 2), :], ACT.Copy)
        Act(M[:, 1, :, :], Y[:, bass.ds(i * 2 + 8, 2), :], ACT.Copy).then_inc(sem("head_staged"), 1)
        act.wait_ge(sem("g_logits"), i + 1)
        Act(tmp, ps[:, 4:8, :], ACT.Abs)
        high_to(5)
        nc.scalar.drain()
        Act(tmp, tmp, ACT.Exp, scale=-1.0)
        high_to(6)
        nc.scalar.drain()
        Act(tmp, tmp, ACT.Ln, bias=1.0).then_inc(sem("g_log"), 1)
        high_to(8)
        act.wait_ge(sem("totals"), i + 1)
        Act(B.small[:, 16:32], tot, ACT.Exp, scale=1.0 / TAU).then_inc(sem("block_decays"), 1)
        for n in range(2 * len(LEVELS)):
            h, d = LEVELS[n // 2], n % 2
            act.wait_ge(sem("distances"), i * 14 + n + 1)
            seg = M[:, d, :, :].rearrange("p a (s t) -> p (a s) t", t=2 * h)
            Act(seg[:, :, 0:h], seg[:, :, 0:h], ACT.Exp, scale=-1.0 / TAU)
            Act(seg[:, :, h:2 * h], seg[:, :, h:2 * h], ACT.Exp, scale=1.0 / TAU).then_inc(sem("decays"), 1)
            high_to(level_tiles(n - 3) + RING)
            if n and level_tiles(n - 3) < KT <= level_tiles(n - 2):
                leave(0)
        act.wait_ge(sem("block_distances"), i + 1)
        Act(M[:, 0, :, :], G, ACT.Exp, scale=1.0 / TAU)
        high_to(28)
        Act(M[:, 1, :, :], M[:, 1, :, :], ACT.Exp, scale=-1.0 / TAU)
        high_to(29)
        Act(tmp[:, 0:2, :], tmp[:, 0:2, :], ACT.Exp, scale=-1.0 / TAU)
        Act(tmp[:, 2:4, :], E, ACT.Exp, scale=1.0 / TAU).then_inc(sem("cross_decays"), 1)
        high_to(32)
        act.wait_ge(sem("cross_scores"), i + 1)
        for j in range(NT):
            if j:
                last = Act(am[:, j, 0:P * j], ps[:, 4 + j, 0:P * j], ACT.Copy)
            if j < NT - 1:
                last = Act(am[:, j, P * (j + 1):S], ps[:, 4 + j, P * (j + 1):S], ACT.Copy)
        last.then_inc(sem("cross_taken"), 1)
        high_to(34)
        act.wait_ge(sem("o_mm"), i + 1)
        Act(tmp[:, 0:2, :], ps[:, 4:6, :], ACT.Square).then_inc(sem("o_squared"), 1)
        high_to(35)
        act.wait_ge(sem("o_variance"), i + 1)
        Act(at(AT_R, 1, S), at(AT_R, 1, S), ACT.Sqrt).then_inc(sem("o_deviation"), 1)
        leave(1)
        high_to(36)
    nc.scalar.drain().then_inc(B.bank_free[(FIRST["egb"] - 1) % 2], GLA_HEADS)
    nc.scalar.drain().then_inc(B.bank_free[FIRST["egb"] % 2], GLA_HEADS)


def tensor_program(B, pe):
    nc, sem, at, ps, Y = B.nc, B.sem, B.at, B.ps, B.Y
    f32 = mybir.dt.float32
    mm = nc.tensor.matmul

    def turn(out, src, rows=P):
        return nc.tensor.transpose(out, src, B.ident[0:rows, 0:rows])

    def reduce_parts(parity, out):
        for v in range(2):
            for j in range(4):
                last = mm(out[:, 4 * v + j:4 * v + j + 1], B.acc[:, parity, v, j * P:(j + 1) * P], B.ones[:, 0:1],
                          start=True, stop=True)
        return last

    def tile_products(g, n, slot, t, taken=None, left=None):
        bank = 4 * (n % 2)
        k = g["tile0"] + t
        first, last_t = t == 0, t == g["kt"] - 1
        hi, lo = B.w_hi[:, slot, :], B.w_lo[:, slot, :]
        if g["mode"] == "T":
            w, tok = g["width"], g["tok"]
            for j in range((w + P - 1) // P):
                m = min(P, w - j * P)
                if left:
                    left(j)
                if j == 3 and taken is not None:
                    pe.wait_ge(sem("part_taken"), taken)
                dst = ps[0:m, bank + j, 0:tok]
                cols = slice(j * P, j * P + m)
                mm(dst, hi[:, cols], B.op_hi[:, k, 0:tok], start=first, stop=False)
                mm(dst, hi[:, cols], B.op_lo[:, k, 0:tok], start=False, stop=False)
                last = mm(dst, lo[:, cols], B.op_hi[:, k, 0:tok], start=False, stop=last_t)
        else:
            for j in range(g["tok"] // P):
                if j == 3 and taken is not None:
                    pe.wait_ge(sem("part_taken"), taken)
                dst = ps[:, bank + j, :]
                rows = slice(j * P, j * P + P)
                mm(dst, B.op_hi[:, k, rows], hi, start=first, stop=False)
                mm(dst, B.op_lo[:, k, rows], hi, start=False, stop=False)
                last = mm(dst, B.op_hi[:, k, rows], lo, start=False, stop=last_t)
        return last

    def group(n, r=None):
        g = GROUPS[n]
        c = lambda v, per: v if r is None else r * per + v
        if n >= 2:
            pe.wait_ge(B.bank_free[n % 2], c(n // 2, 1))
        pending = n >= 2 and GROUPS[n - 2]["part"] is not None
        taken = c(ordinal(n - 1), 2) if pending else None
        hook = n >= 1 and GROUPS[n - 1]["part"] is not None
        for t in range(g["kt"]):
            pe.wait_ge(sem("lo_done"), c(g["kc"] + t + 1, 32))
            pe.wait_ge(sem("op_tile"), KT * g["operand"] + g["tile0"] + t + 1)
            tile_products(g, n, (g["kc"] + t) % RING, t, taken if t == 0 else None).then_inc(sem("w_used"), 1)
            if hook and t == 5:
                o = ordinal(n)
                pe.wait_ge(sem("part_tile"), c(KT * o, 2 * KT))
                pe.wait_ge(B.bank_free[(n - 1) % 2], c((n - 1) // 2 + 1, 1))
                reduce_parts((o - 1) % 2, ps[:, 4 * ((n + 1) % 2) + 3, :]).then_inc(sem("part_summed"), 1)

    def norm_sums(m):
        if m >= 2:
            name = ("wo2", "wo3")[m - 2]
            for n in (FIRST[name] + 2, FIRST[name] + 3):
                pe.wait_ge(B.bank_free[n % 2], n // 2 + 1)
            for t in range(KT):
                last = mm(ps[:, 3, :], B.ones, Y[:, t, :], start=t == 0, stop=t == KT - 1)
            last.then_inc(sem("summed"), 1)

    def norm_squares(m):
        sqr = at(AT_SQ, 2, 4, S)
        for j in range(4):
            pe.wait_ge(sem("squared"), 4 * m + j + 1)
            for t in range(4):
                last = mm(ps[:, 7, :], B.ones, sqr[:, j % 2, t, :], start=j + t == 0, stop=j + t == 6)
            last.then_inc(sem("squares_summed"), 1)

    rows = Y[:, 15, :].rearrange("p (r c) -> p r c", c=P)
    pe.wait_ge(sem("rows_in"), 16 * N_ROW_LOADS)
    pe.wait_ge(sem("const_in"), 16)
    for r in range((NVEC + P - 1) // P):
        k = min(P, NVEC - r * P)
        last = turn(ps[:, 0, r * P:r * P + k], rows[0:k, r, :], k)
    last.then_inc(sem("columns"), 1)
    pe.wait_ge(sem("x_in"), 16)
    x_tok = at(AT_X_TOK, NT, D)
    for t in range(KT):
        if t >= 4:
            pe.wait_ge(sem("x_turned"), t - 3)
        for j in range(NT):
            last = turn(ps[:, 1 + t % 4, j * P:(j + 1) * P], x_tok[:, j, t * P:(t + 1) * P])
        last.then_inc(sem("turned"), 1)
    pe.wait_ge(sem("ws_in"), 16)
    for h in range(HEADS_A):
        last = turn(ps[:, 5 + h // 4, h % 4 * P:(h % 4 + 1) * P], at(AT_WS_RAW, HEADS_A, P)[:, h, :])
    last.then_inc(sem("ws_turned"), 1)
    norm_squares(0)
    for p in range(4):
        pe.wait_ge(sem("acc_step"), 34 * (p + 1))
        reduce_parts(p % 2, ps[:, 0, 8 * p:8 * p + 8]).then_inc(sem("start_summed"), 1)

    def run(first, pairs):
        beside = lambda n: [GROUPS[k]["part"] is not None for k in (n - 2, n - 1, n)]
        assert all(beside(first + 2 * k) == beside(first) for k in range(pairs))
        if pairs == 1:
            group(first)
            group(first + 1)
        else:
            with pe.Fori(0, pairs) as r:
                group(first, r)
                group(first + 1, r)

    F = FIRST
    run(F["va"], 1)
    group(F["f"])
    run(F["q"], 2)
    run(F["v"], 1)
    mixer_tensor(B, pe)
    run(F["ua"], 3)
    run(F["wo1"], 1)
    run(F["wo1"] + 2, 1)
    pe.wait_ge(sem("ctx_in"), 16)
    c_tok = at(AT_CTOK, NTC, D)
    for n in range(F["cr"] - 2, F["cr"]):
        pe.wait_ge(B.bank_free[n % 2], n // 2 + 1)
    for t in range(KT):
        if t >= 4:
            pe.wait_ge(sem("modulated"), modulated(2) + t - 3)
        for j in range(NTC):
            last = turn(ps[:, t % 4, j * P:(j + 1) * P], c_tok[:, j, t * P:(t + 1) * P])
        last.then_inc(sem("ctx_turned"), 1)
    pe.wait_ge(sem("modulated"), modulated(2) + KT)
    group(F["cr"])
    norm_squares(1)
    run(F["ck"], 1)
    run(F["cv"], 1)
    context_tensor(B, pe)
    group(F["r"])
    run(F["ek"], 1)
    run(F["eq"], 1)
    run(F["ev"], 1)
    gla_tensor(B, pe, tile_products)
    run(F["egb"], 1)
    run(F["wo2"], 1)
    run(F["wo2"] + 2, 1)
    norm_sums(2)
    norm_squares(2)
    run(F["xp"], 1)
    run(F["xp"] + 2, 1)
    run(F["xp"] + 4, 2)
    for i in range(4):
        group(F["pool"] + i)
    run(F["wo3"], 2)
    norm_sums(3)
    norm_squares(3)
    for t in range(NT):
        for j in range(4):
            k = 4 * t + j
            pe.wait_ge(sem("scaled"), 4 * 3 + j + 1)
            if k >= 4:
                pe.wait_ge(sem("out_taken"), k - 3)
            for q in range(4):
                last = turn(ps[:, k % 4, q * P:(q + 1) * P], Y[:, 4 * j + q, t * P:(t + 1) * P])
            last.then_inc(sem("out_turned"), 1)


def mixer_tensor(B, pe):
    nc, sem, at, ps, Y = B.nc, B.sem, B.at, B.ps, B.Y
    mm = nc.tensor.matmul
    for n in (FIRST["v"], FIRST["v"] + 1):
        pe.wait_ge(B.bank_free[n % 2], n // 2 + 1)
    pe.wait_ge(sem("part_taken"), ordinal(FIRST["v"] + 1))
    pe.wait_ge(sem("value_normed"), 1)
    pe.wait_ge(sem("ws_masked"), 1)
    for h in range(HEADS_A):
        for b in range(NT):
            last = mm(ps[:, h, b * P:(b + 1) * P], at(AT_VA, NT, 1024)[:, b, h * P:(h + 1) * P],
                      at(AT_WST, HEADS_A, P)[:, h, :], start=True, stop=True)
        last.then_inc(sem("mixing"), 1)
    pe.wait_ge(sem("mixed"), HEADS_A)
    pe.sem_inc(sem("scores"), 1)
    pe.sem_inc(sem("pv"), 2)
    pe.sem_inc(sem("p_turned"), 2)
    pe.sem_inc(sem("o_turned"), 1)
    q, k, v = at(AT_QST, S), at(AT_KST, S), at(AT_V, NT, 1024)
    logit, p_t, o_tok = at(AT_LOGIT, 2, S), at(AT_PT, 2, S), at(AT_OTOK, NT, P)
    with pe.Fori(0, HEADS_B // 2) as i:
        pe.wait_ge(sem("staged"), i * 2 + 2)
        for s in range(10):
            if s < 8:
                half, b = s // 4, s % 4
                rows = slice(DH_B * half, DH_B * (half + 1))
                pe.wait_ge(sem("score_slots"), i * 8 + s + 1)
                last = mm(ps[:, s % 2, 0:P * (b + 1)], q[rows, b * P:(b + 1) * P], k[rows, 0:P * (b + 1)],
                          start=True, stop=True)
                last.then_inc(sem("scores"), 1)
            if 1 <= s < 9:
                u = s - 1
                pe.wait_ge(sem("probs"), i * 8 + u + 1)
                pe.wait_ge(sem("p_taken"), i * 8 + u + 1)
                for c in range(u % 4 + 1):
                    last = nc.tensor.transpose(ps[:, 2 + u % 2, c * P:(c + 1) * P], logit[:, u % 2, c * P:(c + 1) * P],
                                               B.ident)
                last.then_inc(sem("p_turned"), 1)
            if s >= 2:
                u = s - 2
                pe.wait_ge(sem("p_taken"), i * 8 + u + 3)
                pe.wait_ge(sem("o_scaled"), i * 8 + u + 1)
                for c in range(u % 4 + 1):
                    last = mm(ps[:, 4 + u % 2, 0:DH_B], p_t[:, u % 2, c * P:(c + 1) * P],
                              v[:, c, bass.ds(i * P + DH_B * (u // 4), DH_B)], start=c == 0, stop=c == u % 4)
                last.then_inc(sem("pv"), 1)
        pe.wait_ge(sem("o_scaled"), i * 8 + 10)
        pe.wait_ge(sem("o_taken"), i + 1)
        for b in range(NT):
            last = nc.tensor.transpose(ps[:, 6, b * P:(b + 1) * P], o_tok[:, b, :], B.ident)
        last.then_inc(sem("o_turned"), 1)
    pe.wait_ge(sem("o_taken"), HEADS_B // 2 + 1)


def context_tensor(B, pe):
    nc, sem, at, ps = B.nc, B.sem, B.at, B.ps
    mm = nc.tensor.matmul
    for n in (FIRST["cv"], FIRST["cv"] + 1):
        pe.wait_ge(B.bank_free[n % 2], n // 2 + 1)
    pe.wait_ge(sem("ctx_gates_in"), 64)
    pe.wait_ge(sem("normed"), 8)
    r_c, wg = at(AT_RC, SC), at(AT_WGC, 2, 1024)
    for d in range(2):
        for t in range(NTC):
            for c in range(2):
                last = mm(ps[:, 4 * d + 2 * t + c, :], r_c[0:33, t * P:(t + 1) * P], wg[0:33, d, c * GC:(c + 1) * GC],
                          start=True, stop=True)
    last.then_inc(sem("ctx_logits"), 1)
    pe.wait_ge(sem("ctx_gates"), 1)
    la = at(AT_LAC, 8, GC)
    for d in range(2):
        for t in range(NTC):
            for c in range(2):
                bank = 4 * d + 2 * t + c
                tri = (B.tri_gt, B.tri_lt)[d]
                other = t == d
                mm(ps[:, bank, :], tri, la[:, bank, :], start=True, stop=not other)
                last = mm(ps[:, bank, :], B.ones, la[:, 4 * d + 2 * (1 - t) + c, :], start=False, stop=True) if other else last
    nc.tensor.drain().then_inc(sem("ctx_sums"), 1)
    pe.wait_ge(sem("ctx_keys"), 1)
    keys, vc = at(AT_TC, 2, 2, 1024), at(AT_VC, NTC, 1024)
    for h in range(GLA_HEADS):
        for d in range(2):
            for a in range(2):
                for t in range(NTC):
                    last = mm(ps[:, 2 * h + d, a * DK:(a + 1) * DK], keys[:, d, t, h * DK + a * P:h * DK + (a + 1) * P],
                              vc[:, t, h * DK:(h + 1) * DK], start=t == 0, stop=t == 1)
    last.then_inc(sem("ctx_states"), 1)
    pe.wait_ge(sem("states_out"), 1)


def gla_tensor(B, pe, tile_products):
    nc, sem, at, ps = B.nc, B.sem, B.at, B.ps
    mm = nc.tensor.matmul
    M, tmp, G, E = at(AT_M, 2, 2, S), at(TMP, 4, S), at(AT_G, 2, S), at(AT_E, 2, S)
    am, vh, st = at(AT_AM, NT, S), at(AT_VH, NT, DK), at(AT_ST, 4, DK)
    wg, r_t, qb = at(AT_WG, 2, DK), at(AT_RT, S), at(AT_QB, 2, S)
    primed = at(AT_G, 4, 2, P)
    for n in (FIRST["ev"], FIRST["ev"] + 1):
        pe.wait_ge(B.bank_free[n % 2], n // 2 + 1)
    pe.wait_ge(sem("part_taken"), ordinal(FIRST["ev"] + 1))
    kc = GROUPS[FIRST["beside"]]["kc"]
    with pe.Fori(0, GLA_HEADS) as i:
        used = 0

        def tiles(count):
            nonlocal used
            for _ in range(count):
                k, t = divmod(used, KT)
                g = GROUPS[FIRST["beside"] + k]
                pe.wait_ge(sem("lo_done"), i * 32 + (kc + used + 1))

                def left(bank):
                    pe.wait_ge(sem("beside_left"), i * 8 + (4 * k + bank + 1))
                tile_products(g, 0, (kc + used) % RING, t, left=left if t == 0 else None).then_inc(sem("w_used"), 1)
                used += 1

        tiles(T_ENTER)
        pe.wait_ge(sem("head_in"), i * 80 + 80)
        pe.wait_ge(sem("heads_done"), i + 1)
        for d in range(2):
            for a in range(2):
                last = mm(ps[:, 4 + 2 * d + a, :], wg[0:33, d, a * P:(a + 1) * P], r_t[0:33, :], start=True, stop=True)
        last.then_inc(sem("g_logits"), 1)
        tiles(T_LOGIT)
        pe.wait_ge(sem("totals"), i + 1)
        pe.wait_ge(sem("head_staged"), i + 1)
        for b in range(NT):
            for a in range(2):
                last = mm(ps[:, 4, b * P:(b + 1) * P], M[:, 0, a, b * P:(b + 1) * P], M[:, 1, a, b * P:(b + 1) * P],
                          start=a == 0, stop=a == 1)
        last.then_inc(sem("diagonal"), 1)
        tiles(T_DIAGONAL)
        for n in range(2 * len(LEVELS)):
            d = n % 2
            pe.wait_ge(sem("weighted"), i * 14 + n + 1)
            if n >= 3:
                pe.wait_ge(sem("level_taken"), i * 14 + n - 2)
            for b in range(NT):
                for a in range(2):
                    x = M[:, d, a, b * P:(b + 1) * P]
                    last = mm(ps[:, 5 + n % 3, b * P:(b + 1) * P], x, x, start=a == 0, stop=a == 1)
            last.then_inc(sem("level_scores"), 1)
            tiles(T_LEVEL[n])
        tiles(T_CROSS)
        pe.wait_ge(sem("cross_weighted"), i + 1)
        qf, kf, qbk, kb = M[:, 0, :, :], M[:, 1, :, :], tmp[:, 0:2, :], tmp[:, 2:4, :]
        for j in range(NT):
            for b in range(NT):
                if j == b:
                    continue
                for a in range(2):
                    blk = lambda x, y: x[:, a, y * P:(y + 1) * P]
                    if j < b:
                        far_k, far_q = j == 0 and b >= 2, b == 3 and j <= 1
                        key = primed[:, 0, a, :] if far_k else blk(kf, j)
                        query = primed[:, 1, a, :] if far_q else blk(qf, b)
                    else:
                        far_q, far_k = b == 0 and j >= 2, j == 3 and b <= 1
                        query = primed[:, 2, a, :] if far_q else blk(qbk, b)
                        key = primed[:, 3, a, :] if far_k else blk(kb, j)
                    last = mm(ps[:, 4 + j, b * P:(b + 1) * P], key, query, start=a == 0, stop=a == 1)
        last.then_inc(sem("cross_scores"), 1)
        tiles(T_TAKEN)
        pe.wait_ge(sem("cross_taken"), i + 1)
        pe.wait_ge(sem("state_queries"), i + 1)
        for a in range(2):
            cols = slice(a * P, (a + 1) * P)
            for j in range(NT):
                mm(ps[:, 4 + a, :], vh[:, j, cols], am[:, j, :], start=j == 0, stop=False)
            for d in range(2):
                for e in range(2):
                    last = mm(ps[:, 4 + a, :], st[:, 2 * d + e, cols], (E if d == 0 else qb)[:, e, :],
                              start=False, stop=d + e == 2)
        last.then_inc(sem("o_mm"), 1)
        tiles(T_OUT)
        pe.wait_ge(sem("o_squared"), i + 1)
        for a in range(2):
            last = mm(ps[:, 6, :], B.ones, tmp[:, a, :], start=a == 0, stop=a == 1)
        last.then_inc(sem("o_summed"), 1)
    pe.wait_ge(sem("heads_done"), GLA_HEADS + 1)


def vector_program(B, dve):
    nc, sem, at, ps, Y = B.nc, B.sem, B.at, B.ps, B.Y
    ALU, AX = mybir.AluOpType, mybir.AxisListType
    f32 = mybir.dt.float32
    V = nc.vector

    def low_tile(c, width):
        dve.wait_ge(sem("hi_done"), c + 1)
        if c >= RING:
            dve.wait_ge(sem("w_used"), c - RING + 1)
        V.tensor_tensor(B.w_lo[:, c % RING, 0:width], B.w_raw[:, c // 2 % RAW, c % 2, 0:width],
                        B.w_hi[:, c % RING, 0:width].bitcast(f32), ALU.subtract).then_inc(sem("lo_done"), 1)

    def part_tile(n, t, r=0):
        part, o = GROUPS[n]["part"], ordinal(n)
        vectors = [(VEC["c"] if part < 12 else VEC["c2"])] + ([VEC["cc"]] if ctx_part(part) else [])
        dve.wait_ge(B.a_in[t // 2 % 2], r * 32 + 16 * (4 * o + t // 4 + 1))
        if o or t or not isinstance(r, int):
            dve.wait_ge(sem("part_tile"), r * 8 + KT * o + t)
        for v, first in enumerate(vectors):
            col = B.vec[:, first + t:first + t + 1] if isinstance(r, int) else B.vec[:, bass.ds(r * 8 + (first + t), 1)]
            sums = B.acc[:, o % 2, v, :]
            last = V.scalar_tensor_tensor(out=sums, in0=B.a_raw[:, t // 2 % 2, t % 2, :], scalar=col, in1=sums,
                                          op0=ALU.mult, op1=ALU.add)
        last.then_inc(sem("part_tile"), 1)

    def ahead(n):
        g = GROUPS[n]
        c, k, width, part = g["kc"], g["kt"], g["width"], g["part"]
        after = GROUPS[n + 1]["width"] if n + 1 < len(GROUPS) else 0
        if part is not None:
            V.memset(B.acc[:, ordinal(n) % 2, :, :], 0.0)
            V.drain()
        if k == KT and after == width and n > 0:
            with dve.Fori(0, 2) as r:
                for t in range(8):
                    x = c + 4 + t
                    dve.wait_ge(sem("hi_done"), r * 8 + (x + 1))
                    dve.wait_ge(sem("w_used"), r * 8 + (x - RING + 1))
                    V.tensor_tensor(B.w_lo[:, x % RING, 0:width], B.w_raw[:, x // 2 % RAW, x % 2, 0:width],
                                    B.w_hi[:, x % RING, 0:width].bitcast(f32), ALU.subtract).then_inc(sem("lo_done"), 1)
                    if part is not None:
                        part_tile(n, t, r)
        else:
            for t in range(max(k, 4)):
                if t < k - 4:
                    low_tile(c + 4 + t, width)
                elif after:
                    low_tile(c + 4 + t, after)
                if part is not None:
                    part_tile(n, t)
        if n and GROUPS[n - 1]["part"] is not None:
            take_part(GROUPS[n - 1]["part"], ps[:, 4 * ((n + 1) % 2) + 3, :], ordinal(n))

    def conv_ahead(n):
        for t in range(KT):
            low_tile(GROUPS[n]["kc"] + 4 + t, GC)
            for j in range(8):
                if CONV_AT[j] == (GROUPS[n]["i"], t):
                    conv_tile(j)

    def conv_tile(j):
        dve.wait_ge(sem(f"conv_in_{j}"), 16)
        dve.wait_ge(sem("conv_gate"), j + 1)
        x = at(AT_CONV, CONV_SLOTS, 4, S)[:, j % CONV_SLOTS, :, :]
        u, v = (x[:, k, :].rearrange("p (r w) -> p r w", w=GRID_W) for k in (1, 2))
        tap = [B.vec[:, VEC["conv"] + 8 * k + j:VEC["conv"] + 8 * k + j + 1] for k in range(3)]
        V.tensor_tensor(x[:, 1, :], x[:, 1, :], x[:, 2, :], ALU.mult)
        V.tensor_tensor(x[:, 0, :], x[:, 0, :], x[:, 3, :], ALU.mult)
        V.drain()
        V.tensor_scalar(v, u, tap[1], None, ALU.mult)
        V.drain()
        V.scalar_tensor_tensor(out=v[:, :, 1:], in0=u[:, :, :-1], scalar=tap[0], in1=v[:, :, 1:],
                               op0=ALU.mult, op1=ALU.add)
        V.drain()
        V.scalar_tensor_tensor(out=v[:, :, :-1], in0=u[:, :, 1:], scalar=tap[2], in1=v[:, :, :-1],
                               op0=ALU.mult, op1=ALU.add)
        V.drain()
        V.tensor_tensor(Y[:, 8 + j, :], x[:, 2, :], x[:, 0, :], ALU.mult).then_inc(sem("conv_done"), 1)

    def take_part(part, bank, count):
        dve.wait_ge(sem("part_summed"), count)
        put_part(part, bank[:, 0:4], 4 * part)
        if ctx_part(part):
            put_part(part, bank[:, 4:8], 144 + 4 * (part - 12))
        V.drain().then_inc(sem("part_taken"), 1)

    def put_part(part, sums, col):
        bias = B.vec[:, VEC["b_ada"] + 4 * part:VEC["b_ada"] + 4 * part + 4]
        V.tensor_tensor(B.mod[:, col:col + 4], sums, bias, ALU.add)
        if part % 12 // 4 == 1:
            V.drain()
            V.tensor_scalar(B.mod[:, col:col + 4], B.mod[:, col:col + 4], 1.0, None, ALU.add)

    def split_lo(t, src, tok=S, signal=True):
        V.tensor_tensor(B.op_lo[:, t, 0:tok], src, B.op_hi[:, t, 0:tok].bitcast(f32), ALU.subtract)\
            .then_inc(sem("op_tile"), 1)

    def last_use(operand):
        return max(x["kc"] + x["kt"] for x in GROUPS if x["operand"] == operand)

    def modulate(operand, shift, scale, src, tok=S, ready=None):
        if operand:
            dve.wait_ge(sem("w_used"), last_use(operand - 1))
        buf = at(TMP, 4, S)
        base = modulated(operand)
        V.drain()
        for t in range(KT + 2):
            if t < KT:
                if t >= 4:
                    dve.wait_ge(sem("op_tile"), KT * operand + t - 3)
                if ready:
                    ready(t)
                V.tensor_scalar(buf[:, t % 4, 0:tok], src(t), B.mod[:, scale + t:scale + t + 1],
                                B.mod[:, shift + t:shift + t + 1], ALU.mult, ALU.add).then_inc(sem("modulated"), 1)
            if t >= 2:
                u = t - 2
                dve.wait_ge(sem("op_high"), KT * operand + u + 1)
                dve.wait_ge(sem("modulated"), base + u + 1)
                split_lo(u, buf[:, u % 4, 0:tok], tok)

    def split_y(operand):
        V.drain().then_inc(sem("mixer_out" if operand != 6 else "pooled_all"), 1)
        dve.wait_ge(sem("w_used"), last_use(operand - 1))
        for t in range(KT):
            dve.wait_ge(sem("op_high"), KT * operand + t + 1)
            split_lo(t, Y[:, t, :])

    def norm(m):
        eps = EPS if m < 2 else LN_EPS
        if m >= 2:
            dve.wait_ge(sem("summed"), m - 1)
            for j in range(4):
                y = Y[:, 4 * j:4 * j + 4, :]
                V.scalar_tensor_tensor(out=y, in0=ps[:, 3:4, :].to_broadcast([P, 4, S]), scalar=-1.0 / D, in1=y,
                                       op0=ALU.mult, op1=ALU.add).then_inc(sem("centred"), 1)
        dve.wait_ge(sem("squares_summed"), 4 * m + 4)
        r = at(AT_RSTD, 1, S)
        V.tensor_scalar(r[:, 0, :], ps[:, 7, :], 1.0 / D, eps, ALU.mult, ALU.add).then_inc(sem("variance"), 1)
        dve.wait_ge(sem("deviation"), m + 1)
        V.reciprocal(r[:, 0, :], r[:, 0, :])
        V.drain()
        if m == 0:
            dve.wait_ge(sem("spilled"), 16)
        for j in range(4):
            y = Y[:, 4 * j:4 * j + 4, :]
            V.tensor_tensor(y, y, r.to_broadcast([P, 4, S]), ALU.mult).then_inc(sem("normed"), 1)

    V.memset(B.small[:, :], 0.0)
    ring = at(AT_START, 8, 1024)
    for pair in range(4):
        base = 34 * pair
        if pair >= 2:
            dve.wait_ge(sem("start_summed"), pair - 1)
        for v in range(2):
            V.memset(B.acc[:, pair % 2, v, :], 0.0).then_inc(sem("acc_step"), 1)
        if pair == 0:
            dve.wait_ge(sem("vec_ready"), 1)
        with dve.Fori(0, 2) as r:
            for s in range(8):
                dve.wait_ge(B.start_in[s], r * 16 + 16 * (2 * pair + 1))
                for v in range(2):
                    dve.wait_ge(sem("acc_step"), r * 16 + (base + 2 * s + v + 1))
                    sums = B.acc[:, pair % 2, v, :]
                    V.scalar_tensor_tensor(out=sums, in0=ring[:, s, v * GC:(v + 1) * GC],
                                           scalar=B.vec[:, bass.ds(r * 8 + (VEC["c"] + s), 1)], in1=sums,
                                           op0=ALU.mult, op1=ALU.add).then_inc(sem("acc_step"), 1)
    dve.wait_ge(sem("masks_in"), 16)
    V.tensor_copy(B.masks[:, :, :].rearrange("p l c -> p (l c)"),
                  B.a_raw[:, :, :, :].rearrange("p a b c -> p (a b c)")[:, 0:2 * len(LEVELS) * P])\
        .then_inc(sem("masks_made"), 1)
    dve.wait_ge(sem("start_summed"), 4)
    V.tensor_tensor(B.mod[:, 0:32], ps[:, 0, 0:32], B.vec[:, VEC["b_ada"]:VEC["b_ada"] + 32], ALU.add)
    V.drain()
    V.tensor_scalar(B.mod[:, 16:32], B.mod[:, 16:32], 1.0, None, ALU.add)
    dve.wait_ge(sem("ws_turned"), 1)
    V.tensor_tensor(at(AT_WST, HEADS_A, P), ps[:, 5:7, :].rearrange("p b (h t) -> p (b h) t", t=P),
                    B.tri_le.unsqueeze(1).to_broadcast([P, HEADS_A, P]), ALU.mult).then_inc(sem("ws_masked"), 1)
    norm(0)

    def scaled(m):
        def ready(t):
            if t % 4 == 0:
                dve.wait_ge(sem("scaled"), 4 * m + t // 4 + 1)
        return ready

    y_tile = lambda t: Y[:, t, :]
    modulate(0, 0, 16, y_tile, ready=scaled(0))
    for c in range(4):
        low_tile(c, GC)

    for n, g in enumerate(GROUPS):
        name, i = g["name"], g["i"]
        if name == "beside":
            if i == 0:
                gla_vector(B, dve)
            continue
        if name == "egb":
            conv_ahead(n)
        else:
            ahead(n)
        bank = 4 * (n % 2)
        free = B.bank_free[n % 2]
        banks = ps[:, bank:bank + 4, :]
        if name in DVE_EVAC:
            dve.wait_ge(sem("w_used"), g["kc"] + g["kt"])
            V.drain()
        if name == "va" and i == 1:
            for k in range(2):
                dve.wait_ge(B.bank_free[(n - 1 + k) % 2], (n - 1 + k) // 2 + 1)
            va = at(AT_VA, NT, 1024)
            stats = B.small[:, 16:16 + 48].rearrange("p (a s) -> p a s", s=12)
            for b in range(NT):
                for h in range(2):
                    V.bn_stats(stats[:, b, 6 * h:6 * h + 6], va[:, b, h * GC:(h + 1) * GC])
            V.drain()
            for b in range(NT):
                V.bn_aggr(B.small[:, 64 + 2 * b:66 + 2 * b], stats[:, b, :])
            V.drain()
            mv = B.small[:, 64:72].rearrange("p (a b) -> p a b", b=2)
            V.tensor_scalar(B.small[:, 0:4], mv[:, :, 1], EPS, None, ALU.add).then_inc(sem("value_variance"), 1)
            dve.wait_ge(sem("value_deviation"), 1)
            V.reciprocal(B.small[:, 4:8], B.small[:, 0:4])
            V.drain()
            dve.wait_ge(sem("ln_rows_in"), 32)
            rows = at(TMP, 2, 1024)
            for b in range(NT):
                V.tensor_scalar(va[:, b, :], va[:, b, :], B.small[:, 64 + 2 * b:65 + 2 * b], B.small[:, 4 + b:5 + b],
                                ALU.subtract, ALU.mult)
            V.drain()
            V.tensor_tensor(va, va, rows[:, 0:1, :].to_broadcast([P, NT, 1024]), ALU.mult)
            V.drain()
            V.tensor_tensor(va, va, rows[:, 1:2, :].to_broadcast([P, NT, 1024]), ALU.add)\
                .then_inc(sem("value_normed"), 1)
        if name == "f":
            dve.wait_ge(sem("f_log"), 1)
            f = B.arena[96:112, AT_F:AT_F + S]
            V.scalar_tensor_tensor(out=f, in0=f, scalar=0.0, in1=B.arena[96:112, AT_FQ:AT_FQ + S],
                                   op0=ALU.min, op1=ALU.subtract)
            V.drain()
            V.tensor_tensor_scan(B.arena[96:112, AT_FQ:AT_FQ + S], f, f, 0.0, ALU.add, ALU.min)
            V.drain()
            V.tensor_scalar(f, B.arena[96:112, AT_FQ:AT_FQ + S], -1.0, None, ALU.mult).then_inc(sem("f_summed"), 1)
        if name == "v" and i == 1:
            dve.wait_ge(sem("bs_in"), 16)
            for h in range(HEADS_A):
                dve.wait_ge(sem("mixing"), h + 1)
                V.tensor_tensor(Y[:, h, :].rearrange("p (b t) -> p b t", t=P),
                                ps[:, h, :].rearrange("p (b t) -> p b t", t=P),
                                at(AT_BS, HEADS_A, P)[:, h:h + 1, :].to_broadcast([P, NT, P]), ALU.add)\
                    .then_inc(sem("mixed"), 1)
            attention_vector(B, dve)
        if name in TMP_USERS:
            dve.wait_ge(sem("tmp_full"), tmp_uses(n) + 1)
            if name == "gb" and i == 0:
                dve.wait_ge(sem("o_taken"), HEADS_B // 2 + 1)
            t = 4 * i + (8 if name == "gb" else 0)
            V.drain()
            V.tensor_tensor(Y[:, t:t + 4, :], Y[:, t:t + 4, :], at(TMP, 4, S), ALU.mult).then_inc(sem("tmp_free"), 1)
            if name == "gb" and i == 1:
                split_y(1)
            if name == "egb" and i == 1:
                split_y(4)
        if name in ("wo1", "wo2", "wo3"):
            k = ("wo1", "wo2", "wo3").index(name)
            dve.wait_ge(sem("residual_in"), 16 * (4 * k + i + 1))
            gate = 48 * k + 32
            x = at(AT_XRES, 4, S)
            if k:
                V.tensor_scalar(x, x, ALPHA, None, ALU.mult)
                V.drain()
            for t in range(4):
                f = 4 * i + t
                last = V.scalar_tensor_tensor(out=Y[:, f, :], in0=ps[:, bank + t, :],
                                              scalar=B.mod[:, gate + f:gate + f + 1], in1=x[:, t, :],
                                              op0=ALU.mult, op1=ALU.add)
            last.then_inc(free, 1)
            if name == "wo1" and i == 3:
                def turned(t):
                    dve.wait_ge(sem("ctx_turned"), t + 1)
                modulate(2, 144, 160, lambda t: ps[:, t % 4, 0:SC], SC, ready=turned)
            if name == "wo2" and i == 3:
                norm(2)
                modulate(5, 96, 112, y_tile, ready=scaled(2))
            if name == "wo3" and i == 3:
                norm(3)
        if name == "cr":
            norm(1)
        if name == "cv" and i == 1:
            context_vector(B, dve)
            modulate(3, 48, 64, y_tile, ready=scaled(1))
        if name == "xp":
            pool_vector(B, dve, i, banks, free)
        if name == "gt" and i == 3:
            split_y(6)
        if name == "pool":
            if i == 0:
                m = FIRST["gt"] + 3
                for k in (m - 1, m):
                    dve.wait_ge(B.bank_free[k % 2], k // 2 + 1)
            for t in range(4):
                f = 4 * i + t
                last = V.scalar_tensor_tensor(out=Y[:, f, :], in0=ps[:, bank + t, :],
                                              scalar=B.vec[:, VEC["pool_s"] + f:VEC["pool_s"] + f + 1],
                                              in1=at(AT_GATE, KT, S)[:, f, :], op0=ALU.mult, op1=ALU.mult)
            last.then_inc(free, 1)
            if i == 3:
                split_y(7)


def attention_vector(B, dve):
    nc, sem, at, ps = B.nc, B.sem, B.at, B.ps
    ALU, AX = mybir.AluOpType, mybir.AxisListType
    V = nc.vector
    logit, neg_f, f_col, o_tok = at(AT_LOGIT, 2, S), at(AT_NEGF, 2, S), at(AT_FQ, NT, HEADS_B), at(AT_OTOK, NT, P)
    dve.wait_ge(sem("f_cols_in"), 64)
    dve.sem_inc(sem("score_slots"), 2)
    dve.sem_inc(sem("o_scaled"), 2)
    with dve.Fori(0, HEADS_B // 2) as i:
        for u in range(10):
            if u < 8:
                h, b = u // 4, u % 4
                w = P * (b + 1)
                if b == 0:
                    dve.wait_ge(B.sem(f"f_row_in_{h}"), i * 16 + 16)
                dve.wait_ge(sem("scores"), i * 8 + u + 2)
                dve.wait_ge(sem("p_turned"), i * 8 + u + 1)
                L = logit[:, u % 2, 0:w]
                V.scalar_tensor_tensor(out=L, in0=neg_f[:, h, 0:w], scalar=f_col[:, b, bass.ds(i * 2 + h, 1)],
                                       in1=ps[:, u % 2, 0:w], op0=ALU.subtract, op1=ALU.add)\
                    .then_inc(sem("score_slots"), 1)
                V.drain()
                diag = logit[:, u % 2, w - P:w]
                V.tensor_tensor(diag, diag, B.causal, ALU.add)
                V.drain()
                V.tensor_reduce(B.small[:, 8 + u % 2:9 + u % 2], L, AX.X, ALU.max, negate=True)\
                    .then_inc(sem("logits"), 1)
            if u >= 2:
                k = u - 2
                dve.wait_ge(sem("probs"), i * 8 + k + 1)
                V.reciprocal(B.small[:, 24 + k:25 + k], B.small[:, 16 + k:17 + k])
                V.drain()
                dve.wait_ge(sem("pv"), i * 8 + k + 3)
                if k == 0:
                    dve.wait_ge(sem("o_turned"), i + 1)
                V.tensor_scalar(o_tok[:, k % 4, DH_B * (k // 4):DH_B * (k // 4 + 1)], ps[:, 4 + k % 2, 0:DH_B],
                                B.small[:, 24 + k:25 + k], None, ALU.mult).then_inc(sem("o_scaled"), 1)


def context_vector(B, dve):
    nc, sem, at, ps = B.nc, B.sem, B.at, B.ps
    ALU = mybir.AluOpType
    V = nc.vector
    dve.wait_ge(sem("ctx_log"), 1)
    tc, la, kc = at(AT_TC, 8, GC), at(AT_LAC, 8, GC), at(AT_KC, NTC, 1024)
    for b in range(0, 8, 4):
        V.scalar_tensor_tensor(out=la[:, b:b + 4, :], in0=ps[:, b:b + 4, :], scalar=0.0, in1=tc[:, b:b + 4, :],
                               op0=ALU.min, op1=ALU.subtract)
    V.drain().then_inc(sem("ctx_gates"), 1)
    dve.wait_ge(sem("ctx_decays"), 1)
    for n in (FIRST["ck"], FIRST["ck"] + 1):
        dve.wait_ge(B.bank_free[n % 2], n // 2 + 1)
    kv = at(AT_TC, 2, 2 * 1024)
    for d in range(2):
        V.tensor_tensor(kv[:, d, :], kv[:, d, :], kc.rearrange("p a b -> p (a b)"), ALU.mult)
    V.drain().then_inc(sem("ctx_keys"), 1)


def gla_vector(B, dve):
    nc, sem, at, ps, Y = B.nc, B.sem, B.at, B.ps, B.Y
    ALU = mybir.AluOpType
    V = nc.vector
    M, tmp, G, E = at(AT_M, 2, 2, S), at(TMP, 4, S), at(AT_G, 2, S), at(AT_E, 2, S)
    am = at(AT_AM, NT * NT, P)
    am_diag = am[:, 0:NT * NT:NT + 1, :]
    tot = B.small[:, 0:16]
    dec = B.small[:, 16:32].rearrange("p (d a b) -> p d a b", d=2, a=2)
    cum = B.small[:, 32:48].rearrange("p (d a b) -> p d a b", d=2, a=2)
    t8 = lambda x: x.rearrange("p a (b t) -> p (a b) t", t=P)
    kc = GROUPS[FIRST["beside"]]["kc"]
    dve.sem_inc(sem("heads_done"), 1)
    with dve.Fori(0, GLA_HEADS) as i:
        made = 4

        def low_to(tiles):
            nonlocal made
            while made < tiles:
                c = kc + made
                dve.wait_ge(sem("hi_done"), i * 32 + (c + 1))
                dve.wait_ge(sem("w_used"), i * 32 + (c - RING + 1))
                V.tensor_tensor(B.w_lo[:, c % RING, :], B.w_raw[:, c // 2 % RAW, c % 2, :],
                                B.w_hi[:, c % RING, :].bitcast(mybir.dt.float32), ALU.subtract)\
                    .then_inc(sem("lo_done"), 1)
                made += 1

        low_to(5)
        kh, qh = Y[:, bass.ds(i * 2, 2), :], Y[:, bass.ds(i * 2 + 8, 2), :]
        dve.wait_ge(sem("g_log"), i + 1)
        V.scalar_tensor_tensor(out=tmp, in0=ps[:, 4:8, :], scalar=0.0, in1=tmp, op0=ALU.min, op1=ALU.subtract)
        low_to(6)
        V.drain()
        for a in range(2):
            V.tensor_tensor_scan(G[:, a, :], B.restart, tmp[:, a, :], 0.0, ALU.mult, ALU.add)
            V.tensor_tensor_scan(E[:, a, :], B.restart, tmp[:, 2 + a, :], 0.0, ALU.mult, ALU.add)
        V.drain()
        V.tensor_copy(tot[:, 0:8].unsqueeze(2), t8(G)[:, :, P - 1:P])
        V.tensor_copy(tot[:, 8:16].unsqueeze(2), t8(E)[:, :, P - 1:P]).then_inc(sem("totals"), 1)
        V.drain()
        low_to(8)
        V.tensor_tensor(E, E, tmp[:, 2:4, :], ALU.subtract)
        dve.wait_ge(sem("diagonal"), i + 1)
        V.tensor_tensor(am_diag, ps[:, 4, :].rearrange("p (b t) -> p b t", t=P),
                        B.eye2.unsqueeze(1).to_broadcast([P, NT, P]), ALU.mult)
        V.drain()

        def distance(n):
            h, d = LEVELS[n // 2], n % 2
            x = (G, E)[d].rearrange("p a (s t) -> p (a s) t", t=2 * h)
            m = M[:, d, :, :].rearrange("p a (s t) -> p (a s) t", t=2 * h)
            if n >= 2:
                dve.wait_ge(sem("level_scores"), i * 14 + n - 1)
            V.tensor_tensor(m, x, x[:, :, h:h + 1].to_broadcast([P, 2 * S // (2 * h), 2 * h]), ALU.subtract)\
                .then_inc(sem("distances"), 1)

        def take(n):
            h, d = LEVELS[n // 2], n % 2
            dve.wait_ge(sem("level_scores"), i * 14 + n + 1)
            if n:
                dve.wait_ge(sem("level_taken"), i * 14 + n)
            dve.sem_inc(sem("vector_passed"), 1)
            V.copy_predicated(am_diag, B.masks[:, n:n + 1, :].to_broadcast([P, NT, P]),
                              ps[:, 5 + n % 3, :].rearrange("p (b t) -> p b t", t=P)).then_inc(sem("level_taken"), 1)

        distance(0)
        distance(1)
        for n in range(2 * len(LEVELS)):
            h, d = LEVELS[n // 2], n % 2
            dve.wait_ge(sem("decays"), i * 14 + n + 1)
            m, k, q = (x.rearrange("p a (s t) -> p (a s) t", t=2 * h) for x in (M[:, d, :, :], kh, qh))
            low, high = (k, q) if d == 0 else (q, k)
            V.tensor_tensor(m[:, :, 0:h], m[:, :, 0:h], low[:, :, 0:h], ALU.mult)
            V.tensor_tensor(m[:, :, h:2 * h], m[:, :, h:2 * h], high[:, :, h:2 * h], ALU.mult)\
                .then_inc(sem("weighted"), 1)
            if n >= 1:
                take(n - 1)
                if n + 1 < 2 * len(LEVELS):
                    distance(n + 1)
            low_to(level_tiles(n - 3) + RING)
        take(2 * len(LEVELS) - 1)
        V.drain()
        ends = lambda d: tot[:, 8 * d:8 * d + 8].unsqueeze(2).to_broadcast([P, 8, P])
        V.tensor_tensor(t8(M[:, 1, :, :]), t8(G), ends(0), ALU.subtract)
        V.tensor_tensor(t8(tmp[:, 0:2, :]), t8(E), ends(1), ALU.subtract).then_inc(sem("block_distances"), 1)
        low_to(27)
        dve.wait_ge(sem("block_decays"), i + 1)
        V.memset(B.small[:, 32:48], 1.0)
        V.drain()
        for k in range(3):
            V.tensor_tensor(cum[:, 0, :, k + 1:k + 2], cum[:, 0, :, k:k + 1], dec[:, 0, :, k:k + 1], ALU.mult)
            V.tensor_tensor(cum[:, 1, :, 2 - k:3 - k], cum[:, 1, :, 3 - k:4 - k], dec[:, 1, :, 3 - k:4 - k], ALU.mult)
            V.drain()
        low_to(29)
        dve.wait_ge(sem("cross_decays"), i + 1)
        V.tensor_tensor(M[:, 0, :, :], M[:, 0, :, :], qh, ALU.mult)
        V.tensor_tensor(M[:, 1, :, :], M[:, 1, :, :], kh, ALU.mult)
        V.tensor_tensor(tmp[:, 0:2, :], tmp[:, 0:2, :], qh, ALU.mult)
        V.tensor_tensor(tmp[:, 2:4, :], tmp[:, 2:4, :], kh, ALU.mult)
        low_to(31)
        V.drain()
        primed = at(AT_G, 4, 2, P)
        for n, (x, b, d, k) in enumerate(((M[:, 1, :, :], 0, 0, 1), (M[:, 0, :, :], 3, 0, 2),
                                          (tmp[:, 0:2, :], 0, 1, 1), (tmp[:, 2:4, :], 3, 1, 2))):
            V.tensor_tensor(primed[:, n, :, :], x[:, :, b * P:(b + 1) * P],
                            dec[:, d, :, k:k + 1].to_broadcast([P, 2, P]), ALU.mult)
        V.drain().then_inc(sem("cross_weighted"), 1)
        c8 = lambda d: B.small[:, 32 + 8 * d:40 + 8 * d].unsqueeze(2).to_broadcast([P, 8, P])
        V.tensor_tensor(t8(E), t8(M[:, 0, :, :]), c8(0), ALU.mult)
        V.tensor_tensor(t8(at(AT_QB, 2, S)), t8(tmp[:, 0:2, :]), c8(1), ALU.mult)
        V.drain().then_inc(sem("state_queries"), 1)
        low_to(34)
        dve.wait_ge(sem("o_summed"), i + 1)
        R = at(AT_R, S)
        V.tensor_scalar(R, ps[:, 6, :], 1.0 / DK, LN_EPS, ALU.mult, ALU.add).then_inc(sem("o_variance"), 1)
        dve.wait_ge(sem("o_deviation"), i + 1)
        V.reciprocal(R, R)
        V.drain()
        for a in range(2):
            V.scalar_tensor_tensor(out=Y[:, bass.ds(i * 2 + a, 1), :], in0=ps[:, 4 + a:5 + a, :],
                                   scalar=B.vec[:, VEC["gla_w"] + a:VEC["gla_w"] + a + 1], in1=R.unsqueeze(1),
                                   op0=ALU.mult, op1=ALU.mult)
        V.drain().then_inc(sem("heads_done"), 1)
        low_to(36)


def pool_vector(B, dve, i, banks, free):
    nc, sem, at, Y = B.nc, B.sem, B.at, B.Y
    ALU = mybir.AluOpType
    V = nc.vector
    x = at(TMP, 4, S)
    V.tensor_copy(x, banks).then_inc(free, 1)
    V.drain()
    g = x.rearrange("p a (r w) -> p a r w", w=GRID_W)
    sums = at(AT_ROWS, 4, (GRID_R + 1) * GRID_W).rearrange("p a (r w) -> p a r w", w=GRID_W)
    if i == 0:
        V.memset(sums[:, :, 0, :], 0.0)
    V.tensor_copy(sums[:, :, 1, :], g[:, :, 0, :])
    V.drain()
    for r in range(1, GRID_R):
        V.tensor_tensor(sums[:, :, r + 1, :], sums[:, :, r, :], g[:, :, r, :], ALU.add)
        V.drain()
    window = 2 << i
    out = Y[:, 4 * i:4 * i + 4, :].rearrange("p a (r w) -> p a r w", w=GRID_W)
    for r in range(GRID_R):
        a, b = max(r - window // 2, 0), min(r + window - window // 2, GRID_R)
        V.tensor_tensor(out[:, :, r, :], sums[:, :, b, :], sums[:, :, a, :], ALU.subtract)
    V.drain()
    for r in range(GRID_R):
        a, b = max(r - window // 2, 0), min(r + window - window // 2, GRID_R)
        last = V.scalar_tensor_tensor(out=out[:, :, r, :], in0=out[:, :, r, :], scalar=1.0 / (b - a),
                                      in1=g[:, :, r, :], op0=ALU.mult, op1=ALU.subtract)
    last.then_inc(sem("pooled"), 1)


def model_kernel(nc, A, out):
    B = Build(nc, A, out)
    with nc.Block() as block:

        @block.sync
        def _(sp):
            with nc.allow_non_contiguous_dma(reason="columns of small tables"):
                sync_program(B, sp)

        @block.gpsimd
        def _(pool):
            pool_program(B, pool)

        @block.scalar
        def _(act):
            scalar_program(B, act)

        @block.vector
        def _(dve):
            vector_program(B, dve)

        @block.tensor
        def _(pe):
            tensor_program(B, pe)


def constants():
    i = np.arange(P)
    row, col = i[:, None], i[None, :]
    f = lambda c: c.astype(np.float32)
    restart = np.broadcast_to(f(np.arange(S) % P != 0), (P, S))
    table = np.concatenate([f(row == col), np.ones((P, P), np.float32), f(row > col), f(row < col),
                            np.where(col > row, np.float32(NEG), np.float32(0)), 2 * f(row == col), f(row <= col),
                            restart], axis=1)
    masks = []
    for h in LEVELS:
        pair = (row // (2 * h) == col // (2 * h)) & (row // h != col // h)
        masks += [pair & (row < col), pair & (row > col)]
    return np.ascontiguousarray(table), np.ascontiguousarray(f(np.stack(masks, 1).reshape(P, -1)))


_INS = ["x", "c", "norm_g", "w_ada", "b_ada", "w_in", "ln_v_g", "ln_v_b", "w_s", "b_s", "b_f", "w_out", "final_g",
        "c_2", "ctx_2", "c_ctx_2", "w_ada_2", "b_ada_2", "ln_g_2", "ln_b_2", "w_in_e_2", "w_gate_f_2", "b_gate_f_2",
        "w_gate_b_2", "b_gate_b_2", "gla_norm_w_2", "conv_w_2", "w_out_e_2", "w_in_o_2", "w_pool_2", "pool_scale_2",
        "w_out_o_2"]


def kernel(**inputs):
    import concourse.bacc as _bacc
    from concourse.bass_utils import run_bass_kernel_spmd as _run

    nc = _bacc.Bacc("TRN2", target_bir_lowering=False, num_devices=1, dynamic_dma_scratch_size=1024)
    arrays = {name: np.ascontiguousarray(inputs[name]) for name in _INS}
    arrays["const"], arrays["masks"] = constants()
    A, feeds = {}, {}
    for name, a in arrays.items():
        feeds[f"in_{name}"] = a
        A[name] = nc.dram_tensor(f"in_{name}", a.shape, mybir.dt.from_np(a.dtype), kind="ExternalInput").ap()
    out = nc.dram_tensor("out_0", (1, S, D), mybir.dt.float32, kind="ExternalOutput").ap()
    model_kernel(nc, A, out)
    return _run(nc, [feeds], core_ids=[0]).results[0]["out_0"]
```

```python
import numpy as np
import concourse.bass as bass
from concourse import mybir

P = 128
D = 2048
S = 512
SC = 256
KT = D // P
GC = 512
NT = S // P
NTC = SC // P
EPS, LN_EPS = 1e-6, 1e-5
ALPHA = float(np.float32(4.0 ** 0.25))
TAU = 16.0
HEADS_A, HEADS_B, DH_B = 8, 16, 64
GLA_HEADS, DK = 4, 256
GRID_R, GRID_W = 8, 64
LEVELS = (64, 32, 16, 8, 4, 2, 1)
RING = 4
RAW = 4
NEG = -1.0e30

B1, E_IN = "w_in", "w_in_e_2"


def plan():
    g = []

    def add(name, w, col, n, mode, operand, kt=KT, tile0=0, tok=S, width=GC):
        for i in range(n):
            g.append(dict(name=name, i=i, n=n, w=w, col=col + GC * i, width=width, mode=mode,
                          operand=operand, kt=kt, tile0=tile0 + 4 * i if kt < KT else 0, tok=tok, part=None))

    add("va", B1, 1024, 2, "N", 0)
    add("f", B1, 7072, 1, "T", 0, width=112)
    add("q", B1, 3072, 2, "T", 0)
    add("k", B1, 4096, 2, "T", 0)
    add("v", B1, 5120, 2, "N", 0)
    add("ua", B1, 0, 2, "T", 0)
    add("ga", B1, 2048, 2, "T", 0)
    add("gb", B1, 6144, 2, "T", 0)
    add("wo1", "w_out", 0, 4, "T", 1)
    add("cr", E_IN, 2048, 1, "T", 2, tok=SC, width=P)
    add("ck", E_IN, 0, 2, "N", 2, tok=SC)
    add("cv", E_IN, 1024, 2, "N", 2, tok=SC)
    add("r", E_IN, 2048, 1, "T", 3, width=P)
    add("ek", E_IN, 0, 2, "T", 3)
    add("eq", E_IN, 2080, 2, "T", 3)
    add("ev", E_IN, 1024, 2, "N", 3)
    add("beside", E_IN, 4128, 2 * GLA_HEADS, "T", 3)
    add("egb", E_IN, 3104, 2, "T", 3)
    add("wo2", "w_out_e_2", 0, 4, "T", 4)
    add("xp", "w_in_o_2", 0, 4, "T", 5)
    add("gt", "w_in_o_2", 2048, 4, "T", 5)
    for i in range(4):
        g.append(dict(name="pool", i=i, n=4, w=f"w_pool_2.{i}", col=0, width=GC, mode="T", operand=6,
                      kt=4, tile0=4 * i, tok=S, part=None))
    add("wo3", "w_out_o_2", 0, 4, "T", 7)
    first = {}
    kc = 0
    for n, x in enumerate(g):
        x["kc"] = kc
        kc += x["kt"]
        first.setdefault(x["name"], n)
    total = kc
    part = 8
    for start, count in ((first["va"], 8), (first["gb"], 5), (first["ck"], 1), (first["r"], 6),
                         (first["egb"] + 1, 8)):
        for j in range(count):
            g[start + j]["part"] = part
            part += 1
    return g, first, total


GROUPS, FIRST, CHUNKS = plan()
DVE_EVAC = ("wo1", "wo2", "wo3", "xp", "pool")
VEC = {}
_at = 0
for _n, _k in (("c", 16), ("c2", 16), ("cc", 16), ("norm_g", 16), ("final_g", 16), ("b_ada", 144),
               ("ln_g", 32), ("ln_b", 32), ("gla_w", 2), ("conv", 24), ("pool_s", 16)):
    VEC[_n] = _at
    _at += _k
NVEC = _at


T_ENTER, T_LOGIT, T_DIAGONAL = 2, 4, 3
T_LEVEL = [2 if n == len(LEVELS) else 1 for n in range(2 * len(LEVELS))]
T_CROSS, T_TAKEN, T_OUT = 5, 1, 2
T_HEAD = T_ENTER + T_LOGIT + T_DIAGONAL
assert T_HEAD + sum(T_LEVEL) + T_CROSS + T_TAKEN + T_OUT == 2 * KT


def first_use(operand):
    return next(n for n, x in enumerate(GROUPS) if x["operand"] == operand)


def early(n):
    if n and GROUPS[n - 1]["operand"] == GROUPS[n]["operand"] or GROUPS[n]["name"] == "cr":
        return 0
    return min(GROUPS[n]["kt"], KT - 4)


def attention_first(k):
    return FIRST[("ua", "ga")[k]]


def level_tiles(n):
    return T_HEAD + sum(T_LEVEL[:n + 1]) if n >= 0 else T_HEAD + n + 1


N_CONST = 7 * P + S
TMP = 0
AT_X_TOK, AT_START, AT_WS_RAW = 0, 8192, 16384
AT_VA, AT_K, AT_V, AT_WST, AT_BS, AT_F, AT_FQ = 2048, 6144, 10240, 14336, 15360, 16384, 16896
AT_NEGF, AT_LOGIT, AT_PT, AT_OTOK, AT_QST, AT_KST = 2048, 3072, 4096, 5120, 14336, 15360
AT_XRES, AT_SQ, AT_RSTD, AT_SUM = 2048, 4096, 8192, 12544
AT_CTOK, AT_KC, AT_VC, AT_RC, AT_WGC = 8704, 8704, 10752, 12800, 13056
AT_LAC, AT_TC, AT_STO = 0, 4096, 13056
AT_RT, AT_WG, AT_VE, AT_ST, AT_VH, AT_G, AT_E, AT_M, AT_AM, AT_R, AT_QB = (
    2048, 2560, 3072, 7168, 8192, 9216, 10240, 11264, 13312, 15360, 15872)
AT_CONV, CONV_SLOTS = 3072, 7
AT_ROWS, AT_GATE = 2048, 4352
AT_OUT = 8704
ARENA = 17408


class Build:

    def __init__(self, nc, A, out):
        self.nc, self.A, self.out = nc, A, out
        f32, f32r, u8 = mybir.dt.float32, mybir.dt.float32r, mybir.dt.uint8

        def sb(name, shape, dt=f32):
            return nc.alloc_sbuf_tensor(name, shape, dt)

        self.op_hi = sb("op_hi", [P, KT, S], f32r)
        self.op_lo = sb("op_lo", [P, KT, S], f32r)
        self.Y = sb("Y", [P, KT, S])
        self.w_raw = sb("w_raw", [P, RAW, 2, GC])
        self.w_hi = sb("w_hi", [P, RING, GC], f32r)
        self.w_lo = sb("w_lo", [P, RING, GC], f32r)
        self.a_raw = sb("a_raw", [P, 2, 2, GC])
        self.acc = sb("acc", [P, 2, 2, GC])
        self.const = sb("const", [P, N_CONST])
        self.masks = sb("masks", [P, 2 * len(LEVELS), P], u8)
        self.vec = sb("vec", [P, NVEC])
        self.mod = sb("mod", [P, 144 + 32])
        self.bf = sb("bf", [P, 1])
        self.small = sb("small", [P, 96])
        self.arena = sb("arena", [P, ARENA])
        self.ps = nc.alloc_psum_tensor("ps", [P, 8, GC], f32)
        c = self.const
        self.ident, self.ones = c[:, 0:P], c[:, P:2 * P]
        self.tri_gt, self.tri_lt = c[:, 2 * P:3 * P], c[:, 3 * P:4 * P]
        self.causal, self.eye2 = c[:, 4 * P:5 * P], c[:, 5 * P:6 * P]
        self.tri_le = c[:, 6 * P:7 * P]
        self.restart = c[:, 7 * P:7 * P + S]
        self.x_sp = nc.dram_tensor("x_spill", (P, KT, S), f32, kind="Internal").ap()
        self.f_sp = nc.dram_tensor("f_spill", (HEADS_B, S), f32, kind="Internal").ap()
        self.s_sp = nc.dram_tensor("state_spill", (P, GLA_HEADS, 4 * DK), f32, kind="Internal").ap()
        self.c_sp = nc.dram_tensor("conv_spill", (P, 2 * GLA_HEADS, 4 * S), f32, kind="Internal").ap()
        self.sems = {}
        self.bank_free = [self.sem("even_banks_free"), self.sem("odd_banks_free")]
        self.w_in = [self.sem(f"weights_in_{i}") for i in range(RAW)]
        self.a_in = [self.sem(f"modulation_in_{i}") for i in range(2)]
        self.start_in = [self.sem(f"start_in_{i}") for i in range(8)]

    def at(self, word, *shape):
        n = 1
        for k in shape:
            n *= k
        assert word + n <= ARENA, (word, shape)
        v = self.arena[:, word:word + n]
        if len(shape) == 2:
            v = v.rearrange("p (a b) -> p a b", a=shape[0])
        if len(shape) == 3:
            v = v.rearrange("p (a b c) -> p a b c", a=shape[0], b=shape[1])
        return v

    def sem(self, name):
        if name not in self.sems:
            self.sems[name] = self.nc.alloc_semaphore(name)
        return self.sems[name]

    def weight(self, g):
        name, _, part = g["w"].partition(".")
        w = self.A[name]
        w = w[0, int(part)] if part else w[0]
        return w.rearrange("(k p) n -> p k n", p=P)


def ordinal(n):
    return sum(x["part"] is not None for x in GROUPS[:n])


def ctx_part(part):
    return 12 <= part < 20


TMP_USERS = ("ua", "ga", "gb", "egb")


def tmp_uses(n):
    return sum(x["name"] in TMP_USERS for x in GROUPS[:n])


def sync_program(B, sp):
    A, sem, at = B.A, B.sem, B.at

    rows = B.Y[:, 15, :].rearrange("p (r c) -> p r c", c=P)
    loads = 0

    def vector(name, src):
        nonlocal loads
        k, n = VEC[name], src.shape[0]
        while n:
            r, q = divmod(k, P)
            m = min(n, P - q)
            sp.dma_start(rows[q:q + m, r, :], src[0:m, :]).then_inc(sem("rows_in"), 16)
            loads += 1
            k, n = k + m, n - m
            src = src[m:, :] if n else src

    cut = lambda a: a.rearrange("(k p) -> k p", p=P)
    vector("c", cut(A["c"][0]))
    vector("c2", cut(A["c_2"][0]))
    vector("cc", cut(A["c_ctx_2"]))
    vector("norm_g", cut(A["norm_g"][0]))
    vector("final_g", cut(A["final_g"]))
    vector("b_ada", cut(A["b_ada"][0]))
    VEC["b_ada_2"] = VEC["b_ada"] + 48
    vector("b_ada_2", A["b_ada_2"].rearrange("l (k p) -> (l k) p", p=P))
    vector("ln_g", A["ln_g_2"].rearrange("l (k p) -> (l k) p", p=P))
    vector("ln_b", A["ln_b_2"].rearrange("l (k p) -> (l k) p", p=P))
    vector("gla_w", cut(A["gla_norm_w_2"][0]))
    vector("conv", A["conv_w_2"][0].rearrange("t (k p) -> (t k) p", p=P))
    vector("pool_s", cut(A["pool_scale_2"][0]))
    assert loads == N_ROW_LOADS, loads
    sp.dma_start(B.const[:, :], A["const"]).then_inc(sem("const_in"), 16)

    ring = at(AT_START, 8, 1024)
    w_ada = A["w_ada"][0].rearrange("(k p) n -> p k n", p=P)
    for n in range(64):
        pair, kt = divmod(n, KT)
        if n >= 8:
            sp.wait_ge(sem("acc_step"), start_step(n - 8))
        sp.dma_start(ring[:, n % 8, :], w_ada[:, kt, pair * 1024:(pair + 1) * 1024]).then_inc(B.start_in[n % 8], 16)
        if n == 7:
            sp.dma_start(at(AT_X_TOK, NT, D), A["x"][0].rearrange("(n p) d -> p n d", p=P)).then_inc(sem("x_in"), 16)
            sp.dma_start(at(AT_WS_RAW, HEADS_A, P), A["w_s"][0].rearrange("h t s -> t h s")).then_inc(sem("ws_in"), 16)
            sp.dma_start(B.bf[96:112, :], A["b_f"].rearrange("o h -> h o")).then_inc(sem("bf_in"), 16)
            sp.dma_start(B.a_raw[:, :, :, :].rearrange("p a b c -> p (a b c)")[:, 0:2 * len(LEVELS) * P],
                         A["masks"]).then_inc(sem("masks_in"), 16)
    sp.wait_ge(sem("x_turned"), KT)
    sp.dma_start(B.x_sp, B.Y[:, :, :]).then_inc(sem("spilled"), 16)

    def spill_stream(m):
        sp.wait_ge(sem("scaled"), 4 * (m + 1))
        sp.dma_start(B.x_sp, B.Y[:, :, :]).then_inc(sem("spilled"), 16)

    def weights(n, m, r=0):
        g = GROUPS[n]
        slot = (g["kc"] // 2 + m) % RAW
        if g["kc"] + 2 * m >= 2 * RAW:
            sp.wait_ge(sem("lo_done"), r * 8 + (g["kc"] + 2 * m - 2 * RAW + 2))
        tiles = slice(2 * m, 2 * m + 2) if isinstance(r, int) else bass.ds(r * 8 + 2 * m, 2)
        sp.dma_start(B.w_raw[:, slot, :, 0:g["width"]],
                     B.weight(g)[:, tiles, g["col"]:g["col"] + g["width"]]).then_inc(B.w_in[slot], 16)

    def modulation(n, m):
        part, o = GROUPS[n]["part"], ordinal(n)
        if part is None:
            return
        src = A["w_ada"][0] if part < 12 else A["w_ada_2"][(part - 12) // 12]
        src = src.rearrange("(k p) n -> p k n", p=P)
        c = part % 12 * GC
        if o or m >= 2:
            sp.wait_ge(sem("part_tile"), KT * o + 2 * m - 2)
        sp.dma_start(B.a_raw[:, m % 2, :, :], src[:, 2 * m:2 * m + 2, c:c + GC]).then_inc(B.a_in[m % 2], 16)

    def stream(n, middle=None):
        pairs = GROUPS[n]["kt"] // 2
        before = n and GROUPS[n - 1]["part"] is not None
        if GROUPS[n]["part"] is None and not before and not middle and pairs == 8 and GROUPS[n]["name"] != "egb":
            with sp.Fori(0, 2) as r:
                for m in range(4):
                    weights(n, m, r)
            return
        for m in range(pairs):
            weights(n, m)
            if GROUPS[n]["name"] == "egb":
                conv_loads(GROUPS[n]["i"], m)
            if m < LAG and before and not (middle and m == 2):
                modulation(n - 1, 8 - LAG + m)
            if middle and m == 1:
                if before:
                    modulation(n - 1, 7)
                middle()
            if m >= LAG:
                modulation(n, m - LAG)

    def residual(n):
        i = GROUPS[n]["i"]
        if i == 0:
            if GROUPS[n]["name"] == "wo2":
                sp.wait_ge(sem("conv_done"), 8)
            sp.wait_ge(sem("spilled"), 16 * (1 + ("wo1", "wo2", "wo3").index(GROUPS[n]["name"])))
            sp.wait_ge(B.bank_free[(n - 1) % 2], (n - 1) // 2 + 1)
        else:
            sp.wait_ge(B.bank_free[(n - 1) % 2], (n - 1) // 2 + 1)
        sp.dma_start(at(AT_XRES, 4, S), B.x_sp[:, 4 * i:4 * i + 4, :]).then_inc(sem("residual_in"), 16)

    def attention_turn(r, k):
        g = GROUPS[attention_first(k)]

        def f_row(q, h):
            sp.wait_ge(sem("logits"), r * 16 + (32 * k + 8 * q + 4 * h + 4))
            sp.dma_start(at(AT_NEGF, 2, S)[:, h, :],
                         B.f_sp[bass.ds(r * 4 + (8 * k + 2 * q + h), 1), :].to_broadcast([P, S]))\
                .then_inc(B.sem(f"f_row_in_{h}"), 16)

        for m in range(KT // 2):
            slot = (g["kc"] // 2 + m) % RAW
            sp.wait_ge(sem("lo_done"), r * 16 + (g["kc"] + 2 * m - 2 * RAW + 2))
            sp.dma_start(B.w_raw[:, slot, :, :],
                         B.weight(g)[:, 2 * m:2 * m + 2, bass.ds(r * GC + g["col"], GC)]).then_inc(B.w_in[slot], 16)
            if m in (2, 4):
                f_row(0, m // 2 - 1)
            if m in (6, 7):
                f_row(1, m - 6)

    def state_stores():
        spill_stream(1)
        sp.wait_ge(sem("states_out"), 1)
        sp.dma_start(B.s_sp.rearrange("p h w -> p (h w)"), at(AT_STO, 1, 4096)[:, 0, :]).then_inc(sem("states_spilled"), 16)

    def head_loads(i):
        at_int = isinstance(i, int)
        gate_weights(B, sp, at(AT_WG, 2, DK), slice(0, DK) if at_int else bass.ds(i * DK, DK), sem("head_in"))
        sp.dma_start(at(AT_ST, 1, 4 * DK)[:, 0, :], B.s_sp[:, i, :] if at_int else
                     B.s_sp[:, bass.ds(i, 1), :].rearrange("p o w -> p (o w)")).then_inc(sem("head_in"), 16)

    def beside_store(k, i):
        sp.wait_ge(sem("beside_left"), i * 8 + (4 * k + 8))
        rows = B.c_sp[:, 2 * i + k, :] if isinstance(i, int) else \
            B.c_sp[:, bass.ds(i * 2 + k, 1), :].rearrange("p o w -> p (o w)")
        sp.dma_start(rows, B.a_raw[:, :, :, :].rearrange("p a b c -> p (a b c)")).then_inc(sem("beside_stored"), 16)

    def head_turn(i):
        g = GROUPS[FIRST["beside"]]
        for m in range(KT):
            slot = (g["kc"] // 2 + m) % RAW
            sp.wait_ge(sem("lo_done"), i * 32 + (g["kc"] + 2 * m - 2 * RAW + 2))
            col = g["col"] + m // 8 * GC
            cols = slice(col, col + GC) if isinstance(i, int) else bass.ds(i * 2 * GC + col, GC)
            sp.dma_start(B.w_raw[:, slot, :, :], B.weight(g)[:, 2 * (m % 8):2 * (m % 8) + 2, cols])\
                .then_inc(B.w_in[slot], 16)
            if m == 1 and isinstance(i, int):
                state_in()
            if m == 3 and not isinstance(i, int):
                sp.wait_ge(sem("o_mm"), i)
                head_loads(i)
            if m == 5 and not isinstance(i, int):
                beside_store(1, i - 1)
            if m == 12:
                beside_store(0, i)

    def state_in():
        sp.wait_ge(sem("states_spilled"), 16)
        sp.wait_ge(sem("gates_cleared"), 2)
        head_loads(0)

    def conv_loads(i, m):
        if i == 0 and m == 3:
            sp.wait_ge(sem("heads_done"), GLA_HEADS + 1)
            beside_store(1, GLA_HEADS - 1)
            sp.wait_ge(sem("beside_stored"), 16 * (2 * GLA_HEADS + 1))
        j = m - 3 if i == 0 else m + 5
        if 0 <= j < 8:
            if j >= CONV_SLOTS:
                sp.wait_ge(sem("conv_done"), j - CONV_SLOTS + 1)
            src = B.c_sp.rearrange("p (v h) (t s) -> p v (h t) s", v=4, t=4)
            sp.dma_start(at(AT_CONV, CONV_SLOTS, 4, S)[:, j % CONV_SLOTS, :, :], src[:, :, j, :])\
                .then_inc(B.sem(f"conv_in_{j}"), 16)

    middles = {FIRST["r"]: state_stores}
    sp.wait_ge(sem("masks_made"), 1)
    sp.wait_ge(sem("acc_step"), start_step(63))
    sp.dma_start(at(AT_BS, 1, HEADS_A * P)[:, 0, :],
                 A["b_s"].rearrange("o h t -> o (h t)").to_broadcast([P, HEADS_A * P])).then_inc(sem("bs_in"), 16)
    names = [x["name"] for x in GROUPS]
    for n, name in enumerate(names):
        g = GROUPS[n]
        if name == "beside":
            if g["i"] == 0:
                head_turn(0)
                with sp.Fori(1, GLA_HEADS) as i:
                    head_turn(i)
            continue
        if name in ("ua", "ga"):
            if g["i"] == 0:
                with sp.Fori(0, 2) as r:
                    attention_turn(r, name == "ga")
            continue
        stream(n, middles.get(n))
        if name == "xp" and g["i"] == 0:
            spill_stream(2)
        if name == "va" and g["i"] == 1:
            sp.wait_ge(sem("op_tile"), KT)
            for r, v in enumerate(("ln_v_g", "ln_v_b")):
                sp.dma_start(at(TMP, 2, 1024)[:, r, :], A[v].to_broadcast([P, 1024])).then_inc(sem("ln_rows_in"), 16)
        if name == "q" and g["i"] == 0:
            sp.wait_ge(sem("f_summed"), 1)
            sp.dma_start(B.f_sp, B.arena[96:112, AT_F:AT_F + S]).then_inc(sem("f_spilled"), 16)
            sp.wait_ge(sem("f_spilled"), 16)
            for b in range(NT):
                sp.dma_start(at(AT_FQ, NT, HEADS_B)[:, b, :],
                             B.f_sp[:, b * P:(b + 1) * P].rearrange("h p -> p h")).then_inc(sem("f_cols_in"), 16)
        if name in ("wo1", "wo2", "wo3"):
            residual(n)
        if name == "wo1" and g["i"] == 3:
            sp.dma_start(at(AT_CTOK, NTC, D), A["ctx_2"][0].rearrange("(n p) d -> p n d", p=P)).then_inc(sem("ctx_in"), 16)
        if name == "cr":
            sp.wait_ge(sem("gates_cleared"), 1)
            gate_weights(B, sp, at(AT_WGC, 2, 1024), slice(0, 1024), sem("ctx_gates_in"))
    for t in range(NT):
        sp.wait_ge(sem("out_rows"), t + 1)
        sp.dma_start(B.out[0, t * P:(t + 1) * P, :], at(AT_OUT, 2, D)[:, t % 2, :]).then_inc(sem(f"out_done_{t % 2}"), 16)
    for k in range(2):
        sp.wait_ge(sem(f"out_done_{k}"), 16 * NT // 2)


def gate_weights(B, sp, dst, cols, signal):
    for d, (w, b) in enumerate((("w_gate_f_2", "b_gate_f_2"), ("w_gate_b_2", "b_gate_b_2"))):
        sp.dma_start(dst[16 * d:16 * d + 16, d, :], B.A[w][0][:, cols]).then_inc(signal, 16)
        sp.dma_start(dst[32:33, d, :], B.A[b][0:1, cols]).then_inc(signal, 16)


N_ROW_LOADS = 12
LAG = 3


def start_step(n):
    pair, kt = divmod(n, KT)
    return 34 * pair + 2 + 2 * (kt + 1)


def pool_program(B, pool):
    nc, sem, at = B.nc, B.sem, B.at
    n = FIRST["wo1"]
    pool.wait_ge(B.bank_free[n % 2], n // 2 + 1)
    nc.gpsimd.memset(at(AT_WGC, 1, 2048)[0:33, 0, :], 0.0)
    nc.gpsimd.drain()
    nc.gpsimd.memset(B.arena[32:33, AT_RC:AT_RC + SC], 1.0)
    nc.gpsimd.drain()
    nc.gpsimd.memset(B.small[0:1, 95:96], 0.0).then_inc(sem("gates_cleared"), 1)
    pool.wait_ge(sem("states_out"), 1)
    nc.gpsimd.memset(at(AT_WG, 1, 512)[0:33, 0, :], 0.0)
    nc.gpsimd.drain()
    nc.gpsimd.memset(B.arena[32:33, AT_RT:AT_RT + S], 1.0)
    nc.gpsimd.drain()
    nc.gpsimd.memset(B.small[0:1, 95:96], 0.0).then_inc(sem("gates_cleared"), 1)


def scalar_program(B, act):
    nc, sem, at, ps, Y = B.nc, B.sem, B.at, B.ps, B.Y
    ACT = mybir.ActivationFunctionType
    f32 = mybir.dt.float32
    Act = nc.scalar.activation

    def high_tile(c, width):
        raw, fill = c // 2 % RAW, c // (2 * RAW)
        if c % 2 == 0:
            act.wait_ge(B.w_in[raw], 16 * (fill + 1))
        if c >= RING:
            act.wait_ge(sem("w_used"), c - RING + 1)
        Act(B.w_hi[:, c % RING, 0:width], B.w_raw[:, raw, c % 2, 0:width], ACT.Copy).then_inc(sem("hi_done"), 1)

    def step(n, t):
        c, k, width = GROUPS[n]["kc"], GROUPS[n]["kt"], GROUPS[n]["width"]
        after = GROUPS[n + 1]["width"] if n + 1 < len(GROUPS) else 0
        if t < k - 4:
            high_tile(c + 4 + t, width)
        elif after:
            high_tile(c + 4 + t, after)

    def ahead(n):
        c, k, width = GROUPS[n]["kc"], GROUPS[n]["kt"], GROUPS[n]["width"]
        after = GROUPS[n + 1]["width"] if n + 1 < len(GROUPS) else 0
        if k == KT and after == width and not early(n):
            with act.Fori(0, 2) as r:
                for t in range(c + 4, c + 12):
                    raw = t // 2 % RAW
                    if t % 2 == 0:
                        act.wait_ge(B.w_in[raw], r * 16 + 16 * (t // (2 * RAW) + 1))
                    act.wait_ge(sem("w_used"), r * 8 + (t - RING + 1))
                    Act(B.w_hi[:, t % RING, 0:width], B.w_raw[:, raw, t % 2, 0:width],
                        ACT.Copy).then_inc(sem("hi_done"), 1)
        else:
            for t in range(early(n), k):
                step(n, t)

    def conv_ahead(n):
        for t in range(KT):
            high_tile(GROUPS[n]["kc"] + 4 + t, GC)
            for j in range(8):
                if CONV_AT[j] == (GROUPS[n]["i"], t):
                    act.wait_ge(sem(f"conv_in_{j}"), 16)
                    x = at(AT_CONV, CONV_SLOTS, 4, S)[:, j % CONV_SLOTS, 3, :]
                    Act(x, x, ACT.Silu).then_inc(sem("conv_gate"), 1)

    def split_hi(operand, src, tok=S, tiles=KT):
        if operand:
            last = max(x["kc"] + x["kt"] for x in GROUPS if x["operand"] == operand - 1)
            act.wait_ge(sem("w_used"), last)
        for t in range(tiles):
            Act(B.op_hi[:, t, 0:tok], src(t), ACT.Copy).then_inc(sem("op_high"), 1)
            if 4 <= t < 4 + early(first_use(operand)):
                step(first_use(operand), t - 4)

    def from_mod(operand, tok=S, m=None):
        def src(t):
            if m is not None and t % 4 == 0 and t < 12:
                gains(m, t // 4 + 1)
            act.wait_ge(sem("modulated"), modulated(operand) + t + 1)
            return at(TMP, 4, S)[:, t % 4, 0:tok]
        split_hi(operand, src, tok)

    def from_y(operand, first=0, tiles=KT):
        def src(t):
            return Y[:, t, :]
        split_hi(operand, src)

    def norm(m, chunks=4):
        sqr = at(AT_SQ, 2, 2048)
        for j in range(4):
            if m >= 2:
                act.wait_ge(sem("centred"), 4 * (m - 2) + j + 1)
            elif m == 1:
                n = FIRST["wo1"] + j
                act.wait_ge(B.bank_free[n % 2], n // 2 + 1)
            if m == 0:
                act.wait_ge(sem("x_turned"), 4 * j + 4)
            k = 4 * m + j
            if j >= 2:
                act.wait_ge(sem("squares_summed"), k - 1)
            Act(sqr[:, j % 2, :], Y[:, 4 * j:4 * j + 4, :].rearrange("p a b -> p (a b)"),
                ACT.Square).then_inc(sem("squared"), 1)
        act.wait_ge(sem("variance"), m + 1)
        r = at(AT_RSTD, 1, S)[:, 0, :]
        Act(r, r, ACT.Ln)
        nc.scalar.drain()
        Act(r, r, ACT.Exp, scale=-0.5).then_inc(sem("deviation"), 1)
        if m == 0:
            for c in range(4):
                high_tile(c, GC)
        for j in range(chunks):
            gains(m, j)

    def gains(m, j):
        gain = VEC["norm_g"] if m == 0 else VEC["final_g"] if m == 1 else VEC["ln_g"] + 16 * (m - 2)
        act.wait_ge(sem("normed"), 4 * m + j + 1)
        for t in range(4 * j, 4 * j + 4):
            scale = B.vec[:, gain + t:gain + t + 1]
            if m < 2:
                last = Act(Y[:, t, :], Y[:, t, :], ACT.Copy, scale=scale)
            else:
                b = VEC["ln_b"] + 16 * (m - 2) + t
                last = Act(Y[:, t, :], Y[:, t, :], ACT.Identity, scale=scale, bias=B.vec[:, b:b + 1])
        last.then_inc(sem("scaled"), 1)

    act.wait_ge(sem("columns"), 1)
    Act(B.vec[:, :], ps[:, 0, 0:NVEC], ACT.Copy)
    nc.scalar.drain()
    Act(B.vec[:, 0:48], B.vec[:, 0:48], ACT.Silu).then_inc(sem("vec_ready"), 1)
    for t in range(KT):
        act.wait_ge(sem("turned"), t + 1)
        Act(Y[:, t, :], ps[:, 1 + t % 4, :], ACT.Copy).then_inc(sem("x_turned"), 1)
    norm(0, 1)
    from_mod(0, m=0)

    for n, g in enumerate(GROUPS):
        name, i = g["name"], g["i"]
        if name == "beside":
            if i == 0:
                gla_scalar(B, act)
            continue
        if name in ("ua", "ga"):
            if i == 0:
                attention_scalar(B, act, name == "ga")
            continue
        if name == "egb":
            conv_ahead(n)
        else:
            ahead(n)
        bank = 4 * (n % 2)
        free = B.bank_free[n % 2]
        if name not in DVE_EVAC:
            act.wait_ge(sem("w_used"), g["kc"] + g["kt"])
        banks = ps[:, bank:bank + 4, :]
        if name == "va":
            Act(at(AT_VA, NT, 1024)[:, :, i * GC:(i + 1) * GC], banks, ACT.Gelu).then_inc(free, 1)
        if name == "f":
            f = B.arena[96:112, AT_F:AT_F + S]
            f2 = B.arena[96:112, AT_FQ:AT_FQ + S]
            act.wait_ge(sem("bf_in"), 16)
            Act(f, ps[96:112, bank, :], ACT.Identity, bias=B.bf[96:112, :]).then_inc(free, 1)
            nc.scalar.drain()
            Act(f2, f, ACT.Abs)
            nc.scalar.drain()
            Act(f2, f2, ACT.Exp, scale=-1.0)
            nc.scalar.drain()
            Act(f2, f2, ACT.Ln, bias=1.0).then_inc(sem("f_log"), 1)
            act.wait_ge(sem("value_variance"), 1)
            Act(B.small[:, 0:4], B.small[:, 0:4], ACT.Sqrt).then_inc(sem("value_deviation"), 1)
        if name == "q":
            Act(Y[:, 8 + 4 * i:12 + 4 * i, :], banks, ACT.Copy, scale=DH_B ** -0.5).then_inc(free, 1)
        if name == "k":
            Act(at(AT_K, 8, S)[:, 4 * i:4 * i + 4, :], banks, ACT.Copy).then_inc(free, 1)
        if name == "v":
            Act(at(AT_V, NT, 1024)[:, :, i * GC:(i + 1) * GC], banks, ACT.Copy).then_inc(free, 1)
            if i == 1:
                nc.scalar.drain()
                act.wait_ge(sem("value_normed"), 2)
                act.wait_ge(sem("mixing"), HEADS_A)
        if name in TMP_USERS:
            act.wait_ge(sem("tmp_free"), tmp_uses(n) + 1)
            Act(at(TMP, 4, S), banks, ACT.Silu).then_inc(sem("tmp_full"), 1)
            nc.scalar.drain().then_inc(free, 1)
        if name == "gb" and i == 1:
            act.wait_ge(sem("mixer_out"), 1)
            from_y(1)
        if name == "wo1" and i == 3:
            from_mod(2, SC)
        if name == "cr":
            Act(B.arena[0:32, AT_RC:AT_RC + SC], ps[0:32, bank, 0:SC], ACT.Copy).then_inc(free, 1)
            norm(1)
        if name == "ck":
            Act(at(AT_KC, NTC, 1024)[:, :, i * GC:(i + 1) * GC], ps[:, bank:bank + 2, :], ACT.Copy).then_inc(free, 1)
        if name == "cv":
            Act(at(AT_VC, NTC, 1024)[:, :, i * GC:(i + 1) * GC], ps[:, bank:bank + 2, :], ACT.Copy).then_inc(free, 1)
            if i == 1:
                context_scalar(B, act)
                from_mod(3)
        if name == "r":
            act.wait_ge(sem("gates_cleared"), 2)
            Act(B.arena[0:32, AT_RT:AT_RT + S], ps[0:32, bank, :], ACT.Copy).then_inc(free, 1)
        if name == "ek":
            Act(Y[:, 4 * i:4 * i + 4, :], banks, ACT.Copy).then_inc(free, 1)
        if name == "eq":
            Act(Y[:, 8 + 4 * i:12 + 4 * i, :], banks, ACT.Copy, scale=DK ** -0.5).then_inc(free, 1)
        if name == "ev":
            Act(at(AT_VE, NT, 1024)[:, :, i * GC:(i + 1) * GC], banks, ACT.Copy).then_inc(free, 1)
        if name == "gt":
            Act(at(AT_GATE, KT, S)[:, 4 * i:4 * i + 4, :], banks, ACT.Silu).then_inc(free, 1)
            if i == 3:
                act.wait_ge(sem("pooled"), 4)
                from_y(6)
        if name == "egb" and i == 1:
            act.wait_ge(sem("mixer_out"), 2)
            from_y(4)
        if name == "wo2" and i == 3:
            norm(2, 1)
            from_mod(5, m=2)
        if name == "pool" and i == 3:
            act.wait_ge(sem("mixer_out"), 3)
            from_y(7)
    norm(3)
    for t in range(NT):
        for j in range(4):
            k = 4 * t + j
            act.wait_ge(sem("out_turned"), k + 1)
            if t >= 2 and j == 0:
                act.wait_ge(sem(f"out_done_{t % 2}"), 16 * (t // 2))
            Act(at(AT_OUT, 2, D)[:, t % 2, j * GC:(j + 1) * GC], ps[:, k % 4, :], ACT.Copy).then_inc(sem("out_taken"), 1)
        nc.scalar.drain().then_inc(sem("out_rows"), 1)


CONV_AT = [(0, 9), (0, 12), (0, 15), (1, 1), (1, 4), (1, 7), (1, 10), (1, 13)]
MOD_OPERANDS = {0: 0, 2: 16, 3: 32, 5: 48}


def modulated(operand):
    return MOD_OPERANDS[operand]


def attention_scalar(B, act, k):
    nc, sem, at, ps, Y = B.nc, B.sem, B.at, B.ps, B.Y
    ACT = mybir.ActivationFunctionType
    Act = nc.scalar.activation
    logit, p_t = at(AT_LOGIT, 2, S), at(AT_PT, 2, S)
    kc = GROUPS[attention_first(k)]["kc"]
    if not k:
        act.sem_inc(sem("p_taken"), 1)
        act.sem_inc(sem("gate_left"), 4)
    with act.Fori(0, 2) as i:
        made = 4

        def high_to(tiles):
            nonlocal made
            while made < tiles:
                c = kc + made
                if c % 2 == 0:
                    act.wait_ge(B.w_in[c // 2 % RAW], i * 32 + 16 * (c // (2 * RAW) + 1))
                act.wait_ge(sem("w_used"), i * 16 + (c - RING + 1))
                Act(B.w_hi[:, c % RING, :], B.w_raw[:, c // 2 % RAW, c % 2, :], ACT.Copy).then_inc(sem("hi_done"), 1)
                made += 1

        act.wait_ge(sem("scores"), i * 16 + (32 * k + 1))
        act.sem_inc(sem("scalar_passed"), 1)
        Act(at(AT_QST, 2, S), Y[:, bass.ds(i * 2 + (4 * k + 8), 2), :], ACT.Copy).then_inc(sem("staged"), 1)
        Act(at(AT_KST, 2, S), at(AT_K, 8, S)[:, bass.ds(i * 2 + 4 * k, 2), :], ACT.Copy).then_inc(sem("staged"), 1)
        for u in range(17):
            if u < 16:
                w = P * (u % 4 + 1)
                act.wait_ge(sem("logits"), i * 16 + (32 * k + u + 9))
                Act(logit[:, u % 2, 0:w], logit[:, u % 2, 0:w], ACT.Exp, bias=B.small[:, 8 + u % 2:9 + u % 2],
                    accum_out=B.small[:, 16 + u:17 + u]).then_inc(sem("probs"), 1)
            if u == 11:
                pair_out(B, act, i, k, 0)
            if u >= 1:
                w = P * ((u - 1) % 4 + 1)
                act.wait_ge(sem("p_turned"), i * 16 + (32 * k + u + 2))
                act.wait_ge(sem("pv"), i * 16 + (32 * k + u))
                Act(p_t[:, (u - 1) % 2, 0:w], ps[:, 6, 0:w], ACT.Copy).then_inc(sem("p_taken"), 1)
            high_to(u + 3)
        high_to(20)
        act.wait_ge(sem("w_used"), i * 16 + (kc + KT))
        act.wait_ge(sem("tmp_free"), i + (2 * k + 1))
        for b in range(4):
            Act(at(TMP, 4, S)[:, b, :], ps[:, b, :], ACT.Silu if k else ACT.Gelu).then_inc(sem("gate_left"), 1)
        nc.scalar.drain().then_inc(sem("tmp_full"), 1)
        pair_out(B, act, i, k, 1)
    for n in range(2):
        nc.scalar.drain().then_inc(B.bank_free[n], 1)


def pair_out(B, act, i, k, q):
    act.wait_ge(B.sem("o_turned"), i * 2 + (4 * k + q + 3))
    act.sem_inc(B.sem("scalar_passed"), 1)
    B.nc.scalar.activation(B.Y[:, bass.ds(i * 2 + (4 * k + q + 8), 1), :], B.ps[:, 6:7, :],
                           mybir.ActivationFunctionType.Copy).then_inc(B.sem("o_taken"), 1)


def context_scalar(B, act):
    nc, sem, at, ps = B.nc, B.sem, B.at, B.ps
    ACT = mybir.ActivationFunctionType
    Act = nc.scalar.activation
    tc = at(AT_TC, 8, GC)
    act.wait_ge(sem("ctx_logits"), 1)
    Act(tc, ps[:, :, :], ACT.Abs)
    nc.scalar.drain()
    Act(tc, tc, ACT.Exp, scale=-1.0)
    nc.scalar.drain()
    Act(tc, tc, ACT.Ln, bias=1.0).then_inc(sem("ctx_log"), 1)
    act.wait_ge(sem("ctx_sums"), 1)
    act.wait_ge(sem("ctx_gates"), 1)
    Act(tc, ps[:, :, :], ACT.Exp, scale=1.0 / TAU).then_inc(sem("ctx_decays"), 1)
    act.wait_ge(sem("ctx_states"), 1)
    Act(at(AT_STO, 8, GC), ps[:, :, :], ACT.Copy).then_inc(sem("states_out"), 1)


def gla_scalar(B, act):
    nc, sem, at, ps, Y = B.nc, B.sem, B.at, B.ps, B.Y
    ACT = mybir.ActivationFunctionType
    Act = nc.scalar.activation
    M, tmp, G, E = at(AT_M, 2, 2, S), at(TMP, 4, S), at(AT_G, 2, S), at(AT_E, 2, S)
    am = at(AT_AM, NT, S)
    tot = B.small[:, 0:16]
    first = FIRST["beside"]
    kc = GROUPS[first]["kc"]
    nc.scalar.drain()
    act.sem_inc(sem("beside_left"), 4)
    act.sem_inc(sem("beside_stored"), 16)
    act.wait_ge(sem("part_tile"), KT * ordinal(first))
    with act.Fori(0, GLA_HEADS) as i:
        made = 4

        def high_to(tiles):
            nonlocal made
            while made < tiles:
                c = kc + made
                if c % 2 == 0:
                    act.wait_ge(B.w_in[c // 2 % RAW], i * 64 + 16 * (c // (2 * RAW) + 1))
                act.wait_ge(sem("w_used"), i * 32 + (c - RING + 1))
                Act(B.w_hi[:, c % RING, :], B.w_raw[:, c // 2 % RAW, c % 2, :], ACT.Copy).then_inc(sem("hi_done"), 1)
                made += 1

        def leave(k):
            act.wait_ge(sem("w_used"), i * 32 + (kc + KT * (k + 1)))
            act.wait_ge(sem("beside_stored"), i * 32 + 16 * (k + 1))
            out = B.a_raw[:, :, :, :].rearrange("p a b c -> p (a b) c")
            for b in range(4):
                Act(out[:, b, :], ps[:, b, :], ACT.Copy).then_inc(sem("beside_left"), 1)

        act.wait_ge(sem("heads_done"), i + 1)
        act.sem_inc(sem("scalar_passed"), 1)
        Act(at(AT_VH, NT, DK), at(AT_VE, NT, 1024)[:, :, bass.ds(i * DK, DK)], ACT.Copy)
        Act(M[:, 0, :, :], Y[:, bass.ds(i * 2, 2), :], ACT.Copy)
        Act(M[:, 1, :, :], Y[:, bass.ds(i * 2 + 8, 2), :], ACT.Copy).then_inc(sem("head_staged"), 1)
        act.wait_ge(sem("g_logits"), i + 1)
        Act(tmp, ps[:, 4:8, :], ACT.Abs)
        high_to(5)
        nc.scalar.drain()
        Act(tmp, tmp, ACT.Exp, scale=-1.0)
        high_to(6)
        nc.scalar.drain()
        Act(tmp, tmp, ACT.Ln, bias=1.0).then_inc(sem("g_log"), 1)
        high_to(9)
        act.wait_ge(sem("totals"), i + 1)
        Act(B.small[:, 16:32], tot, ACT.Exp, scale=1.0 / TAU).then_inc(sem("block_decays"), 1)
        for n in range(2 * len(LEVELS)):
            h, d = LEVELS[n // 2], n % 2
            act.wait_ge(sem("distances"), i * 14 + n + 1)
            seg = M[:, d, :, :].rearrange("p a (s t) -> p (a s) t", t=2 * h)
            Act(seg[:, :, 0:h], seg[:, :, 0:h], ACT.Exp, scale=-1.0 / TAU)
            Act(seg[:, :, h:2 * h], seg[:, :, h:2 * h], ACT.Exp, scale=1.0 / TAU).then_inc(sem("decays"), 1)
            high_to(level_tiles(n - 2) + RING)
            if n and level_tiles(n - 3) < KT <= level_tiles(n - 2):
                leave(0)
        act.wait_ge(sem("block_distances"), i + 1)
        Act(M[:, 0, :, :], G, ACT.Exp, scale=1.0 / TAU)
        high_to(28)
        Act(M[:, 1, :, :], M[:, 1, :, :], ACT.Exp, scale=-1.0 / TAU)
        high_to(29)
        Act(tmp[:, 0:2, :], tmp[:, 0:2, :], ACT.Exp, scale=-1.0 / TAU)
        Act(tmp[:, 2:4, :], E, ACT.Exp, scale=1.0 / TAU).then_inc(sem("cross_decays"), 1)
        high_to(32)
        act.wait_ge(sem("cross_scores"), i + 1)
        for j in range(NT):
            if j:
                last = Act(am[:, j, 0:P * j], ps[:, 4 + j, 0:P * j], ACT.Copy)
            if j < NT - 1:
                last = Act(am[:, j, P * (j + 1):S], ps[:, 4 + j, P * (j + 1):S], ACT.Copy)
        last.then_inc(sem("cross_taken"), 1)
        high_to(34)
        act.wait_ge(sem("o_mm"), i + 1)
        Act(tmp[:, 0:2, :], ps[:, 4:6, :], ACT.Square).then_inc(sem("o_squared"), 1)
        high_to(35)
        leave(1)
        act.wait_ge(sem("o_variance"), i + 1)
        Act(at(AT_R, 1, S), at(AT_R, 1, S), ACT.Ln)
        nc.scalar.drain()
        Act(at(AT_R, 1, S), at(AT_R, 1, S), ACT.Exp, scale=-0.5).then_inc(sem("o_deviation"), 1)
        high_to(36)
    nc.scalar.drain().then_inc(B.bank_free[(FIRST["egb"] - 1) % 2], GLA_HEADS)
    nc.scalar.drain().then_inc(B.bank_free[FIRST["egb"] % 2], GLA_HEADS)


def tensor_program(B, pe):
    nc, sem, at, ps, Y = B.nc, B.sem, B.at, B.ps, B.Y
    f32 = mybir.dt.float32
    mm = nc.tensor.matmul

    def turn(out, src, rows=P):
        return nc.tensor.transpose(out, src, B.ident[0:rows, 0:rows])

    def reduce_parts(parity, out):
        for v in range(2):
            for j in range(4):
                last = mm(out[:, 4 * v + j:4 * v + j + 1], B.acc[:, parity, v, j * P:(j + 1) * P], B.ones[:, 0:1],
                          start=True, stop=True)
        return last

    def tile_products(g, n, slot, t, taken=None, left=None):
        bank = 4 * (n % 2)
        k = g["tile0"] + t
        first, last_t = t == 0, t == g["kt"] - 1
        hi, lo = B.w_hi[:, slot, :], B.w_lo[:, slot, :]
        if g["mode"] == "T":
            w, tok = g["width"], g["tok"]
            for j in range((w + P - 1) // P):
                m = min(P, w - j * P)
                if left:
                    left(j)
                if j == 3 and taken is not None:
                    pe.wait_ge(sem("part_taken"), taken)
                dst = ps[0:m, bank + j, 0:tok]
                cols = slice(j * P, j * P + m)
                mm(dst, hi[:, cols], B.op_hi[:, k, 0:tok], start=first, stop=False)
                mm(dst, hi[:, cols], B.op_lo[:, k, 0:tok], start=False, stop=False)
                last = mm(dst, lo[:, cols], B.op_hi[:, k, 0:tok], start=False, stop=last_t)
        else:
            for j in range(g["tok"] // P):
                if j == 3 and taken is not None:
                    pe.wait_ge(sem("part_taken"), taken)
                dst = ps[:, bank + j, :]
                rows = slice(j * P, j * P + P)
                mm(dst, B.op_hi[:, k, rows], hi, start=first, stop=False)
                mm(dst, B.op_lo[:, k, rows], hi, start=False, stop=False)
                last = mm(dst, B.op_hi[:, k, rows], lo, start=False, stop=last_t)
        return last

    def group(n, r=None):
        g = GROUPS[n]
        c = lambda v, per: v if r is None else r * per + v
        if n >= 2:
            pe.wait_ge(B.bank_free[n % 2], c(n // 2, 1))
        pending = n >= 2 and GROUPS[n - 2]["part"] is not None
        taken = c(ordinal(n - 1), 2) if pending else None
        hook = n >= 1 and GROUPS[n - 1]["part"] is not None
        for t in range(g["kt"]):
            pe.wait_ge(sem("lo_done"), c(g["kc"] + t + 1, 32))
            pe.wait_ge(sem("op_tile"), KT * g["operand"] + g["tile0"] + t + 1)
            tile_products(g, n, (g["kc"] + t) % RING, t, taken if t == 0 else None).then_inc(sem("w_used"), 1)
            if hook and t == 5:
                o = ordinal(n)
                pe.wait_ge(sem("part_tile"), c(KT * o, 2 * KT))
                pe.wait_ge(B.bank_free[(n - 1) % 2], c((n - 1) // 2 + 1, 1))
                reduce_parts((o - 1) % 2, ps[:, 4 * ((n + 1) % 2) + 3, :]).then_inc(sem("part_summed"), 1)

    def norm_sums(m):
        if m >= 2:
            name = ("wo2", "wo3")[m - 2]
            for n in (FIRST[name] + 2, FIRST[name] + 3):
                pe.wait_ge(B.bank_free[n % 2], n // 2 + 1)
            pe.wait_ge(sem("tiles_added"), m - 1)
            for t in range(2):
                last = mm(ps[:, 3, :], B.ones, at(AT_SUM, 2, S)[:, t, :], start=t == 0, stop=t == 1)
            last.then_inc(sem("summed"), 1)

    def norm_squares(m):
        sqr = at(AT_SQ, 2, 4, S)
        for j in range(4):
            pe.wait_ge(sem("squared"), 4 * m + j + 1)
            for t in range(4):
                last = mm(ps[:, 7, :], B.ones, sqr[:, j % 2, t, :], start=j + t == 0, stop=j + t == 6)
            last.then_inc(sem("squares_summed"), 1)

    rows = Y[:, 15, :].rearrange("p (r c) -> p r c", c=P)
    pe.wait_ge(sem("rows_in"), 16 * N_ROW_LOADS)
    pe.wait_ge(sem("const_in"), 16)
    for r in range((NVEC + P - 1) // P):
        k = min(P, NVEC - r * P)
        last = turn(ps[:, 0, r * P:r * P + k], rows[0:k, r, :], k)
    last.then_inc(sem("columns"), 1)
    pe.wait_ge(sem("x_in"), 16)
    x_tok = at(AT_X_TOK, NT, D)
    for t in range(KT):
        if t >= 4:
            pe.wait_ge(sem("x_turned"), t - 3)
        for j in range(NT):
            last = turn(ps[:, 1 + t % 4, j * P:(j + 1) * P], x_tok[:, j, t * P:(t + 1) * P])
        last.then_inc(sem("turned"), 1)
    pe.wait_ge(sem("ws_in"), 16)
    for h in range(HEADS_A):
        last = turn(ps[:, 5 + h // 4, h % 4 * P:(h % 4 + 1) * P], at(AT_WS_RAW, HEADS_A, P)[:, h, :])
    last.then_inc(sem("ws_turned"), 1)
    norm_squares(0)
    for p in range(4):
        pe.wait_ge(sem("acc_step"), 34 * (p + 1))
        reduce_parts(p % 2, ps[:, 0, 8 * p:8 * p + 8]).then_inc(sem("start_summed"), 1)

    def run(first, pairs):
        beside = lambda n: [GROUPS[k]["part"] is not None for k in (n - 2, n - 1, n)]
        assert all(beside(first + 2 * k) == beside(first) for k in range(pairs))
        if pairs == 1:
            group(first)
            group(first + 1)
        else:
            with pe.Fori(0, pairs) as r:
                group(first, r)
                group(first + 1, r)

    F = FIRST
    run(F["va"], 1)
    group(F["f"])
    run(F["q"], 2)
    run(F["v"], 1)
    mixer_tensor(B, pe)
    attention_tensor(B, pe, 0, tile_products)
    attention_tensor(B, pe, 1, tile_products)
    run(F["gb"], 1)
    run(F["wo1"], 1)
    run(F["wo1"] + 2, 1)
    pe.wait_ge(sem("ctx_in"), 16)
    c_tok = at(AT_CTOK, NTC, D)
    for n in range(F["cr"] - 2, F["cr"]):
        pe.wait_ge(B.bank_free[n % 2], n // 2 + 1)
    for t in range(KT):
        if t >= 4:
            pe.wait_ge(sem("modulated"), modulated(2) + t - 3)
        for j in range(NTC):
            last = turn(ps[:, t % 4, j * P:(j + 1) * P], c_tok[:, j, t * P:(t + 1) * P])
        last.then_inc(sem("ctx_turned"), 1)
    pe.wait_ge(sem("modulated"), modulated(2) + KT)
    group(F["cr"])
    norm_squares(1)
    run(F["ck"], 1)
    run(F["cv"], 1)
    context_tensor(B, pe)
    group(F["r"])
    run(F["ek"], 1)
    run(F["eq"], 1)
    run(F["ev"], 1)
    gla_tensor(B, pe, tile_products)
    run(F["egb"], 1)
    run(F["wo2"], 1)
    run(F["wo2"] + 2, 1)
    norm_sums(2)
    norm_squares(2)
    run(F["xp"], 1)
    run(F["xp"] + 2, 1)
    run(F["gt"], 1)
    run(F["gt"] + 2, 1)
    for i in range(4):
        group(F["pool"] + i)
    run(F["wo3"], 2)
    norm_sums(3)
    norm_squares(3)
    for t in range(NT):
        for j in range(4):
            k = 4 * t + j
            pe.wait_ge(sem("scaled"), 4 * 3 + j + 1)
            if k >= 4:
                pe.wait_ge(sem("out_taken"), k - 3)
            for q in range(4):
                last = turn(ps[:, k % 4, q * P:(q + 1) * P], Y[:, 4 * j + q, t * P:(t + 1) * P])
            last.then_inc(sem("out_turned"), 1)


def mixer_tensor(B, pe):
    nc, sem, at, ps, Y = B.nc, B.sem, B.at, B.ps, B.Y
    mm = nc.tensor.matmul
    for n in (FIRST["v"], FIRST["v"] + 1):
        pe.wait_ge(B.bank_free[n % 2], n // 2 + 1)
    pe.wait_ge(sem("part_taken"), ordinal(FIRST["v"] + 1))
    pe.wait_ge(sem("value_normed"), 2)
    pe.wait_ge(sem("ws_masked"), 1)
    for h in range(HEADS_A):
        for b in range(NT):
            last = mm(ps[:, h, b * P:(b + 1) * P], at(AT_VA, NT, 1024)[:, b, h * P:(h + 1) * P],
                      at(AT_WST, HEADS_A, P)[:, h, :], start=True, stop=True)
        last.then_inc(sem("mixing"), 1)
    pe.wait_ge(sem("mixed"), HEADS_A)
    pe.sem_inc(sem("scores"), 1)
    pe.sem_inc(sem("pv"), 2)
    pe.sem_inc(sem("p_turned"), 2)
    pe.sem_inc(sem("o_turned"), 2)


def attention_tensor(B, pe, k, tile_products):
    nc, sem, at, ps = B.nc, B.sem, B.at, B.ps
    mm = nc.tensor.matmul
    queries, keys, v = at(AT_QST, 2, S), at(AT_KST, 2, S), at(AT_V, NT, 1024)
    logit, p_t, o_tok = at(AT_LOGIT, 2, S), at(AT_PT, 2, S), at(AT_OTOK, 2, NT, P)
    g = GROUPS[attention_first(k)]
    with pe.Fori(0, 2) as i:

        def tile(t):
            pe.wait_ge(sem("lo_done"), i * 16 + (g["kc"] + t + 1))

            def left(bank):
                pe.wait_ge(sem("gate_left"), i * 4 + (8 * k + bank + 1))
            tile_products(g, 0, (g["kc"] + t) % RING, t, left=left if t == 0 else None).then_inc(sem("w_used"), 1)

        def turn_outputs(q):
            pe.wait_ge(sem("o_scaled"), i * 16 + (32 * k + 8 * q + 10))
            for b in range(NT):
                last = nc.tensor.transpose(ps[:, 6, b * P:(b + 1) * P], o_tok[:, q, b, :], B.ident)
            last.then_inc(sem("o_turned"), 1)

        pe.wait_ge(sem("staged"), i * 2 + (4 * k + 2))
        for s in range(18):
            if s < 16:
                pair, half, b = s // 8, s // 4 % 2, s % 4
                rows = slice(DH_B * half, DH_B * (half + 1))
                pe.wait_ge(sem("score_slots"), i * 16 + (32 * k + s + 1))
                mm(ps[:, 4 + s % 2, 0:P * (b + 1)], queries[rows, pair, b * P:(b + 1) * P],
                   keys[rows, pair, 0:P * (b + 1)], start=True, stop=True).then_inc(sem("scores"), 1)
            if s >= 2:
                u = s - 2
                pe.wait_ge(sem("p_taken"), i * 16 + (32 * k + u + 2))
                pe.wait_ge(sem("o_scaled"), i * 16 + (32 * k + u + 2))
                for c in range(u % 4 + 1):
                    last = mm(ps[:, 7, DH_B * (u % 2):DH_B * (u % 2 + 1)], p_t[:, u % 2, c * P:(c + 1) * P],
                              v[:, c, bass.ds(i * 2 * P + (P * (4 * k + u // 8) + DH_B * (u // 4 % 2)), DH_B)],
                              start=c == 0, stop=c == u % 4)
                last.then_inc(sem("pv"), 1)
            if s == 11:
                turn_outputs(0)
                tile(s)
            if 1 <= s < 17:
                u = s - 1
                pe.wait_ge(sem("probs"), i * 16 + (32 * k + u + 1))
                pe.wait_ge(sem("p_taken"), i * 16 + (32 * k + u + 1))
                if s == 11:
                    pe.wait_ge(sem("o_taken"), i * 2 + (4 * k + 1))
                for c in range(u % 4 + 1):
                    last = nc.tensor.transpose(ps[:, 6, c * P:(c + 1) * P], logit[:, u % 2, c * P:(c + 1) * P], B.ident)
                last.then_inc(sem("p_turned"), 1)
            if s < 16 and s != 11:
                tile(s)
        turn_outputs(1)
        pe.wait_ge(sem("o_taken"), i * 2 + (4 * k + 2))


def context_tensor(B, pe):
    nc, sem, at, ps = B.nc, B.sem, B.at, B.ps
    mm = nc.tensor.matmul
    for n in (FIRST["cv"], FIRST["cv"] + 1):
        pe.wait_ge(B.bank_free[n % 2], n // 2 + 1)
    pe.wait_ge(sem("part_taken"), ordinal(FIRST["ck"] + 1))
    pe.wait_ge(sem("ctx_gates_in"), 64)
    pe.wait_ge(sem("normed"), 8)
    r_c, wg = at(AT_RC, SC), at(AT_WGC, 2, 1024)
    for d in range(2):
        for t in range(NTC):
            for c in range(2):
                last = mm(ps[:, 4 * d + 2 * t + c, :], r_c[0:33, t * P:(t + 1) * P], wg[0:33, d, c * GC:(c + 1) * GC],
                          start=True, stop=True)
    last.then_inc(sem("ctx_logits"), 1)
    pe.wait_ge(sem("ctx_gates"), 1)
    la = at(AT_LAC, 8, GC)
    for d in range(2):
        for t in range(NTC):
            for c in range(2):
                bank = 4 * d + 2 * t + c
                tri = (B.tri_gt, B.tri_lt)[d]
                other = t == d
                mm(ps[:, bank, :], tri, la[:, bank, :], start=True, stop=not other)
                last = mm(ps[:, bank, :], B.ones, la[:, 4 * d + 2 * (1 - t) + c, :], start=False, stop=True) if other else last
    nc.tensor.drain().then_inc(sem("ctx_sums"), 1)
    pe.wait_ge(sem("ctx_keys"), 1)
    keys, vc = at(AT_TC, 2, 2, 1024), at(AT_VC, NTC, 1024)
    for h in range(GLA_HEADS):
        for d in range(2):
            for a in range(2):
                for t in range(NTC):
                    last = mm(ps[:, 2 * h + d, a * DK:(a + 1) * DK], keys[:, d, t, h * DK + a * P:h * DK + (a + 1) * P],
                              vc[:, t, h * DK:(h + 1) * DK], start=t == 0, stop=t == 1)
    last.then_inc(sem("ctx_states"), 1)
    pe.wait_ge(sem("states_out"), 1)


def gla_tensor(B, pe, tile_products):
    nc, sem, at, ps = B.nc, B.sem, B.at, B.ps
    mm = nc.tensor.matmul
    M, tmp, G, E = at(AT_M, 2, 2, S), at(TMP, 4, S), at(AT_G, 2, S), at(AT_E, 2, S)
    am, vh, st = at(AT_AM, NT, S), at(AT_VH, NT, DK), at(AT_ST, 4, DK)
    wg, r_t, qb = at(AT_WG, 2, DK), at(AT_RT, S), at(AT_QB, 2, S)
    primed = at(AT_G, 4, 2, P)
    for n in (FIRST["ev"], FIRST["ev"] + 1):
        pe.wait_ge(B.bank_free[n % 2], n // 2 + 1)
    pe.wait_ge(sem("part_taken"), ordinal(FIRST["ev"] + 1))
    kc = GROUPS[FIRST["beside"]]["kc"]
    with pe.Fori(0, GLA_HEADS) as i:
        used = 0

        def tiles(count):
            nonlocal used
            for _ in range(count):
                k, t = divmod(used, KT)
                g = GROUPS[FIRST["beside"] + k]
                pe.wait_ge(sem("lo_done"), i * 32 + (kc + used + 1))

                def left(bank):
                    pe.wait_ge(sem("beside_left"), i * 8 + (4 * k + bank + 1))
                tile_products(g, 0, (kc + used) % RING, t, left=left if t == 0 else None).then_inc(sem("w_used"), 1)
                used += 1

        tiles(T_ENTER)
        pe.wait_ge(sem("head_in"), i * 80 + 80)
        pe.wait_ge(sem("heads_done"), i + 1)
        for d in range(2):
            for a in range(2):
                last = mm(ps[:, 4 + 2 * d + a, :], wg[0:33, d, a * P:(a + 1) * P], r_t[0:33, :], start=True, stop=True)
        last.then_inc(sem("g_logits"), 1)
        tiles(T_LOGIT)
        pe.wait_ge(sem("totals"), i + 1)
        pe.wait_ge(sem("head_staged"), i + 1)
        for b in range(NT):
            for a in range(2):
                last = mm(ps[:, 4, b * P:(b + 1) * P], M[:, 0, a, b * P:(b + 1) * P], M[:, 1, a, b * P:(b + 1) * P],
                          start=a == 0, stop=a == 1)
        last.then_inc(sem("diagonal"), 1)
        tiles(T_DIAGONAL)
        for n in range(2 * len(LEVELS)):
            d = n % 2
            pe.wait_ge(sem("weighted"), i * 14 + n + 1)
            if n >= 3:
                pe.wait_ge(sem("level_taken"), i * 14 + n - 2)
            h = LEVELS[n // 2]

            def queries(block):
                return block.rearrange("p (s t) -> p s t", t=2 * h)[:, :, (1 - d) * h:(2 - d) * h]
            for b in range(NT):
                for a in range(2):
                    x = M[:, d, a, b * P:(b + 1) * P]
                    last = mm(queries(ps[:, 5 + n % 3, b * P:(b + 1) * P]), x, queries(x), start=a == 0, stop=a == 1)
            last.then_inc(sem("level_scores"), 1)
            tiles(T_LEVEL[n])
        tiles(T_CROSS)
        pe.wait_ge(sem("cross_weighted"), i + 1)
        qf, kf, qbk, kb = M[:, 0, :, :], M[:, 1, :, :], tmp[:, 0:2, :], tmp[:, 2:4, :]
        for j in range(NT):
            for b in range(NT):
                if j == b:
                    continue
                for a in range(2):
                    blk = lambda x, y: x[:, a, y * P:(y + 1) * P]
                    if j < b:
                        far_k, far_q = j == 0 and b >= 2, b == 3 and j <= 1
                        key = primed[:, 0, a, :] if far_k else blk(kf, j)
                        query = primed[:, 1, a, :] if far_q else blk(qf, b)
                    else:
                        far_q, far_k = b == 0 and j >= 2, j == 3 and b <= 1
                        query = primed[:, 2, a, :] if far_q else blk(qbk, b)
                        key = primed[:, 3, a, :] if far_k else blk(kb, j)
                    last = mm(ps[:, 4 + j, b * P:(b + 1) * P], key, query, start=a == 0, stop=a == 1)
        last.then_inc(sem("cross_scores"), 1)
        tiles(T_TAKEN)
        pe.wait_ge(sem("cross_taken"), i + 1)
        pe.wait_ge(sem("state_queries"), i + 1)
        for a in range(2):
            cols = slice(a * P, (a + 1) * P)
            for j in range(NT):
                mm(ps[:, 4 + a, :], vh[:, j, cols], am[:, j, :], start=j == 0, stop=False)
            for d in range(2):
                for e in range(2):
                    last = mm(ps[:, 4 + a, :], st[:, 2 * d + e, cols], (E if d == 0 else qb)[:, e, :],
                              start=False, stop=d + e == 2)
        last.then_inc(sem("o_mm"), 1)
        tiles(T_OUT)
        pe.wait_ge(sem("o_squared"), i + 1)
        for a in range(2):
            last = mm(ps[:, 6, :], B.ones, tmp[:, a, :], start=a == 0, stop=a == 1)
        last.then_inc(sem("o_summed"), 1)
    pe.wait_ge(sem("heads_done"), GLA_HEADS + 1)


def vector_program(B, dve):
    nc, sem, at, ps, Y = B.nc, B.sem, B.at, B.ps, B.Y
    ALU, AX = mybir.AluOpType, mybir.AxisListType
    f32 = mybir.dt.float32
    V = nc.vector

    def low_tile(c, width):
        dve.wait_ge(sem("hi_done"), c + 1)
        if c >= RING:
            dve.wait_ge(sem("w_used"), c - RING + 1)
        V.tensor_tensor(B.w_lo[:, c % RING, 0:width], B.w_raw[:, c // 2 % RAW, c % 2, 0:width],
                        B.w_hi[:, c % RING, 0:width].bitcast(f32), ALU.subtract).then_inc(sem("lo_done"), 1)

    def part_tile(n, t, r=0):
        part, o = GROUPS[n]["part"], ordinal(n)
        vectors = [(VEC["c"] if part < 12 else VEC["c2"])] + ([VEC["cc"]] if ctx_part(part) else [])
        dve.wait_ge(B.a_in[t // 2 % 2], r * 32 + 16 * (4 * o + t // 4 + 1))
        if o or t or not isinstance(r, int):
            dve.wait_ge(sem("part_tile"), r * 8 + KT * o + t)
        for v, first in enumerate(vectors):
            col = B.vec[:, first + t:first + t + 1] if isinstance(r, int) else B.vec[:, bass.ds(r * 8 + (first + t), 1)]
            sums = B.acc[:, o % 2, v, :]
            last = V.scalar_tensor_tensor(out=sums, in0=B.a_raw[:, t // 2 % 2, t % 2, :], scalar=col, in1=sums,
                                          op0=ALU.mult, op1=ALU.add)
        last.then_inc(sem("part_tile"), 1)

    def clear_sums(n):
        if GROUPS[n]["part"] is not None:
            V.memset(B.acc[:, ordinal(n) % 2, :, :], 0.0)
            V.drain()

    def step(n, t):
        g = GROUPS[n]
        after = GROUPS[n + 1]["width"] if n + 1 < len(GROUPS) else 0
        if t < g["kt"] - 4:
            low_tile(g["kc"] + 4 + t, g["width"])
        elif after:
            low_tile(g["kc"] + 4 + t, after)
        if g["part"] is not None:
            part_tile(n, t)
        if g["name"] == "egb":
            for j in range(8):
                if CONV_AT[j] == (g["i"], t):
                    conv_tile(j)

    def ahead(n):
        g = GROUPS[n]
        c, k, width, part = g["kc"], g["kt"], g["width"], g["part"]
        after = GROUPS[n + 1]["width"] if n + 1 < len(GROUPS) else 0
        if not early(n):
            clear_sums(n)
        if k == KT and after == width and not early(n) and g["name"] != "egb":
            with dve.Fori(0, 2) as r:
                for t in range(8):
                    x = c + 4 + t
                    dve.wait_ge(sem("hi_done"), r * 8 + (x + 1))
                    dve.wait_ge(sem("w_used"), r * 8 + (x - RING + 1))
                    V.tensor_tensor(B.w_lo[:, x % RING, 0:width], B.w_raw[:, x // 2 % RAW, x % 2, 0:width],
                                    B.w_hi[:, x % RING, 0:width].bitcast(f32), ALU.subtract).then_inc(sem("lo_done"), 1)
                    if part is not None:
                        part_tile(n, t, r)
        else:
            for t in range(early(n), k):
                step(n, t)
        if n and GROUPS[n - 1]["part"] is not None:
            take_part(GROUPS[n - 1]["part"], ps[:, 4 * ((n + 1) % 2) + 3, :], ordinal(n))

    def conv_tile(j):
        dve.wait_ge(sem(f"conv_in_{j}"), 16)
        dve.wait_ge(sem("conv_gate"), j + 1)
        x = at(AT_CONV, CONV_SLOTS, 4, S)[:, j % CONV_SLOTS, :, :]
        u, v = (x[:, k, :].rearrange("p (r w) -> p r w", w=GRID_W) for k in (1, 2))
        tap = [B.vec[:, VEC["conv"] + 8 * k + j:VEC["conv"] + 8 * k + j + 1] for k in range(3)]
        V.tensor_tensor(x[:, 1, :], x[:, 1, :], x[:, 2, :], ALU.mult)
        V.tensor_tensor(x[:, 0, :], x[:, 0, :], x[:, 3, :], ALU.mult)
        V.drain()
        V.tensor_scalar(v, u, tap[1], None, ALU.mult)
        V.drain()
        V.scalar_tensor_tensor(out=v[:, :, 1:], in0=u[:, :, :-1], scalar=tap[0], in1=v[:, :, 1:],
                               op0=ALU.mult, op1=ALU.add)
        V.drain()
        V.scalar_tensor_tensor(out=v[:, :, :-1], in0=u[:, :, 1:], scalar=tap[2], in1=v[:, :, :-1],
                               op0=ALU.mult, op1=ALU.add)
        V.drain()
        V.tensor_tensor(Y[:, 8 + j, :], x[:, 2, :], x[:, 0, :], ALU.mult).then_inc(sem("conv_done"), 1)

    def take_part(part, bank, count):
        dve.wait_ge(sem("part_summed"), count)
        put_part(part, bank[:, 0:4], 4 * part)
        if ctx_part(part):
            put_part(part, bank[:, 4:8], 144 + 4 * (part - 12))
        V.drain().then_inc(sem("part_taken"), 1)

    def put_part(part, sums, col):
        bias = B.vec[:, VEC["b_ada"] + 4 * part:VEC["b_ada"] + 4 * part + 4]
        V.tensor_tensor(B.mod[:, col:col + 4], sums, bias, ALU.add)
        if part % 12 // 4 == 1:
            V.drain()
            V.tensor_scalar(B.mod[:, col:col + 4], B.mod[:, col:col + 4], 1.0, None, ALU.add)

    def split_lo(t, src, tok=S):
        V.tensor_tensor(B.op_lo[:, t, 0:tok], src, B.op_hi[:, t, 0:tok].bitcast(f32), ALU.subtract)\
            .then_inc(sem("op_tile"), 1)

    def last_use(operand):
        return max(x["kc"] + x["kt"] for x in GROUPS if x["operand"] == operand)

    def modulate(operand, shift, scale, src, tok=S, ready=None):
        if operand:
            dve.wait_ge(sem("w_used"), last_use(operand - 1))
        buf = at(TMP, 4, S)
        base = modulated(operand)
        V.drain()
        n = first_use(operand)
        clear_sums(n)
        for t in range(KT + 2):
            if t < KT:
                if t >= 4:
                    dve.wait_ge(sem("op_tile"), KT * operand + t - 3)
                if ready:
                    ready(t)
                V.tensor_scalar(buf[:, t % 4, 0:tok], src(t), B.mod[:, scale + t:scale + t + 1],
                                B.mod[:, shift + t:shift + t + 1], ALU.mult, ALU.add).then_inc(sem("modulated"), 1)
            if t >= 2:
                u = t - 2
                dve.wait_ge(sem("op_high"), KT * operand + u + 1)
                dve.wait_ge(sem("modulated"), base + u + 1)
                split_lo(u, buf[:, u % 4, 0:tok], tok)
                if 4 <= u < 4 + early(n):
                    step(n, u - 4)

    def split_y(operand):
        V.drain().then_inc(sem("mixer_out" if operand != 6 else "pooled_all"), 1)
        dve.wait_ge(sem("w_used"), last_use(operand - 1))
        n = first_use(operand)
        clear_sums(n)
        for t in range(KT):
            dve.wait_ge(sem("op_high"), KT * operand + t + 1)
            split_lo(t, Y[:, t, :])
            if 4 <= t < 4 + early(n):
                step(n, t - 4)

    def norm(m, chunks=4):
        eps = EPS if m < 2 else LN_EPS
        if m >= 2:
            dve.wait_ge(sem("summed"), m - 1)
            for j in range(4):
                y = Y[:, 4 * j:4 * j + 4, :]
                V.scalar_tensor_tensor(out=y, in0=ps[:, 3:4, :].to_broadcast([P, 4, S]), scalar=-1.0 / D, in1=y,
                                       op0=ALU.mult, op1=ALU.add).then_inc(sem("centred"), 1)
        dve.wait_ge(sem("squares_summed"), 4 * m + 4)
        r = at(AT_RSTD, 1, S)
        V.tensor_scalar(r[:, 0, :], ps[:, 7, :], 1.0 / D, eps, ALU.mult, ALU.add).then_inc(sem("variance"), 1)
        dve.wait_ge(sem("deviation"), m + 1)
        if m == 0:
            dve.wait_ge(sem("spilled"), 16)
        for j in range(chunks):
            norm_chunk(j)

    def norm_chunk(j):
        y = Y[:, 4 * j:4 * j + 4, :]
        V.tensor_tensor(y, y, at(AT_RSTD, 1, S).to_broadcast([P, 4, S]), ALU.mult).then_inc(sem("normed"), 1)

    V.memset(B.small[:, :], 0.0)
    ring = at(AT_START, 8, 1024)
    for pair in range(4):
        base = 34 * pair
        if pair >= 2:
            dve.wait_ge(sem("start_summed"), pair - 1)
        for v in range(2):
            V.memset(B.acc[:, pair % 2, v, :], 0.0).then_inc(sem("acc_step"), 1)
        if pair == 0:
            dve.wait_ge(sem("vec_ready"), 1)
        with dve.Fori(0, 2) as r:
            for s in range(8):
                dve.wait_ge(B.start_in[s], r * 16 + 16 * (2 * pair + 1))
                for v in range(2):
                    dve.wait_ge(sem("acc_step"), r * 16 + (base + 2 * s + v + 1))
                    sums = B.acc[:, pair % 2, v, :]
                    V.scalar_tensor_tensor(out=sums, in0=ring[:, s, v * GC:(v + 1) * GC],
                                           scalar=B.vec[:, bass.ds(r * 8 + (VEC["c"] + s), 1)], in1=sums,
                                           op0=ALU.mult, op1=ALU.add).then_inc(sem("acc_step"), 1)
    dve.wait_ge(sem("masks_in"), 16)
    V.tensor_copy(B.masks[:, :, :].rearrange("p l c -> p (l c)"),
                  B.a_raw[:, :, :, :].rearrange("p a b c -> p (a b c)")[:, 0:2 * len(LEVELS) * P])\
        .then_inc(sem("masks_made"), 1)
    dve.wait_ge(sem("start_summed"), 4)
    V.tensor_tensor(B.mod[:, 0:32], ps[:, 0, 0:32], B.vec[:, VEC["b_ada"]:VEC["b_ada"] + 32], ALU.add)
    V.drain()
    V.tensor_scalar(B.mod[:, 16:32], B.mod[:, 16:32], 1.0, None, ALU.add)
    dve.wait_ge(sem("ws_turned"), 1)
    V.tensor_tensor(at(AT_WST, HEADS_A, P), ps[:, 5:7, :].rearrange("p b (h t) -> p (b h) t", t=P),
                    B.tri_le.unsqueeze(1).to_broadcast([P, HEADS_A, P]), ALU.mult).then_inc(sem("ws_masked"), 1)
    norm(0, 1)

    def scaled(m):
        def ready(t):
            if t % 4 == 0:
                if m != 1 and t < 12:
                    norm_chunk(t // 4 + 1)
                dve.wait_ge(sem("scaled"), 4 * m + t // 4 + 1)
        return ready

    y_tile = lambda t: Y[:, t, :]
    for c in range(4):
        low_tile(c, GC)
    modulate(0, 0, 16, y_tile, ready=scaled(0))

    for n, g in enumerate(GROUPS):
        name, i = g["name"], g["i"]
        if name == "beside":
            if i == 0:
                gla_vector(B, dve)
            continue
        if name in ("ua", "ga"):
            if i == 0:
                attention_vector(B, dve, name == "ga")
            continue
        ahead(n)
        bank = 4 * (n % 2)
        free = B.bank_free[n % 2]
        banks = ps[:, bank:bank + 4, :]
        if name in DVE_EVAC:
            dve.wait_ge(sem("w_used"), g["kc"] + g["kt"])
            V.drain()
        va = at(AT_VA, NT, 1024)
        if name == "f":
            for k in range(FIRST["va"], FIRST["va"] + 2):
                dve.wait_ge(B.bank_free[k % 2], k // 2 + 1)
            stats = B.small[:, 16:16 + 48].rearrange("p (a s) -> p a s", s=12)
            for b in range(NT):
                for h in range(2):
                    V.bn_stats(stats[:, b, 6 * h:6 * h + 6], va[:, b, h * GC:(h + 1) * GC])
            V.drain()
            for b in range(NT):
                V.bn_aggr(B.small[:, 64 + 2 * b:66 + 2 * b], stats[:, b, :])
            V.drain()
            mv = B.small[:, 64:72].rearrange("p (a b) -> p a b", b=2)
            V.tensor_scalar(B.small[:, 0:4], mv[:, :, 1], EPS, None, ALU.add).then_inc(sem("value_variance"), 1)
        if name == "q" and i == 0:
            dve.wait_ge(sem("value_deviation"), 1)
            V.reciprocal(B.small[:, 4:8], B.small[:, 0:4])
            V.drain()
            for b in range(NT):
                V.tensor_scalar(va[:, b, :], va[:, b, :], B.small[:, 64 + 2 * b:65 + 2 * b], B.small[:, 4 + b:5 + b],
                                ALU.subtract, ALU.mult)
            V.drain()
        if name in ("q", "k") and (name, i) != ("q", 0):
            dve.wait_ge(sem("ln_rows_in"), 32)
            row = at(TMP, 2, 1024)[:, (name == "k"):(name == "k") + 1, :]
            halves = (0, 2) if name == "q" else (2 * i,)
            for b in halves:
                last = V.tensor_tensor(va[:, b:b + 2, :], va[:, b:b + 2, :], row.to_broadcast([P, 2, 1024]),
                                       ALU.mult if name == "q" else ALU.add)
            if name == "k":
                last.then_inc(sem("value_normed"), 1)
            V.drain()
        if name == "f":
            dve.wait_ge(sem("f_log"), 1)
            f = B.arena[96:112, AT_F:AT_F + S]
            V.scalar_tensor_tensor(out=f, in0=f, scalar=0.0, in1=B.arena[96:112, AT_FQ:AT_FQ + S],
                                   op0=ALU.min, op1=ALU.subtract)
            V.drain()
            V.tensor_tensor_scan(B.arena[96:112, AT_FQ:AT_FQ + S], f, f, 0.0, ALU.add, ALU.min)
            V.drain()
            V.tensor_scalar(f, B.arena[96:112, AT_FQ:AT_FQ + S], -1.0, None, ALU.mult).then_inc(sem("f_summed"), 1)
        if name == "v" and i == 1:
            dve.wait_ge(sem("bs_in"), 16)
            for h in range(HEADS_A):
                dve.wait_ge(sem("mixing"), h + 1)
                V.tensor_tensor(Y[:, h, :].rearrange("p (b t) -> p b t", t=P),
                                ps[:, h, :].rearrange("p (b t) -> p b t", t=P),
                                at(AT_BS, HEADS_A, P)[:, h:h + 1, :].to_broadcast([P, NT, P]), ALU.add)\
                    .then_inc(sem("mixed"), 1)
            V.drain().then_inc(sem("logits"), 8)
            V.drain().then_inc(sem("tmp_free"), 1)
        if name in TMP_USERS:
            dve.wait_ge(sem("tmp_full"), tmp_uses(n) + 1)
            if name == "gb" and i == 0:
                dve.wait_ge(sem("o_taken"), HEADS_B // 2)
            t = 4 * i + (8 if name == "gb" else 0)
            V.drain()
            V.tensor_tensor(Y[:, t:t + 4, :], Y[:, t:t + 4, :], at(TMP, 4, S), ALU.mult).then_inc(sem("tmp_free"), 1)
            if name == "gb" and i == 1:
                split_y(1)
            if name == "egb" and i == 1:
                split_y(4)
        if name in ("wo1", "wo2", "wo3"):
            k = ("wo1", "wo2", "wo3").index(name)
            dve.wait_ge(sem("residual_in"), 16 * (4 * k + i + 1))
            gate = 48 * k + 32
            x = at(AT_XRES, 4, S)
            if k:
                V.tensor_scalar(x, x, ALPHA, None, ALU.mult)
                V.drain()
            for t in range(4):
                f = 4 * i + t
                last = V.scalar_tensor_tensor(out=Y[:, f, :], in0=ps[:, bank + t, :],
                                              scalar=B.mod[:, gate + f:gate + f + 1], in1=x[:, t, :],
                                              op0=ALU.mult, op1=ALU.add)
            last.then_inc(free, 1)
            if k:
                V.drain()
                pair = at(AT_SUM, 2, S)
                if i == 0:
                    V.tensor_tensor(pair, Y[:, 0:2, :], Y[:, 2:4, :], ALU.add)
                else:
                    for f in (4 * i, 4 * i + 2):
                        V.tensor_tensor(pair, pair, Y[:, f:f + 2, :], ALU.add)
                        V.drain()
                if i == 3:
                    V.drain().then_inc(sem("tiles_added"), 1)
            if name == "wo1" and i == 3:
                def turned(t):
                    dve.wait_ge(sem("ctx_turned"), t + 1)
                modulate(2, 144, 160, lambda t: ps[:, t % 4, 0:SC], SC, ready=turned)
            if name == "wo2" and i == 3:
                norm(2, 1)
                modulate(5, 96, 112, y_tile, ready=scaled(2))
            if name == "wo3" and i == 3:
                norm(3)
        if name == "cr":
            norm(1)
        if name == "cv" and i == 1:
            context_vector(B, dve)
            modulate(3, 48, 64, y_tile, ready=scaled(1))
        if name == "xp":
            dve.wait_ge(sem("spilled"), 48)
            V.drain()
            pool_vector(B, dve, i, banks, free)
        if name == "gt" and i == 3:
            split_y(6)
        if name == "pool":
            if i == 0:
                m = FIRST["gt"] + 3
                for k in (m - 1, m):
                    dve.wait_ge(B.bank_free[k % 2], k // 2 + 1)
            for t in range(4):
                f = 4 * i + t
                last = V.scalar_tensor_tensor(out=Y[:, f, :], in0=ps[:, bank + t, :],
                                              scalar=B.vec[:, VEC["pool_s"] + f:VEC["pool_s"] + f + 1],
                                              in1=at(AT_GATE, KT, S)[:, f, :], op0=ALU.mult, op1=ALU.mult)
            last.then_inc(free, 1)
            if i == 3:
                split_y(7)


def attention_vector(B, dve, k):
    nc, sem, at, ps, Y = B.nc, B.sem, B.at, B.ps, B.Y
    ALU, AX = mybir.AluOpType, mybir.AxisListType
    V = nc.vector
    logit, neg_f, f_col, o_tok = at(AT_LOGIT, 2, S), at(AT_NEGF, 2, S), at(AT_FQ, NT, HEADS_B), at(AT_OTOK, 2, NT, P)
    kc = GROUPS[attention_first(k)]["kc"]
    if not k:
        dve.wait_ge(sem("f_cols_in"), 64)
        dve.sem_inc(sem("score_slots"), 2)
        dve.sem_inc(sem("o_scaled"), 2)
    with dve.Fori(0, 2) as i:
        made = 4

        def low_to(tiles):
            nonlocal made
            while made < tiles:
                c = kc + made
                dve.wait_ge(sem("hi_done"), i * 16 + (c + 1))
                dve.wait_ge(sem("w_used"), i * 16 + (c - RING + 1))
                V.tensor_tensor(B.w_lo[:, c % RING, :], B.w_raw[:, c // 2 % RAW, c % 2, :],
                                B.w_hi[:, c % RING, :].bitcast(mybir.dt.float32), ALU.subtract)\
                    .then_inc(sem("lo_done"), 1)
                made += 1

        for u in range(18):
            if u < 16:
                h, b = u // 4, u % 4
                w = P * (b + 1)
                if b == 0:
                    dve.wait_ge(B.sem(f"f_row_in_{h % 2}"), i * 32 + (64 * k + 16 * (h // 2 + 1)))
                dve.wait_ge(sem("scores"), i * 16 + (32 * k + u + 2))
                dve.wait_ge(sem("p_turned"), i * 16 + (32 * k + u + 1))
                L = logit[:, u % 2, 0:w]
                V.scalar_tensor_tensor(out=L, in0=neg_f[:, h % 2, 0:w],
                                       scalar=f_col[:, b, bass.ds(i * 4 + (8 * k + h), 1)],
                                       in1=ps[:, 4 + u % 2, 0:w], op0=ALU.subtract, op1=ALU.add)\
                    .then_inc(sem("score_slots"), 1)
                V.drain()
                diag = logit[:, u % 2, w - P:w]
                V.tensor_tensor(diag, diag, B.causal, ALU.add)
                V.drain()
                V.tensor_reduce(B.small[:, 8 + u % 2:9 + u % 2], L, AX.X, ALU.max, negate=True)\
                    .then_inc(sem("logits"), 1)
            if u >= 2:
                o = u - 2
                dve.wait_ge(sem("probs"), i * 16 + (32 * k + o + 1))
                V.reciprocal(B.small[:, 32 + o:33 + o], B.small[:, 16 + o:17 + o])
                V.drain()
                dve.wait_ge(sem("pv"), i * 16 + (32 * k + o + 3))
                if o % 8 == 0:
                    dve.wait_ge(sem("o_turned"), i * 2 + (4 * k + o // 8 + 1))
                V.tensor_scalar(o_tok[:, o // 8, o % 4, DH_B * (o // 4 % 2):DH_B * (o // 4 % 2 + 1)],
                                ps[:, 7, DH_B * (o % 2):DH_B * (o % 2 + 1)],
                                B.small[:, 32 + o:33 + o], None, ALU.mult).then_inc(sem("o_scaled"), 1)
            low_to(u + 3)
        dve.wait_ge(sem("tmp_full"), i + (2 * k + 1))
        dve.sem_inc(sem("vector_passed"), 1)
        V.drain()
        V.tensor_tensor(Y[:, bass.ds(i * 4, 4), :], Y[:, bass.ds(i * 4, 4), :], at(TMP, 4, S), ALU.mult)
        V.drain().then_inc(sem("tmp_free"), 1)


def context_vector(B, dve):
    nc, sem, at, ps = B.nc, B.sem, B.at, B.ps
    ALU = mybir.AluOpType
    V = nc.vector
    dve.wait_ge(sem("ctx_log"), 1)
    tc, la, kc = at(AT_TC, 8, GC), at(AT_LAC, 8, GC), at(AT_KC, NTC, 1024)
    for b in range(0, 8, 4):
        V.scalar_tensor_tensor(out=la[:, b:b + 4, :], in0=ps[:, b:b + 4, :], scalar=0.0, in1=tc[:, b:b + 4, :],
                               op0=ALU.min, op1=ALU.subtract)
    V.drain().then_inc(sem("ctx_gates"), 1)
    dve.wait_ge(sem("ctx_decays"), 1)
    for n in (FIRST["ck"], FIRST["ck"] + 1):
        dve.wait_ge(B.bank_free[n % 2], n // 2 + 1)
    kv = at(AT_TC, 2, 2 * 1024)
    for d in range(2):
        V.tensor_tensor(kv[:, d, :], kv[:, d, :], kc.rearrange("p a b -> p (a b)"), ALU.mult)
    V.drain().then_inc(sem("ctx_keys"), 1)


def gla_vector(B, dve):
    nc, sem, at, ps, Y = B.nc, B.sem, B.at, B.ps, B.Y
    ALU = mybir.AluOpType
    V = nc.vector
    M, tmp, G, E = at(AT_M, 2, 2, S), at(TMP, 4, S), at(AT_G, 2, S), at(AT_E, 2, S)
    am = at(AT_AM, NT * NT, P)
    am_diag = am[:, 0:NT * NT:NT + 1, :]
    tot = B.small[:, 0:16]
    dec = B.small[:, 16:32].rearrange("p (d a b) -> p d a b", d=2, a=2)
    cum = B.small[:, 32:48].rearrange("p (d a b) -> p d a b", d=2, a=2)
    t8 = lambda x: x.rearrange("p a (b t) -> p (a b) t", t=P)
    kc = GROUPS[FIRST["beside"]]["kc"]
    dve.sem_inc(sem("heads_done"), 1)
    with dve.Fori(0, GLA_HEADS) as i:
        made = 4

        def low_to(tiles):
            nonlocal made
            while made < tiles:
                c = kc + made
                dve.wait_ge(sem("hi_done"), i * 32 + (c + 1))
                dve.wait_ge(sem("w_used"), i * 32 + (c - RING + 1))
                V.tensor_tensor(B.w_lo[:, c % RING, :], B.w_raw[:, c // 2 % RAW, c % 2, :],
                                B.w_hi[:, c % RING, :].bitcast(mybir.dt.float32), ALU.subtract)\
                    .then_inc(sem("lo_done"), 1)
                made += 1

        low_to(5)
        kh, qh = Y[:, bass.ds(i * 2, 2), :], Y[:, bass.ds(i * 2 + 8, 2), :]
        dve.wait_ge(sem("g_log"), i + 1)
        V.scalar_tensor_tensor(out=tmp, in0=ps[:, 4:8, :], scalar=0.0, in1=tmp, op0=ALU.min, op1=ALU.subtract)
        low_to(6)
        V.drain()
        for a in range(2):
            V.tensor_tensor_scan(G[:, a, :], B.restart, tmp[:, a, :], 0.0, ALU.mult, ALU.add)
            V.tensor_tensor_scan(E[:, a, :], B.restart, tmp[:, 2 + a, :], 0.0, ALU.mult, ALU.add)
        V.drain()
        V.tensor_copy(tot[:, 0:8].unsqueeze(2), t8(G)[:, :, P - 1:P])
        V.tensor_copy(tot[:, 8:16].unsqueeze(2), t8(E)[:, :, P - 1:P]).then_inc(sem("totals"), 1)
        V.drain()
        low_to(9)
        V.tensor_tensor(E, E, tmp[:, 2:4, :], ALU.subtract)
        dve.wait_ge(sem("diagonal"), i + 1)
        V.tensor_tensor(am_diag, ps[:, 4, :].rearrange("p (b t) -> p b t", t=P),
                        B.eye2.unsqueeze(1).to_broadcast([P, NT, P]), ALU.mult)
        V.drain()

        def distance(n):
            h, d = LEVELS[n // 2], n % 2
            x = (G, E)[d].rearrange("p a (s t) -> p (a s) t", t=2 * h)
            m = M[:, d, :, :].rearrange("p a (s t) -> p (a s) t", t=2 * h)
            if n >= 2:
                dve.wait_ge(sem("level_scores"), i * 14 + n - 1)
            V.tensor_tensor(m, x, x[:, :, h:h + 1].to_broadcast([P, 2 * S // (2 * h), 2 * h]), ALU.subtract)\
                .then_inc(sem("distances"), 1)

        def take(n):
            h, d = LEVELS[n // 2], n % 2
            dve.wait_ge(sem("level_scores"), i * 14 + n + 1)
            if n:
                dve.wait_ge(sem("level_taken"), i * 14 + n)
            dve.sem_inc(sem("vector_passed"), 1)
            V.copy_predicated(am_diag, B.masks[:, n:n + 1, :].to_broadcast([P, NT, P]),
                              ps[:, 5 + n % 3, :].rearrange("p (b t) -> p b t", t=P)).then_inc(sem("level_taken"), 1)

        distance(0)
        distance(1)
        for n in range(2 * len(LEVELS)):
            h, d = LEVELS[n // 2], n % 2
            dve.wait_ge(sem("decays"), i * 14 + n + 1)
            m, k, q = (x.rearrange("p a (s t) -> p (a s) t", t=2 * h) for x in (M[:, d, :, :], kh, qh))
            low, high = (k, q) if d == 0 else (q, k)
            V.tensor_tensor(m[:, :, 0:h], m[:, :, 0:h], low[:, :, 0:h], ALU.mult)
            V.tensor_tensor(m[:, :, h:2 * h], m[:, :, h:2 * h], high[:, :, h:2 * h], ALU.mult)\
                .then_inc(sem("weighted"), 1)
            if n >= 1:
                take(n - 1)
                if n + 1 < 2 * len(LEVELS):
                    distance(n + 1)
            low_to(level_tiles(n - 2) + RING)
        take(2 * len(LEVELS) - 1)
        V.drain()
        ends = lambda d: tot[:, 8 * d:8 * d + 8].unsqueeze(2).to_broadcast([P, 8, P])
        V.tensor_tensor(t8(M[:, 1, :, :]), t8(G), ends(0), ALU.subtract)
        V.tensor_tensor(t8(tmp[:, 0:2, :]), t8(E), ends(1), ALU.subtract).then_inc(sem("block_distances"), 1)
        low_to(27)
        dve.wait_ge(sem("block_decays"), i + 1)
        V.memset(B.small[:, 32:48], 1.0)
        V.drain()
        for k in range(3):
            V.tensor_tensor(cum[:, 0, :, k + 1:k + 2], cum[:, 0, :, k:k + 1], dec[:, 0, :, k:k + 1], ALU.mult)
            V.tensor_tensor(cum[:, 1, :, 2 - k:3 - k], cum[:, 1, :, 3 - k:4 - k], dec[:, 1, :, 3 - k:4 - k], ALU.mult)
            V.drain()
        low_to(29)
        dve.wait_ge(sem("cross_decays"), i + 1)
        V.tensor_tensor(M[:, 0, :, :], M[:, 0, :, :], qh, ALU.mult)
        V.tensor_tensor(M[:, 1, :, :], M[:, 1, :, :], kh, ALU.mult)
        V.tensor_tensor(tmp[:, 0:2, :], tmp[:, 0:2, :], qh, ALU.mult)
        V.tensor_tensor(tmp[:, 2:4, :], tmp[:, 2:4, :], kh, ALU.mult)
        low_to(31)
        V.drain()
        primed = at(AT_G, 4, 2, P)
        for n, (x, b, d, k) in enumerate(((M[:, 1, :, :], 0, 0, 1), (M[:, 0, :, :], 3, 0, 2),
                                          (tmp[:, 0:2, :], 0, 1, 1), (tmp[:, 2:4, :], 3, 1, 2))):
            V.tensor_tensor(primed[:, n, :, :], x[:, :, b * P:(b + 1) * P],
                            dec[:, d, :, k:k + 1].to_broadcast([P, 2, P]), ALU.mult)
        V.drain().then_inc(sem("cross_weighted"), 1)
        c8 = lambda d: B.small[:, 32 + 8 * d:40 + 8 * d].unsqueeze(2).to_broadcast([P, 8, P])
        V.tensor_tensor(t8(E), t8(M[:, 0, :, :]), c8(0), ALU.mult)
        V.tensor_tensor(t8(at(AT_QB, 2, S)), t8(tmp[:, 0:2, :]), c8(1), ALU.mult)
        V.drain().then_inc(sem("state_queries"), 1)
        low_to(34)
        dve.wait_ge(sem("o_summed"), i + 1)
        R = at(AT_R, S)
        V.tensor_scalar(R, ps[:, 6, :], 1.0 / DK, LN_EPS, ALU.mult, ALU.add).then_inc(sem("o_variance"), 1)
        dve.wait_ge(sem("o_deviation"), i + 1)
        for a in range(2):
            V.scalar_tensor_tensor(out=Y[:, bass.ds(i * 2 + a, 1), :], in0=ps[:, 4 + a:5 + a, :],
                                   scalar=B.vec[:, VEC["gla_w"] + a:VEC["gla_w"] + a + 1], in1=R.unsqueeze(1),
                                   op0=ALU.mult, op1=ALU.mult)
        V.drain().then_inc(sem("heads_done"), 1)
        low_to(36)


def pool_vector(B, dve, i, banks, free):
    nc, sem, at, Y = B.nc, B.sem, B.at, B.Y
    ALU = mybir.AluOpType
    V = nc.vector
    x = at(TMP, 4, S)
    V.tensor_copy(x, banks).then_inc(free, 1)
    V.drain()
    g = x.rearrange("p a (r w) -> p a r w", w=GRID_W)
    sums = at(AT_ROWS, 4, (GRID_R + 1) * GRID_W).rearrange("p a (r w) -> p a r w", w=GRID_W)
    if i == 0:
        V.memset(sums[:, :, 0, :], 0.0)
    V.tensor_copy(sums[:, :, 1, :], g[:, :, 0, :])
    V.drain()
    for r in range(1, GRID_R):
        V.tensor_tensor(sums[:, :, r + 1, :], sums[:, :, r, :], g[:, :, r, :], ALU.add)
        V.drain()
    window = 2 << i
    out = Y[:, 4 * i:4 * i + 4, :].rearrange("p a (r w) -> p a r w", w=GRID_W)
    for r in range(GRID_R):
        a, b = max(r - window // 2, 0), min(r + window - window // 2, GRID_R)
        V.tensor_tensor(out[:, :, r, :], sums[:, :, b, :], sums[:, :, a, :], ALU.subtract)
    V.drain()
    for r in range(GRID_R):
        a, b = max(r - window // 2, 0), min(r + window - window // 2, GRID_R)
        last = V.scalar_tensor_tensor(out=out[:, :, r, :], in0=out[:, :, r, :], scalar=1.0 / (b - a),
                                      in1=g[:, :, r, :], op0=ALU.mult, op1=ALU.subtract)
    last.then_inc(sem("pooled"), 1)


def model_kernel(nc, A, out):
    B = Build(nc, A, out)
    with nc.Block() as block:

        @block.sync
        def _(sp):
            with nc.allow_non_contiguous_dma(reason="columns of small tables"):
                sync_program(B, sp)

        @block.gpsimd
        def _(pool):
            pool_program(B, pool)

        @block.scalar
        def _(act):
            scalar_program(B, act)

        @block.vector
        def _(dve):
            vector_program(B, dve)

        @block.tensor
        def _(pe):
            tensor_program(B, pe)


def constants():
    i = np.arange(P)
    row, col = i[:, None], i[None, :]
    f = lambda c: c.astype(np.float32)
    restart = np.broadcast_to(f(np.arange(S) % P != 0), (P, S))
    table = np.concatenate([f(row == col), np.ones((P, P), np.float32), f(row > col), f(row < col),
                            np.where(col > row, np.float32(NEG), np.float32(0)), 2 * f(row == col), f(row <= col),
                            restart], axis=1)
    masks = []
    for h in LEVELS:
        pair = (row // (2 * h) == col // (2 * h)) & (row // h != col // h)
        masks += [pair & (row < col), pair & (row > col)]
    return np.ascontiguousarray(table), np.ascontiguousarray(f(np.stack(masks, 1).reshape(P, -1)))


_INS = ["x", "c", "norm_g", "w_ada", "b_ada", "w_in", "ln_v_g", "ln_v_b", "w_s", "b_s", "b_f", "w_out", "final_g",
        "c_2", "ctx_2", "c_ctx_2", "w_ada_2", "b_ada_2", "ln_g_2", "ln_b_2", "w_in_e_2", "w_gate_f_2", "b_gate_f_2",
        "w_gate_b_2", "b_gate_b_2", "gla_norm_w_2", "conv_w_2", "w_out_e_2", "w_in_o_2", "w_pool_2", "pool_scale_2",
        "w_out_o_2"]


def kernel(**inputs):
    import concourse.bacc as _bacc
    from concourse.bass_utils import run_bass_kernel_spmd as _run

    nc = _bacc.Bacc("TRN2", target_bir_lowering=False, num_devices=1, dynamic_dma_scratch_size=1024)
    arrays = {name: np.ascontiguousarray(inputs[name]) for name in _INS}
    arrays["const"], arrays["masks"] = constants()
    A, feeds = {}, {}
    for name, a in arrays.items():
        feeds[f"in_{name}"] = a
        A[name] = nc.dram_tensor(f"in_{name}", a.shape, mybir.dt.from_np(a.dtype), kind="ExternalInput").ap()
    out = nc.dram_tensor("out_0", (1, S, D), mybir.dt.float32, kind="ExternalOutput").ap()
    model_kernel(nc, A, out)
    return _run(nc, [feeds], core_ids=[0]).results[0]["out_0"]
```
